# Optimizing a Trainium2 kernel written in Bass

```python
import jax, jax.numpy as jnp
from jax import lax
import numpy as np
import math
import jax
import jax.numpy as jnp

D_MODEL = 1024
BATCH = 1
SEQ = 256
DEPTH = 1

CHUNK = 64

D_POOL = D_MODEL // 2
POOL_WINDOWS = (2, 4, 8, 16)
POOL_GROUPS = len(POOL_WINDOWS)
POOL_GROUP_DIM = D_POOL // POOL_GROUPS

D_CONV = D_MODEL // 2
CONV_WIDTH = 3

D_IN = D_POOL + 3 * D_CONV + 2 * D_MODEL

N_KEYS = 128
N_EXPERTS = N_KEYS * N_KEYS
PEER_HEADS = 8
PEER_QUERY_DIM = 256
PEER_HALF = PEER_QUERY_DIM // 2
PEER_TOPK = 16
PEER_TOKEN_BLOCK = 128

RMS_EPS = 1e-6


def rmsnorm(x, g):
    xf = x.astype(jnp.float32)
    y = xf * lax.rsqrt(jnp.mean(xf * xf, axis=-1, keepdims=True) + RMS_EPS)
    return (y * g.astype(jnp.float32)).astype(x.dtype)

def pool_mixer(u, group_w, scale):
    S_ = u.shape[1]
    uf = u.astype(jnp.float32)
    csum = jnp.cumsum(uf, axis=1)
    pos = jnp.arange(S_)
    outs = []
    for g, w in enumerate(POOL_WINDOWS):
        sl = slice(g * POOL_GROUP_DIM, (g + 1) * POOL_GROUP_DIM)
        c = csum[:, :, sl]
        c_shift = jnp.pad(c[:, :S_ - w, :], ((0, 0), (w, 0), (0, 0)))
        cnt = jnp.minimum(pos + 1, w).astype(jnp.float32)[None, :, None]
        outs.append((c - c_shift) / cnt - uf[:, :, sl])
    p = jnp.stack(outs, axis=2).astype(u.dtype)
    p = jnp.einsum('bsgc,gcd->bsgd', p, group_w)
    return p.reshape(u.shape) * scale

def short_conv_mixer(c_gate, b_gate, v, conv_w):
    S_ = v.shape[1]
    u = c_gate * v
    up = jnp.pad(u, ((0, 0), (CONV_WIDTH - 1, 0), (0, 0)))
    y = up[:, 0:S_, :] * conv_w[0]
    for k in range(1, CONV_WIDTH):
        y = y + up[:, k:k + S_, :] * conv_w[k]
    return b_gate * y

def peer_ffn(h, w_q, sub_keys, expert_u, expert_v):
    B_, S_, D_ = h.shape
    hb_all = h.reshape(B_ * S_ // PEER_TOKEN_BLOCK, PEER_TOKEN_BLOCK, D_)

    def block(hb):
        q = (hb @ w_q).reshape(PEER_TOKEN_BLOCK, PEER_HEADS, 2, PEER_HALF)
        s = jnp.einsum('thpc,hpkc->thpk', q, sub_keys).astype(jnp.float32)
        top_s, top_i = lax.top_k(s, PEER_TOPK)
        cand_s = top_s[:, :, 0, :, None] + top_s[:, :, 1, None, :]
        cand_i = top_i[:, :, 0, :, None] * N_KEYS + top_i[:, :, 1, None, :]
        cand_s = cand_s.reshape(PEER_TOKEN_BLOCK, PEER_HEADS, PEER_TOPK * PEER_TOPK)
        cand_i = cand_i.reshape(PEER_TOKEN_BLOCK, PEER_HEADS, PEER_TOPK * PEER_TOPK)
        fin_s, fin_pos = lax.top_k(cand_s, PEER_TOPK)
        idx = jnp.take_along_axis(cand_i, fin_pos, axis=-1)
        gates = jax.nn.softmax(fin_s, axis=-1)
        u = expert_u[idx]
        act = jax.nn.gelu(jnp.einsum('thkd,td->thk', u, hb).astype(jnp.float32), approximate=False)
        wts = (gates * act).astype(hb.dtype)
        return jnp.einsum('thk,thkd->td', wts, expert_v[idx])

    out = lax.map(block, hb_all)
    return out.reshape(B_, S_, D_)

def first_inputs(seed: int = 0) -> dict:
    key = jax.random.key(seed)
    ks = jax.random.split(key, 16)
    f32 = jnp.float32
    nrm = lambda k, shape, s: jax.random.normal(k, shape, f32) * s
    L = DEPTH
    return {
        "x": nrm(ks[0], (BATCH, SEQ, D_MODEL), 1.0),
        "g_mix": 1.0 + nrm(ks[1], (L, D_MODEL), 0.02),
        "w_in": nrm(ks[2], (L, D_MODEL, D_IN), D_MODEL ** -0.5),
        "pool_group_w": nrm(ks[3], (L, POOL_GROUPS, POOL_GROUP_DIM, POOL_GROUP_DIM), POOL_GROUP_DIM ** -0.5),
        "pool_scale": 1.0 + nrm(ks[4], (L, D_POOL), 0.02),
        "conv_w": nrm(ks[5], (L, CONV_WIDTH, D_CONV), CONV_WIDTH ** -0.5),
        "w_branch_pool": nrm(ks[6], (L, D_POOL, D_MODEL), D_POOL ** -0.5),
        "w_branch_conv": nrm(ks[7], (L, D_CONV, D_MODEL), D_CONV ** -0.5),
        "w_out": nrm(ks[8], (L, D_MODEL, D_MODEL), D_MODEL ** -0.5),
        "g_ffn": 1.0 + nrm(ks[9], (L, D_MODEL), 0.02),
        "w_q": nrm(ks[10], (L, D_MODEL, PEER_HEADS * PEER_QUERY_DIM), D_MODEL ** -0.5),
        "sub_keys": nrm(ks[11], (L, PEER_HEADS, 2, N_KEYS, PEER_HALF), PEER_HALF ** -0.5),
        "expert_u": nrm(ks[12], (L, N_EXPERTS, D_MODEL), D_MODEL ** -0.5),
        "expert_v": nrm(ks[13], (L, N_EXPERTS, D_MODEL), PEER_HEADS ** -0.5),
        "g_final": 1.0 + nrm(ks[14], (D_MODEL,), 0.02),
    }

def first_block(x, g_mix, w_in, pool_group_w, pool_scale, conv_w, w_branch_pool, w_branch_conv,
              w_out, g_ffn, w_q, sub_keys, expert_u, expert_v, g_final):
    for l in range(DEPTH):
        h = rmsnorm(x, g_mix[l])
        z = h @ w_in[l]
        o1 = D_POOL
        o2 = o1 + D_CONV
        o3 = o2 + D_CONV
        o4 = o3 + D_CONV
        o5 = o4 + D_MODEL
        z_pool, z_c, z_b, z_v = z[..., :o1], z[..., o1:o2], z[..., o2:o3], z[..., o3:o4]
        gate_a, gate_b = z[..., o4:o5], z[..., o5:]
        a = pool_mixer(z_pool, pool_group_w[l], pool_scale[l]) @ w_branch_pool[l]
        b = short_conv_mixer(z_c, z_b, z_v, conv_w[l]) @ w_branch_conv[l]
        m = jax.nn.sigmoid(gate_a) * a + jax.nn.sigmoid(gate_b) * b
        x = x + m @ w_out[l]
        h2 = rmsnorm(x, g_ffn[l])
        x = x + peer_ffn(h2, w_q[l], sub_keys[l], expert_u[l], expert_v[l])
    return rmsnorm(x, g_final)


A_HEADS = 8
A_HEAD_DIM = 128
IDX_HEADS = 8
IDX_DIM = 64
TOPK_MAX = 256
Q_BLOCK = 128
REL_BUCKETS = 32
REL_MAX_DIST = 128
B_HEADS = 8
B_HEAD_DIM = D_MODEL // B_HEADS
B_CHUNK = 64
C_HEADS = 4
C_QK_DIM = 256
C_V_DIM = 512
C_CHUNK = 128
N_GROUPS = 4
EXPERTS_PER_GROUP = 8
N_EXPERTS_2 = N_GROUPS * EXPERTS_PER_GROUP
EXPERT_TOPK = 2
D_EXPERT = 512
EPS = 1e-6

A_WIDTH = A_HEADS * A_HEAD_DIM
B_WIDTH = B_HEADS * B_HEAD_DIM
C_QK_WIDTH = C_HEADS * C_QK_DIM
C_V_WIDTH = C_HEADS * C_V_DIM
IN_SPLITS = (A_WIDTH, A_WIDTH, A_WIDTH, IDX_HEADS * IDX_DIM, IDX_DIM, IDX_HEADS,
             B_WIDTH, B_WIDTH, B_WIDTH, B_WIDTH,
             C_QK_WIDTH, C_QK_WIDTH, C_V_WIDTH, C_V_WIDTH,
             D_MODEL, D_MODEL, D_MODEL)
N_IN = sum(IN_SPLITS)


def rmsnorm_2(x, g=None):
    xf = x.astype(jnp.float32)
    y = xf * lax.rsqrt(jnp.mean(xf * xf, axis=-1, keepdims=True) + EPS)
    if g is not None:
        y = y * g.astype(jnp.float32)
    return y.astype(x.dtype)

def t5_bucket(rel):
    max_exact = REL_BUCKETS // 2
    relf = jnp.maximum(rel, 1).astype(jnp.float32)
    large = max_exact + (jnp.log(relf / max_exact) / math.log(REL_MAX_DIST / max_exact)
                         * (REL_BUCKETS - max_exact)).astype(jnp.int32)
    large = jnp.minimum(large, REL_BUCKETS - 1)
    return jnp.where(rel < max_exact, rel, large)

def split_cols(proj):
    offs = np.cumsum(np.array(IN_SPLITS))[:-1].tolist()
    return jnp.split(proj, offs, axis=-1)

def dsa_attention(q, k, v, q_idx, k_idx, w_idx, rel_bias):
    bsz, seq = q.shape[0], q.shape[1]
    top_k = min(TOPK_MAX, seq // 4)
    n_blk = seq // Q_BLOCK
    s_pos = jnp.arange(seq, dtype=jnp.int32)
    k_idx32 = k_idx.astype(jnp.float32)
    idx_scale = (IDX_HEADS * IDX_DIM) ** -0.5

    def to_blocks(a):
        return jnp.moveaxis(a.reshape((bsz, n_blk, Q_BLOCK) + a.shape[2:]), 1, 0)

    def one_block(args):
        qb, qib, wb, t0 = args
        t_pos = t0 + jnp.arange(Q_BLOCK, dtype=jnp.int32)
        rel = jax.nn.relu(jnp.einsum('bqhd,bsd->bqhs', qib.astype(jnp.float32), k_idx32))
        score = jnp.einsum('bqhs,bqh->bqs', rel, wb.astype(jnp.float32) * idx_scale)
        causal = s_pos[None, :] <= t_pos[:, None]
        score = jnp.where(causal[None], score, -jnp.inf)
        _, sel = lax.top_k(score, top_k)
        valid = sel <= t_pos[None, :, None]
        k_sel = jax.vmap(lambda kb, ib: kb[ib])(k, sel)
        v_sel = jax.vmap(lambda vb, ib: vb[ib])(v, sel)
        logits = jnp.einsum('bqhd,bqkhd->bqhk', qb, k_sel).astype(jnp.float32) * (A_HEAD_DIM ** -0.5)
        bucket = t5_bucket(jnp.maximum(t_pos[None, :, None] - sel, 0))
        logits = logits + jnp.transpose(rel_bias[bucket], (0, 1, 3, 2)).astype(jnp.float32)
        logits = jnp.where(valid[:, :, None, :], logits, -jnp.inf)
        p = jax.nn.softmax(logits, axis=-1).astype(v.dtype)
        return jnp.einsum('bqhk,bqkhd->bqhd', p, v_sel)

    t0s = jnp.arange(n_blk, dtype=jnp.int32) * Q_BLOCK
    out = lax.map(one_block, (to_blocks(q), to_blocks(q_idx), to_blocks(w_idx), t0s))
    return jnp.moveaxis(out, 0, 1).reshape(bsz, seq, A_WIDTH)

def hgrn2(q, f_pre, i, g_out, lb, norm_g):
    bsz, seq = q.shape[0], q.shape[1]
    nc = seq // B_CHUNK
    lb = lb.reshape(B_HEADS, B_HEAD_DIM).astype(jnp.float32)
    f = lb + (1.0 - lb) * jax.nn.sigmoid(f_pre.astype(jnp.float32))
    log_f = jnp.log(f)
    kk = 1.0 - f

    def chunks(a):
        return jnp.transpose(a.reshape(bsz, nc, B_CHUNK, B_HEADS, -1), (1, 0, 3, 2, 4))

    causal = jnp.tril(jnp.ones((B_CHUNK, B_CHUNK), dtype=bool))

    def step(state, inp):
        qt, kt, vt, gt = inp
        b = jnp.cumsum(gt, axis=2)
        diff = b[:, :, :, None, :] - b[:, :, None, :, :]
        decay = jnp.exp(jnp.where(causal[None, None, :, :, None], diff, -jnp.inf))
        attn = jnp.einsum('bhtd,bhsd,bhtsd->bhts', qt, kt, decay)
        o = (jnp.einsum('bhts,bhsv->bhtv', attn, vt)
             + jnp.einsum('bhtd,bhdv->bhtv', qt * jnp.exp(b), state))
        b_last = b[:, :, -1:, :]
        state = (jnp.exp(b_last[:, :, 0, :, None]) * state
                 + jnp.einsum('bhsd,bhsv->bhdv', kt * jnp.exp(b_last - b), vt))
        return state, o

    s0 = jnp.zeros((bsz, B_HEADS, B_HEAD_DIM, B_HEAD_DIM), jnp.float32)
    _, o = lax.scan(step, s0, (chunks(q.astype(jnp.float32)), chunks(kk),
                               chunks(i.astype(jnp.float32)), chunks(log_f)))
    o = jnp.transpose(o, (1, 0, 3, 2, 4)).reshape(bsz, seq, B_HEADS, B_HEAD_DIM)
    o = rmsnorm_2(o, norm_g) * jax.nn.silu(g_out.astype(jnp.float32))
    return o.reshape(bsz, seq, B_WIDTH).astype(q.dtype)

def retention(q, k, v, g):
    bsz, seq = q.shape[0], q.shape[1]
    nc = seq // C_CHUNK
    pos = jnp.arange(seq, dtype=jnp.float32)
    theta = jnp.repeat(1.0 / (10000.0 ** jnp.linspace(0.0, 1.0, C_QK_DIM // 2)), 2)
    ang = pos[:, None] * theta[None, :]
    sin = jnp.sin(ang)[None, :, None, :]
    cos = jnp.cos(ang)[None, :, None, :]

    def rot(a):
        a2 = jnp.stack([-a[..., 1::2], a[..., 0::2]], axis=-1).reshape(a.shape)
        return a * cos + a2 * sin

    qr = rot(q.astype(jnp.float32))
    kr = rot(k.astype(jnp.float32)) * (C_QK_DIM ** -0.5)
    log_gamma = jnp.log(1.0 - 2.0 ** (-5.0 - jnp.arange(C_HEADS, dtype=jnp.float32)))
    idx = jnp.arange(C_CHUNK, dtype=jnp.float32)
    causal = idx[:, None] >= idx[None, :]
    intra_decay = jnp.exp(jnp.where(causal[None], (idx[:, None] - idx[None, :])[None] * log_gamma[:, None, None], -jnp.inf))
    q_decay = jnp.exp((idx + 1.0)[None, :] * log_gamma[:, None])[..., None]
    k_decay = jnp.exp((C_CHUNK - 1.0 - idx)[None, :] * log_gamma[:, None])[..., None]
    chunk_decay = jnp.exp(C_CHUNK * log_gamma)[:, None, None]

    def chunks(a):
        return jnp.transpose(a.reshape(bsz, nc, C_CHUNK, C_HEADS, -1), (1, 0, 3, 2, 4))

    def step(state, inp):
        qt, kt, vt = inp
        attn = jnp.einsum('bhtd,bhsd->bhts', qt, kt) * intra_decay
        o = (jnp.einsum('bhts,bhsv->bhtv', attn, vt)
             + jnp.einsum('bhtd,bhdv->bhtv', qt * q_decay, state))
        state = chunk_decay * state + jnp.einsum('bhsd,bhsv->bhdv', kt * k_decay, vt)
        return state, o

    s0 = jnp.zeros((bsz, C_HEADS, C_QK_DIM, C_V_DIM), jnp.float32)
    _, o = lax.scan(step, s0, (chunks(qr), chunks(kr), chunks(v.astype(jnp.float32))))
    o = jnp.transpose(o, (1, 0, 3, 2, 4)).reshape(bsz, seq, C_HEADS, C_V_DIM)
    o = rmsnorm_2(o).reshape(bsz, seq, C_V_WIDTH)
    return (jax.nn.silu(g.astype(jnp.float32)) * o).astype(q.dtype)

def hier_moe(h, rg_w, rg_b, re_w, re_b, w_gate, w_up, w_down):
    bsz, seq, dm = h.shape
    x = h.reshape(-1, dm)
    group_logits = (x @ rg_w + rg_b).astype(jnp.float32)
    group_p = jax.nn.softmax(group_logits, axis=-1)
    g_sel = jnp.argmax(group_logits, axis=-1)
    g_prob = jnp.take_along_axis(group_p, g_sel[:, None], axis=-1)
    exp_logits = (x @ re_w + re_b).astype(jnp.float32).reshape(-1, N_GROUPS, EXPERTS_PER_GROUP)
    in_group = jnp.take_along_axis(exp_logits, g_sel[:, None, None], axis=1)[:, 0]
    top_v, top_i = lax.top_k(in_group, EXPERT_TOPK)
    top_w = jax.nn.softmax(top_v, axis=-1) * g_prob
    w_group = jnp.sum(jax.nn.one_hot(top_i, EXPERTS_PER_GROUP, dtype=jnp.float32) * top_w[..., None], axis=1)
    gates = (jax.nn.one_hot(g_sel, N_GROUPS, dtype=jnp.float32)[:, :, None] * w_group[:, None, :]).astype(x.dtype)
    wg = w_gate.reshape(N_GROUPS, EXPERTS_PER_GROUP, dm, D_EXPERT)
    wu = w_up.reshape(N_GROUPS, EXPERTS_PER_GROUP, dm, D_EXPERT)
    wd = w_down.reshape(N_GROUPS, EXPERTS_PER_GROUP, D_EXPERT, dm)
    y = jnp.zeros_like(x)
    for gi in range(N_GROUPS):
        hg = jax.nn.silu(jnp.einsum('nd,edf->nef', x, wg[gi])) * jnp.einsum('nd,edf->nef', x, wu[gi])
        y = y + jnp.einsum('nef,efd->nd', hg * gates[:, gi, :, None], wd[gi])
    return y.reshape(bsz, seq, dm)

def hybrid_layer(x, c, lb, rel_bias, norm1_g, norm2_g, ada_w, ada_b, w_in, hgrn_norm_g,
                 w_branch_a, w_branch_b, w_branch_c, w_out, rg_w, rg_b, re_w, re_b,
                 e_gate, e_up, e_down):
    bsz, seq, _ = x.shape
    mod = (jax.nn.silu(c) @ ada_w + ada_b)[:, None, :]
    sh1, sc1, gt1, sh2, sc2, gt2 = jnp.split(mod, 6, axis=-1)
    h = rmsnorm_2(x, norm1_g) * (1.0 + sc1) + sh1
    (aq, ak, av, iq, ik, iw, bq, bf, bi, bg, cq, ck, cv, cg, ga, gb, gc) = split_cols(h @ w_in)
    o_a = dsa_attention(aq.reshape(bsz, seq, A_HEADS, A_HEAD_DIM),
                        ak.reshape(bsz, seq, A_HEADS, A_HEAD_DIM),
                        av.reshape(bsz, seq, A_HEADS, A_HEAD_DIM),
                        iq.reshape(bsz, seq, IDX_HEADS, IDX_DIM), ik, iw, rel_bias)
    hs = (bsz, seq, B_HEADS, B_HEAD_DIM)
    o_b = hgrn2(bq.reshape(hs), bf.reshape(hs), bi.reshape(hs), bg.reshape(hs), lb, hgrn_norm_g)
    o_c = retention(cq.reshape(bsz, seq, C_HEADS, C_QK_DIM), ck.reshape(bsz, seq, C_HEADS, C_QK_DIM),
                    cv.reshape(bsz, seq, C_HEADS, C_V_DIM), cg)
    merged = (jax.nn.sigmoid(ga) * (o_a @ w_branch_a)
              + jax.nn.sigmoid(gb) * (o_b @ w_branch_b)
              + jax.nn.sigmoid(gc) * (o_c @ w_branch_c))
    x = x + gt1 * (merged @ w_out)
    h2 = rmsnorm_2(x, norm2_g) * (1.0 + sc2) + sh2
    x = x + gt2 * hier_moe(h2, rg_w, rg_b, re_w, re_b, e_gate, e_up, e_down)
    return x

def second_inputs(seed: int = 0) -> dict:
    key = jax.random.key(seed)
    ks = jax.random.split(key, 22)
    D = D_MODEL

    def nrm(k, shape, scale):
        return jax.random.normal(k, shape, jnp.float32) * scale

    return {
        'x': nrm(ks[0], (BATCH, SEQ, D), 1.0),
        'c': nrm(ks[1], (BATCH, D), 1.0),
        'rel_bias': nrm(ks[2], (REL_BUCKETS, A_HEADS), 0.5),
        'hgrn_lb_raw': nrm(ks[3], (DEPTH, B_WIDTH), 0.5),
        'norm1_g': 1.0 + nrm(ks[4], (DEPTH, D), 0.05),
        'norm2_g': 1.0 + nrm(ks[5], (DEPTH, D), 0.05),
        'ada_w': nrm(ks[6], (DEPTH, D, 6 * D), 0.5 * D ** -0.5),
        'ada_b': nrm(ks[7], (DEPTH, 6 * D), 0.02),
        'w_in': nrm(ks[8], (DEPTH, D, N_IN), D ** -0.5),
        'hgrn_norm_g': 1.0 + nrm(ks[9], (DEPTH, B_HEAD_DIM), 0.05),
        'w_branch_a': nrm(ks[10], (DEPTH, A_WIDTH, D), A_WIDTH ** -0.5),
        'w_branch_b': nrm(ks[11], (DEPTH, B_WIDTH, D), B_WIDTH ** -0.5),
        'w_branch_c': nrm(ks[12], (DEPTH, C_V_WIDTH, D), C_V_WIDTH ** -0.5),
        'w_out': nrm(ks[13], (DEPTH, D, D), D ** -0.5),
        'router_group_w': nrm(ks[14], (DEPTH, D, N_GROUPS), D ** -0.5),
        'router_group_b': nrm(ks[15], (DEPTH, N_GROUPS), 0.01),
        'router_expert_w': nrm(ks[16], (DEPTH, D, N_EXPERTS_2), D ** -0.5),
        'router_expert_b': nrm(ks[17], (DEPTH, N_EXPERTS_2), 0.01),
        'expert_w_gate': nrm(ks[18], (DEPTH, N_EXPERTS_2, D, D_EXPERT), D ** -0.5),
        'expert_w_up': nrm(ks[19], (DEPTH, N_EXPERTS_2, D, D_EXPERT), D ** -0.5),
        'expert_w_down': nrm(ks[20], (DEPTH, N_EXPERTS_2, D_EXPERT, D), D_EXPERT ** -0.5),
        'final_norm_g': 1.0 + nrm(ks[21], (D,), 0.05),
    }

def second_block(x, c, rel_bias, hgrn_lb_raw, norm1_g, norm2_g, ada_w, ada_b, w_in, hgrn_norm_g,
              w_branch_a, w_branch_b, w_branch_c, w_out, router_group_w, router_group_b,
              router_expert_w, router_expert_b, expert_w_gate, expert_w_up, expert_w_down,
              final_norm_g):
    lb_soft = jax.nn.softmax(hgrn_lb_raw.astype(jnp.float32), axis=0)
    lb_all = jnp.cumsum(lb_soft, axis=0) - lb_soft[0:1]
    for l in range(DEPTH):
        x = hybrid_layer(x, c, lb_all[l], rel_bias, norm1_g[l], norm2_g[l], ada_w[l], ada_b[l],
                         w_in[l], hgrn_norm_g[l], w_branch_a[l], w_branch_b[l], w_branch_c[l],
                         w_out[l], router_group_w[l], router_group_b[l], router_expert_w[l],
                         router_expert_b[l], expert_w_gate[l], expert_w_up[l], expert_w_down[l])
    return rmsnorm_2(x, final_norm_g)


def setup_inputs(seed=0):
    out = dict(first_inputs(seed))
    for name, value in second_inputs(seed + 1).items():
        if name != "x":
            out[name + "_2"] = value
    return out


def reference(
    x, g_mix, w_in, pool_group_w, pool_scale, conv_w, w_branch_pool, w_branch_conv, w_out,
    g_ffn, w_q, sub_keys, expert_u, expert_v, g_final, c_2, rel_bias_2, hgrn_lb_raw_2,
    norm1_g_2, norm2_g_2, ada_w_2, ada_b_2, w_in_2, hgrn_norm_g_2, w_branch_a_2, w_branch_b_2,
    w_branch_c_2, w_out_2, router_group_w_2, router_group_b_2, router_expert_w_2,
    router_expert_b_2, expert_w_gate_2, expert_w_up_2, expert_w_down_2, final_norm_g_2,
):
    x = first_block(
        x, g_mix, w_in, pool_group_w, pool_scale, conv_w, w_branch_pool, w_branch_conv, w_out,
        g_ffn, w_q, sub_keys, expert_u, expert_v, g_final,
    )
    return second_block(
        x, c_2, rel_bias_2, hgrn_lb_raw_2, norm1_g_2, norm2_g_2, ada_w_2, ada_b_2, w_in_2,
        hgrn_norm_g_2, w_branch_a_2, w_branch_b_2, w_branch_c_2, w_out_2, router_group_w_2,
        router_group_b_2, router_expert_w_2, router_expert_b_2, expert_w_gate_2, expert_w_up_2,
        expert_w_down_2, final_norm_g_2,
    )


_drawn_inputs = setup_inputs


def setup_inputs(seed=0):
    import zlib

    import numpy as np

    out = dict(_drawn_inputs(seed))
    spreads = {}
    factors = {'pool_scale': 2.871,
     'rel_bias_2': 2.79,
     'norm2_g_2': 3.129,
     'hgrn_norm_g_2': 8.0,
     'router_group_b_2': 8.0,
     'router_expert_b_2': 8.0}
    for name, (base, spread) in spreads.items():
        noise = np.random.default_rng([zlib.crc32(name.encode()), seed]).standard_normal(out[name].shape)
        drawn = base * np.exp(spread * noise) if base else spread * noise
        out[name] = jnp.asarray(drawn.astype(out[name].dtype))
    for name, factor in factors.items():
        out[name] = (out[name] * factor).astype(out[name].dtype)
    return out
```

```python
from contextlib import ExitStack

import numpy as np
import concourse.bass as bass
from concourse import mybir

F32 = mybir.dt.float32
U32 = mybir.dt.uint32
I32 = mybir.dt.int32
ALU = mybir.AluOpType
ACT = mybir.ActivationFunctionType
AX = mybir.AxisListType

P = 128
RING = 4
NGB = 9
BIG = 3.0e38
IDX_SCALE = float(512) ** -0.5
ATT_SCALE = float(128) ** -0.5

C_ID, C_IOTA = 0, 128
C_COS, C_SIN, C_DEC, C_INV, C_OH = 144, 400, 656, 1680, 2704
C_END = 2704 + 640


class Queue:

    def __init__(self, sem, linked):
        self.sem, self.linked = sem, linked
        self.count, self.ops, self.met = 0, [], {}

    def wait(self, *tokens):
        for t in tokens:
            if not t:
                continue
            if isinstance(t, list):
                self.wait(*t)
                continue
            sem, value = t
            if self.met.get(sem.name, 0) < value:
                self.met[sem.name] = value
                self.ops.append(lambda e, s=sem, v=value: e.wait_ge(s, v))

    def last(self):
        return (self.sem, self.count) if self.count else None

    def do(self, fn, *tokens):
        if self.linked:
            self.wait(self.last())
        self.wait(*tokens)
        self.count += 1
        self.ops.append(lambda e: fn(e).then_inc(self.sem, 1))
        return (self.sem, self.count)

    def plain(self, fn, *tokens):
        self.wait(*tokens)
        self.ops.append(fn)

    def dma(self, group, fn, *tokens):
        self.wait(*tokens)
        group.count += 16
        self.ops.append(lambda e: fn(e).then_inc(group.sem, 16))
        return (group.sem, group.count)


class Group:

    def __init__(self, sem):
        self.sem, self.count = sem, 0


class Chunk:

    def __init__(self, n, src, cols, sems):
        self.n, self.src, self.cols, self.slot = n, src, cols, n % RING
        self.tok = (sems[n % RING], 16 * (n // RING + 1))
        self.done = None


class Bank:
    def __init__(self, ap):
        self.ap, self.free = ap, None


def free_dims(ap, *dims):
    return bass.AP(tensor=ap.tensor, offset=ap.offset, ap=[list(ap.ap[0])] + [list(d) for d in dims])


def build(nc, a, out):
    ctx = ExitStack()
    with ctx:
        def sb(name, n, dt=F32):
            return ctx.enter_context(nc.sbuf_tensor(name, [P, n], dt))

        def sem(name):
            return ctx.enter_context(nc.semaphore(name))

        ring = [sb(f"ring{i}", 4096) for i in range(RING)]
        arena = sb("arena", 100 * 256)
        x_t = sb("x", 2048)
        hT_t = sb("hT", 2048)
        mT_t = sb("mT", 2048)
        grow = [sb(f"g{i}", 1024) for i in range(3)]
        cid = sb("cid", 144)
        st = sb("st", 64)
        banks = [Bank(ctx.enter_context(nc.psum_tensor(f"ps{i}", [P, 512], F32))[:, :]) for i in range(8)]
        mod_d = nc.dram_tensor("mod_scratch", [6, 1024], F32, kind="Internal").ap()
        rr_d = nc.dram_tensor("rr_scratch", [8, 512], F32, kind="Internal").ap()

        ring_sems = [sem(f"s_ring{i}") for i in range(RING)]
        V = Queue(sem("s_dve"), True)
        A = Queue(sem("s_act"), True)
        G = Queue(sem("s_pool"), True)
        T = Queue(sem("s_pe"), False)

        def group(name):
            return Group(sem("d_" + name))

        chunks = []

        def chunk(src, cols=4096):
            c = Chunk(len(chunks), src, cols, ring_sems)
            chunks.append(c)
            c.ap = ring[c.slot][:, 0:cols]
            return c

        usable = list(range(8))
        turn = [0]

        def bank():
            b = banks[usable[turn[0] % len(usable)]]
            turn[0] += 1
            return b

        def barrier():
            toks = [q.last() for q in (T, A, V, G)]
            for q in (T, A, V, G):
                q.wait(*toks)
            place[0] = 0
            return toks

        place = [0]

        def ar(n):
            o = place[0]
            place[0] += n
            assert place[0] <= 100 * 256, place[0]
            return arena[:, o:o + n]

        def r3(ap, n):
            return ap.rearrange("p (a b) -> p a b", a=n)

        def mm(o, l, r, start, stop):
            return lambda e: e.matmul(o, l, r, start=start, stop=stop)

        x = r3(x_t[:, :], 2)
        hT = r3(hT_t[:, :], 8)
        mT = r3(mT_t[:, :], 8)
        ident = cid[:, C_ID:C_ID + 128]
        iota = cid[:, C_IOTA:C_IOTA + 16]

        g_c = group("const")
        A.dma(g_c, lambda e: e.dma_start(x, a["x"].rearrange("b (t p) d -> p (b t) d", p=P)))
        A.dma(g_c, lambda e: e.dma_start(cid[:, :], a["cst"][:, 0:144]))
        pgw = ar(512)
        invc = ar(1024)
        pcs = ar(4)
        cvw = ar(12)
        A.dma(g_c, lambda e: e.dma_start(pgw, a["pgw"]))
        A.dma(g_c, lambda e: e.dma_start(invc, a["cst"][:, C_INV:C_INV + 1024]))
        A.dma(g_c, lambda e: e.dma_start(pcs, a["pcs"]))
        A.dma(g_c, lambda e: e.dma_start(cvw, a["cvw"]))

        def row_load(q, grp, i, src, *toks):
            return q.dma(grp, lambda e: e.dma_start(grow[i][:, :], src.partition_broadcast(P)), *toks)

        row_load(A, g_c, 0, a["g_mix"][0, :])
        row_load(A, g_c, 1, a["g_ffn"][0, :])
        c_tok = row_load(A, g_c, 2, a["g_final"])

        def rmsnorm(src, g, dst, junk, cols, *toks):
            ss, ms, sq, r, t = (st[:, 2 * i:2 * i + 2] for i in range(5))
            for tt in range(2):
                s = A.do(lambda e, tt=tt: e.activation(junk, src[:, tt, :], ACT.Square,
                                                       accum_out=ss[:, tt:tt + 1]), *toks)
            m = V.do(lambda e: e.tensor_scalar(ms, ss, 1.0 / cols, 1e-6, ALU.mult, ALU.add), s)
            s = A.do(lambda e: e.activation(sq, ms, ACT.Sqrt), m)
            inv_sqrt(r, sq, ms, t, s)
            for tt in range(2):
                k = V.do(lambda e, tt=tt: e.scalar_tensor_tensor(
                    out=dst[:, tt, :], in0=src[:, tt, :], scalar=r[:, tt:tt + 1], in1=g,
                    op0=ALU.mult, op1=ALU.mult), *toks)
            return k

        def inv_sqrt(r, sq, ms, t, *toks):
            V.do(lambda e: e.reciprocal(r, sq), *toks)
            V.do(lambda e: e.tensor_tensor(t, r, r, ALU.mult))
            V.do(lambda e: e.tensor_tensor(t, t, ms, ALU.mult))
            V.do(lambda e: e.tensor_scalar(t, t, -0.5, 1.5, ALU.mult, ALU.add))
            return V.do(lambda e: e.tensor_tensor(r, r, t, ALU.mult))

        def copy_out(n, dst, src, *toks):
            if n % 2:
                return A.do(lambda e: e.activation(dst, src, ACT.Copy), *toks)
            return V.do(lambda e: e.tensor_copy(dst, src), *toks)

        def transposes(src, dst, nk, *toks):
            got = []
            for kp in range(nk // 2):
                b = bank()
                for kk in range(2):
                    for tt in range(2):
                        o = b.ap[:, kk * 256 + tt * 128:kk * 256 + tt * 128 + 128]
                        i = src[:, tt, (2 * kp + kk) * 128:(2 * kp + kk + 1) * 128]
                        f = (lambda e, o=o, i=i: e.transpose(o, i, ident))
                        if kk and tt:
                            t = T.do(f, *toks)
                        else:
                            T.plain(f, b.free, *toks)
                k = copy_out(kp, dst[:, 2 * kp:2 * kp + 2, :], r3(b.ap[:, :], 2), t)
                b.free = k
                got.append(k)
            return got[-2:]

        def proj_t(c, rhs, nk, evac, *toks):
            w = r3(c.ap, nk)
            for half in range(2):
                b = bank()
                for j in range(2):
                    blk = 2 * half + j
                    for k in range(nk):
                        f = mm(b.ap[:, j * 256:j * 256 + 256], w[:, k, blk * 128:blk * 128 + 128],
                               rhs[:, k, :], k == 0, k == nk - 1)
                        if j == 1 and k == nk - 1:
                            t = T.do(f)
                        else:
                            T.plain(f, c.tok, b.free, *toks)
                b.free = evac(half, b.ap, t)
            c.done = t

        def proj_n(c, lhs, nk, evac, *toks):
            w = r3(c.ap, nk)
            for tt in range(2):
                b = bank()
                for k in range(nk):
                    f = mm(b.ap[:, :], lhs[:, k, tt * 128:tt * 128 + 128], w[:, k, :], k == 0, k == nk - 1)
                    if k == nk - 1:
                        t = T.do(f)
                    else:
                        T.plain(f, c.tok, b.free, *toks)
                b.free = evac(tt, b.ap, t)
            c.done = t

        hN = r3(ar(2048), 2)
        junk = ar(1024)
        ht = transposes(hN, hT, 8, rmsnorm(x, grow[0][:, :], hN, junk, 1024, c_tok))

        pp = [ar(4 * 272) for _ in range(5)]
        cu = ar(4 * 258)
        zc, zb, zv, pf, aT, bT, cy = (ar(1024) for _ in range(7))
        zc, zb, zv, pf, aT, bT, cy = (r3(t, 4) for t in (zc, zb, zv, pf, aT, bT, cy))
        pp = [r3(t, 4) for t in pp]
        cu = r3(cu, 4)
        z1 = G.do(lambda e: e.memset(pp[0][:, :, 0:16], 0.0))
        z2 = G.do(lambda e: e.memset(cu[:, :, 0:2], 0.0))
        pre = {}
        for name, dst, off in (("p", pp[0], 16), ("c", zc, 0), ("b", zb, 0), ("v", zv, 0)):
            c = chunk(a["w_in"]["pcbv".index(name)])

            def evac(half, ps, t, dst=dst, off=off, name=name):
                k = copy_out(half, dst[:, 2 * half:2 * half + 2, off:off + 256], r3(ps, 2), t)
                pre.setdefault(name, []).append(k)
                return k
            proj_t(c, hT, 8, evac, ht)

        for lv in range(4):
            d = 1 << lv
            lo = 2 * d - 1
            V.do(lambda e, lv=lv, d=d, lo=lo: e.tensor_tensor(
                pp[lv + 1][:, lv:4, lo:272], pp[lv][:, lv:4, lo:272], pp[lv][:, lv:4, lo - d:272 - d], ALU.add),
                pre["p"], z1)
            V.do(lambda e, lv=lv: e.tensor_tensor(pf[:, lv, :], pp[lv + 1][:, lv, 16:272],
                                                  invc[:, lv * 256:lv * 256 + 256], ALU.mult))
        t_pf = V.do(lambda e: e.tensor_tensor(pf, pf, pp[0][:, :, 16:272], ALU.subtract))
        t_a = []
        for half in range(2):
            b = bank()
            for j in range(2):
                g = 2 * half + j
                f = mm(b.ap[:, j * 256:j * 256 + 256], pgw[:, g * 128:g * 128 + 128], pf[:, g, :], True, True)
                if j:
                    t = T.do(f)
                else:
                    T.plain(f, t_pf, b.free)
            for j in range(2):
                g = 2 * half + j
                k = A.do(lambda e, g=g, j=j, b=b: e.activation(aT[:, g, :], b.ap[:, j * 256:j * 256 + 256],
                                                               ACT.Copy, scale=pcs[:, g:g + 1]), t)
            b.free = k
            t_a.append(k)
        V.do(lambda e: e.tensor_tensor(cu[:, :, 2:258], zc, zv, ALU.mult), pre["c"], pre["v"], z2)
        for g in range(4):
            V.do(lambda e, g=g: e.tensor_scalar(cy[:, g, :], cu[:, g, 0:256], cvw[:, g:g + 1], None, ALU.mult))
            for k in (1, 2):
                V.do(lambda e, g=g, k=k: e.scalar_tensor_tensor(
                    out=cy[:, g, :], in0=cu[:, g, k:k + 256], scalar=cvw[:, 4 * k + g:4 * k + g + 1],
                    in1=cy[:, g, :], op0=ALU.mult, op1=ALU.add))
        t_b = V.do(lambda e: e.tensor_tensor(bT, cy, zb, ALU.mult), pre["b"])

        sg = [r3(ar(1024), 4) for _ in range(4)]
        t_sg = {}
        for n in range(4):
            def evac(half, ps, t, n=n):
                k = A.do(lambda e: e.activation(sg[n][:, 2 * half:2 * half + 2, :], r3(ps, 2), ACT.Sigmoid), t)
                t_sg[n, half] = k
                return k
            proj_t(chunk(a["w_in"][4 + n]), hT, 8, evac)
        tmp = r3(ar(512), 2)

        def branch(c, tmp, kts, blks, sgs, tsg, m0, first, *toks):
            b = bank()
            for j, blk in enumerate(blks):
                for n, (l, r) in enumerate(kts(blk)):
                    f = mm(b.ap[:, j * 256:j * 256 + 256], l, r, n == 0, n == len(kts(blk)) - 1)
                    if j == 1 and n == len(kts(blk)) - 1:
                        t = T.do(f)
                    else:
                        T.plain(f, c, b.free, *toks)
            if first:
                k = V.do(lambda e: e.tensor_tensor(mT[:, m0:m0 + 2, :], sgs, r3(b.ap[:, :], 2), ALU.mult), t, tsg)
                b.free = k
            else:
                b.free = V.do(lambda e: e.tensor_tensor(tmp, sgs, r3(b.ap[:, :], 2), ALU.mult), t, tsg)
                k = V.do(lambda e: e.tensor_tensor(mT[:, m0:m0 + 2, :], mT[:, m0:m0 + 2, :], tmp, ALU.add))
            return t, k

        for br, (src, rhs, toks) in enumerate((("wbp", aT, t_a), ("wbc", bT, t_b))):
            c = chunk(a[src])
            w = r3(c.ap, 4)
            for q in range(4):
                n = 2 * br + q // 2
                t, t_m = branch(c.tok, tmp,
                                lambda blk, w=w, rhs=rhs: [(w[:, k, blk * 128:blk * 128 + 128], rhs[:, k, :])
                                                           for k in range(4)],
                                (2 * q, 2 * q + 1), sg[n][:, 2 * (q % 2):2 * (q % 2) + 2, :], t_sg[n, q % 2],
                                2 * q, br == 0, toks)
            c.done = t

        def add_x(tt, n):
            def f(ps, t):
                return V.do(lambda e: e.tensor_tensor(x[:, tt, n * 512:n * 512 + 512],
                                                      x[:, tt, n * 512:n * 512 + 512], ps, ALU.add), t)
            return f

        for n in range(2):
            proj_n(chunk(a["w_out"][n]), mT, 8, lambda tt, ps, t, n=n: add_x(tt, n)(ps, t), t_m)

        barrier()
        hN = r3(ar(2048), 2)
        junk = ar(1024)
        idx_u = ar(256).bitcast(U32)
        wts = ar(256)
        act = ar(256)
        keep = place[0]
        t_h2 = rmsnorm(x, grow[1][:, :], hN, junk, 1024)
        ht = transposes(hN, hT, 8, t_h2)
        qT = r3(ar(16 * 256), 16)
        S = ar(2 * 16 * 128).rearrange("p (t h k) -> p t h k", t=2, h=16)
        S2 = ar(256)
        tops = ar(512).rearrange("p (t h k) -> p t h k", t=2, h=16)
        topi = ar(512).bitcast(U32).rearrange("p (t h k) -> p t h k", t=2, h=16)
        topf = ar(512).rearrange("p (t h k) -> p t h k", t=2, h=16)
        cand = ar(2048)
        oh = ar(2048)
        fs = ar(256)
        fp = ar(256).bitcast(U32)
        fa = ar(256).bitcast(U32)
        faf = ar(256)
        ab = [ar(256) for _ in range(2)]
        sm = ar(64)
        t_q = []
        for n in range(4):
            def evac(half, ps, t, n=n):
                k = copy_out(half, qT[:, 4 * n + 2 * half:4 * n + 2 * half + 2, :], r3(ps, 2), t)
                t_q.append(k)
                return k
            proj_t(chunk(a["w_q"][n]), hT, 8, evac, ht)
        c = chunk(a["skT"], 2048)
        sk = r3(c.ap, 16)
        for tt in range(2):
            for q in range(4):
                b = bank()
                for j in range(4):
                    hp = 4 * q + j
                    f = mm(b.ap[:, j * 128:j * 128 + 128], qT[:, hp, tt * 128:tt * 128 + 128], sk[:, hp, :], True, True)
                    if j == 3:
                        t = T.do(f)
                    else:
                        T.plain(f, c.tok, b.free, t_q)
                b.free = A.do(lambda e, tt=tt, q=q, b=b: e.activation(
                    S[:, tt, 4 * q:4 * q + 4, :], r3(b.ap[:, :], 4), ACT.Copy), t)
                t_s = b.free
                for j in range(4):
                    hp = 4 * q + j
                    s, v, i = S[:, tt, hp, :], tops[:, tt, hp, :], topi[:, tt, hp, :]
                    top16(V, s, S2[:, 0:128], v, i, t_s)
        c.done = t
        V.do(lambda e: e.tensor_copy(topf, topi))

        def bc(ap2, off, *dims):
            base = ap2[:, off:off + 1]
            return free_dims(base, *dims)

        flat = lambda ap: ap.rearrange("p t h k -> p (t h k)")
        tops_f, topf_f = flat(tops), flat(topf)
        for tt in range(2):
            o = tt * 256
            V.do(lambda e, o=o: e.tensor_tensor(
                free_dims(cand, [256, 8], [16, 16], [1, 16]),
                bc(tops_f, o, [32, 8], [1, 16], [0, 16]),
                bc(tops_f, o + 16, [32, 8], [0, 16], [1, 16]), ALU.add))
            for h in range(8):
                f0 = tt * 128 + h * 16
                top16(V, cand[:, h * 256:h * 256 + 256], S2, fs[:, f0:f0 + 16], fp[:, f0:f0 + 16])
            for half in range(2):
                fr = slice(tt * 128, tt * 128 + 128)
                if half == 0:
                    V.do(lambda e, fr=fr: e.tensor_scalar(fa[:, fr], fp[:, fr], 4, None, ALU.logical_shift_right))
                else:
                    V.do(lambda e, fr=fr: e.tensor_scalar(fa[:, fr], fp[:, fr], 15, None, ALU.bitwise_and))
                V.do(lambda e, fr=fr: e.tensor_copy(faf[:, fr], fa[:, fr]))
                V.do(lambda e, tt=tt: e.tensor_tensor(
                    free_dims(oh, [256, 8], [16, 16], [1, 16]),
                    bc(faf, tt * 128, [16, 8], [1, 16], [0, 16]),
                    bc(iota, 0, [0, 8], [0, 16], [1, 16]), ALU.is_equal), c_tok)
                V.do(lambda e, o=o, half=half: e.tensor_tensor(
                    free_dims(oh, [256, 8], [16, 16], [1, 16]),
                    free_dims(oh, [256, 8], [16, 16], [1, 16]),
                    bc(topf_f, o + 16 * half, [32, 8], [0, 16], [1, 16]), ALU.mult))
                V.do(lambda e, tt=tt, half=half: e.tensor_reduce(
                    ab[half][:, tt * 128:tt * 128 + 128], free_dims(oh, [16, 128], [1, 16]), AX.X, ALU.add))
        V.do(lambda e: e.scalar_tensor_tensor(out=ab[0], in0=ab[0], scalar=128.0, in1=ab[1],
                                              op0=ALU.mult, op1=ALU.add))
        t_idx = V.do(lambda e: e.tensor_copy(idx_u, ab[0]))
        V.do(lambda e: e.tensor_tensor(free_dims(wts, [16, 16], [1, 16]), free_dims(fs, [16, 16], [1, 16]),
                                       free_dims(fs, [16, 16], [0, 16]), ALU.subtract))
        k = A.do(lambda e: e.activation(wts, wts, ACT.Exp), V.last())
        V.do(lambda e: e.tensor_reduce(sm[:, 0:16], free_dims(wts, [16, 16], [1, 16]), AX.X, ALU.add), k)
        V.do(lambda e: e.reciprocal(sm[:, 16:32], sm[:, 0:16]))
        V.do(lambda e: e.tensor_tensor(free_dims(wts, [16, 16], [1, 16]), free_dims(wts, [16, 16], [1, 16]),
                                       free_dims(sm[:, 16:32], [1, 16], [0, 16]), ALU.mult))

        barrier()
        place[0] = keep
        gb = [ar(1024) for _ in range(NGB)]
        cs = ar(8)
        csg = ar(8)
        adab = ar(6144)
        modr = ar(6144)
        gbs = [group(f"gb{i}") for i in range(NGB)]
        gfree = [None] * NGB
        ng = [0]

        def gather(table, col):
            s = ng[0] % NGB
            ng[0] += 1
            t = G.dma(gbs[s], lambda e: e.indirect_dma_start(
                out=gb[s], out_offset=None, in_=table,
                in_offset=bass.IndirectOffsetOnAxis(ap=idx_u[:, col:col + 1], axis=0)), t_idx, gfree[s])
            return s, t

        g_m = group("mod")
        A.dma(g_m, lambda e: e.dma_start(cs, a["c_2"]))
        t_cm = A.dma(g_m, lambda e: e.dma_start(adab[0:1, :], a["ada_b_2"]))
        A.do(lambda e: e.activation(csg, cs, ACT.Sigmoid), t_cm)
        t_cs = A.do(lambda e: e.activation(csg, csg, ACT.Copy), None)
        t_cs = V.do(lambda e: e.tensor_tensor(csg, csg, cs, ALU.mult), t_cs)
        t_mod = []
        for n in range(12):
            c = chunk(a["ada_w_2"][n])
            w = r3(c.ap, 8)
            b = bank()
            for k in range(8):
                f = mm(b.ap[0:1, :], csg[:, k:k + 1], w[:, k, :], k == 0, k == 7)
                if k == 7:
                    t = T.do(f)
                else:
                    T.plain(f, c.tok, b.free, t_cs)
            c.done = t
            b.free = A.do(lambda e, n=n, b=b: e.activation(modr[0:1, n * 512:n * 512 + 512], b.ap[0:1, :], ACT.Copy), t)
        t_mr = A.last()

        for col in range(256):
            s, t = gather(a["expert_u"], col)
            gfree[s] = V.do(lambda e, s=s, col=col, junk=junk, hN=hN: e.tensor_tensor_reduce(
                out=junk, in0=gb[s], in1=hN[:, col // 128, :], scale=1.0, scalar=0.0,
                op0=ALU.mult, op1=ALU.add, accum_out=act[:, col:col + 1]), t)
        t_mod = V.do(lambda e: e.tensor_tensor(modr[0:1, :], modr[0:1, :], adab[0:1, :], ALU.add), t_mr)
        k = A.do(lambda e: e.activation(act, act, ACT.Gelu), V.last())
        V.do(lambda e: e.tensor_tensor(wts, wts, act, ALU.mult), k)
        t_md = A.dma(g_m, lambda e: e.dma_start(mod_d.rearrange("(a b) d -> a (b d)", a=1), modr[0:1, :]), t_mod)
        for col in range(256):
            s, t = gather(a["expert_v"], col)
            gfree[s] = V.do(lambda e, s=s, col=col: e.scalar_tensor_tensor(
                out=x[:, col // 128, :], in0=gb[s], scalar=wts[:, col:col + 1], in1=x[:, col // 128, :],
                op0=ALU.mult, op1=ALU.add), t)
        t_x = rmsnorm(x, grow[2][:, :], x, junk, 1024, V.last())

        g_r = [group(f"row{i}") for i in range(3)]

        def modulated(norm, sc_row, sh_row, dst, junk, *toks):
            k0 = row_load(A, g_r[0], 0, norm, V.last())
            k1 = row_load(A, g_r[1], 1, mod_d[sc_row, :], V.last(), t_md)
            k2 = row_load(A, g_r[2], 2, mod_d[sh_row, :], V.last(), t_md)
            V.do(lambda e: e.scalar_tensor_tensor(out=grow[1][:, :], in0=grow[1][:, :], scalar=1.0,
                                                  in1=grow[0][:, :], op0=ALU.add, op1=ALU.mult), k0, k1)
            rmsnorm(x, grow[1][:, :], dst, junk, 1024, *toks)
            for tt in range(2):
                k = V.do(lambda e, tt=tt: e.tensor_tensor(dst[:, tt, :], dst[:, tt, :], grow[2][:, :], ALU.add), k2)
            return k

        ht = transposes(hN, hT, 8, modulated(a["norm1_g_2"][0, :], 1, 0, hN, junk, t_x))
        w2 = a["w_in_2"]

        def to_sbuf_t(src, dst, toks_out, fn=None):
            for n, s in enumerate(src):
                def evac(half, ps, t, n=n):
                    d = dst[:, 4 * n + 2 * half:4 * n + 2 * half + 2, :]
                    if fn is None:
                        k = copy_out(half, d, r3(ps, 2), t)
                    else:
                        k = A.do(lambda e: e.activation(d, r3(ps, 2), fn), t)
                    toks_out.append(k)
                    return k
                proj_t(chunk(s), hT, 8, evac, ht)

        def to_sbuf_n(src, dst, toks_out):
            for n, s in enumerate(src):
                def evac(tt, ps, t, n=n):
                    k = copy_out(tt, dst[:, tt, n * 512:n * 512 + 512], ps, t)
                    toks_out.append(k)
                    return k
                proj_n(chunk(s), hT, 8, evac, ht)

        toks = barrier()
        aq, ak = r3(ar(2048), 8), r3(ar(2048), 8)
        iq = r3(ar(1024), 4)
        ikE, ikO = ar(256), ar(256)
        iw = r3(ar(16), 2)
        av = r3(ar(2048), 2)
        oaT = r3(ar(2048), 8)
        bias = [r3(ar(8 * 128), 8), r3(ar(8 * 256), 8)]
        Lb = ar(2048)
        PT = [r3(ar(1024), 8) for _ in range(2)]
        rel = ar(512)
        sc, sc2 = ar(256), ar(256)
        m8 = ar(8)
        mx = ar(24)
        wsm = ar(8 * 136)
        rb = ar(8)
        ohb = ar(640)
        rrs = ar(512)
        g_a = group("att")
        A.dma(g_a, lambda e: e.dma_start(wsm, a["w_small"]), toks)
        A.dma(g_a, lambda e: e.dma_start(rb[0:32, :], a["rel_bias_2"]))
        t_ga = A.dma(g_a, lambda e: e.dma_start(ohb, a["cst"][:, C_OH:C_OH + 640]))
        z1 = G.do(lambda e: e.memset(ikE, 0.0))
        z2 = G.do(lambda e: e.memset(ikO, 0.0))
        b = bank()
        t = T.do(mm(b.ap[0:8, :], rb[0:32, :], ohb[0:32, 0:512], True, True), t_ga, b.free)
        b.free = A.do(lambda e, b=b: e.activation(rrs[0:8, :], b.ap[0:8, :], ACT.Copy), t)
        t_rr = A.dma(g_a, lambda e: e.dma_start(rr_d, rrs[0:8, :]), b.free)
        rev = [PT[0], r3(Lb, 8)]
        for tt in range(2):
            n = 128 * (tt + 1)
            for h in range(8):
                t_rev = A.dma(g_a, lambda e, tt=tt, n=n, h=h: e.dma_start(
                    rev[tt][:, h, :], bass.AP(tensor=rr_d.tensor, offset=h * 512 + 128 - tt * 128,
                                              ap=[[1, 128], [1, n]])), t_rr)
        t_bias = []
        for tt in range(2):
            hs = 4 >> tt
            for hq in range(8 // hs):
                b = bank()
                t = T.do(mm(b.ap[:, :], ohb[:, 512:640], rev[tt][:, hq * hs:hq * hs + hs, :], True, True), t_rev, b.free)
                b.free = copy_out(hq, bias[tt][:, hq * hs:hq * hs + hs, :], r3(b.ap[:, :], hs), t)
                t_bias.append(b.free)
        t_aq, t_av, t_iq = [], [], []
        to_sbuf_t(w2[0:2], aq, t_aq)
        to_sbuf_t(w2[2:4], ak, t_aq)
        to_sbuf_t(w2[4:5], iq, t_iq)
        ws = r3(wsm, 8)
        b = bank()
        for k in range(8):
            f = mm(b.ap[:, 0:256], ws[:, k, 0:128], hT[:, k, :], k == 0, k == 7)
            if k == 7:
                t = T.do(f)
            else:
                T.plain(f, t_ga, b.free)
        A.do(lambda e, b=b: e.activation(ikE[0:64, :], b.ap[0:64, 0:256], ACT.Copy), t, z1)
        b.free = t_ik = A.do(lambda e, b=b: e.activation(ikO[64:128, :], b.ap[64:128, 0:256], ACT.Copy), t, z2)
        b = bank()
        for tt in range(2):
            for k in range(8):
                f = mm(b.ap[:, tt * 8:tt * 8 + 8], hT[:, k, tt * 128:tt * 128 + 128], ws[:, k, 128:136], k == 0, k == 7)
                if k == 7 and tt:
                    t = T.do(f)
                else:
                    T.plain(f, b.free)
        b.free = t_iw = V.do(lambda e, b=b: e.tensor_scalar(iw, r3(b.ap[:, 0:16], 2), IDX_SCALE, None, ALU.mult), t)
        to_sbuf_n(w2[5:7], av, t_av)
        t_oa = []
        for tt in range(2):
            n = 128 * (tt + 1)
            scn, sc2n = sc[:, 0:n], sc2[:, 0:n]
            qs = slice(tt * 128, tt * 128 + 128)
            for hp in range(4):
                b = bank()
                for j in range(2):
                    f = mm(b.ap[:, j * 256:j * 256 + n], iq[:, hp, qs], (ikO if j else ikE)[:, 0:n], True, True)
                    if j:
                        t = T.do(f)
                    else:
                        T.plain(f, b.free, t_ik, t_iq)
                rl = r3(rel, 2)[:, :, 0:n]
                b.free = k = A.do(lambda e, b=b, n=n, rl=rl: e.activation(rl, r3(b.ap[:, :], 2)[:, :, 0:n], ACT.Relu),
                                  t, V.last())
                for j in range(2):
                    h = 2 * hp + j
                    if h == 0:
                        V.do(lambda e, rl=rl, tt=tt, h=h, scn=scn: e.tensor_scalar(
                            scn, rl[:, 0, :], iw[:, tt, h:h + 1], None, ALU.mult), k, t_iw, G.last())
                    else:
                        V.do(lambda e, rl=rl, tt=tt, h=h, j=j, scn=scn: e.scalar_tensor_tensor(
                            out=scn, in0=rl[:, j, :], scalar=iw[:, tt, h:h + 1], in1=scn,
                            op0=ALU.mult, op1=ALU.add), k)
            t = G.do(lambda e, scn=scn, tt=tt, n=n: e.affine_select(
                out=scn, in_=scn, pattern=[[-1, n]], compare_op=ALU.is_ge, fill=-BIG,
                base=tt * 128, channel_multiplier=1), V.last())
            V.do(lambda e, scn=scn: e.max(m8, scn), t)
            V.do(lambda e, scn=scn, sc2n=sc2n: e.match_replace(sc2n, m8, scn, -BIG))
            for _ in range(7):
                V.do(lambda e, sc2n=sc2n: e.max(m8, sc2n))
                V.do(lambda e, sc2n=sc2n: e.match_replace(sc2n, m8, sc2n, -BIG))
            V.do(lambda e, scn=scn, sc2n=sc2n: e.tensor_tensor(sc2n, sc2n, scn, ALU.is_equal))
            L = Lb[:, 0:8 * n]
            L3 = r3(L, 8)
            for hp in range(4):
                b = bank()
                for j in range(2):
                    h = 2 * hp + j
                    f = mm(b.ap[:, j * 256:j * 256 + n], aq[:, h, qs], ak[:, h, 0:n], True, True)
                    if j:
                        t = T.do(f)
                    else:
                        T.plain(f, b.free, t_aq)
                Lh = L3[:, 2 * hp:2 * hp + 2, :]
                b.free = V.do(lambda e, b=b, Lh=Lh, tt=tt, hp=hp, n=n: e.scalar_tensor_tensor(
                    out=Lh, in0=r3(b.ap[:, :], 2)[:, :, 0:n], scalar=ATT_SCALE,
                    in1=bias[tt][:, 2 * hp:2 * hp + 2, :], op0=ALU.mult, op1=ALU.add), t, t_bias, t_pv if tt else t_bias)
            V.do(lambda e, L3=L3, n=n: e.scalar_tensor_tensor(
                out=L3, in0=free_dims(sc2, [0, 8], [1, n]), scalar=-1e30, in1=L3, op0=ALU.mult, op1=ALU.add))
            V.do(lambda e, L3=L3: e.tensor_reduce(mx[:, 0:8], L3, AX.X, ALU.max))
            V.do(lambda e, L3=L3, n=n: e.tensor_tensor(L3, L3, free_dims(mx[:, 0:8], [1, 8], [0, n]), ALU.subtract))
            k = A.do(lambda e, L=L: e.activation(L, L, ACT.Exp), V.last())
            V.do(lambda e, L3=L3: e.tensor_reduce(mx[:, 8:16], L3, AX.X, ALU.add), k)
            V.do(lambda e: e.reciprocal(mx[:, 16:24], mx[:, 8:16]))
            k = V.do(lambda e, L3=L3, n=n: e.tensor_tensor(L3, L3, free_dims(mx[:, 16:24], [1, 8], [0, n]), ALU.mult))
            t_pt = []
            for s in range(tt + 1):
                for hq in range(2):
                    b = bank()
                    for j in range(4):
                        f = (lambda e, b=b, j=j, hq=hq, s=s, L3=L3: e.transpose(
                            b.ap[:, j * 128:j * 128 + 128], L3[:, 4 * hq + j, s * 128:s * 128 + 128], ident))
                        if j == 3:
                            t = T.do(f)
                        else:
                            T.plain(f, b.free, k)
                    b.free = copy_out(hq, PT[s][:, 4 * hq:4 * hq + 4, :], r3(b.ap[:, :], 4), t)
                    t_pt.append(b.free)
            for hq in range(2):
                b = bank()
                for j in range(4):
                    h = 4 * hq + j
                    for s in range(tt + 1):
                        f = mm(b.ap[:, j * 128:j * 128 + 128], av[:, s, h * 128:h * 128 + 128], PT[s][:, h, :],
                               s == 0, s == tt)
                        if j == 3 and s == tt:
                            t = T.do(f)
                        else:
                            T.plain(f, b.free, t_pt, t_av)
                b.free = copy_out(hq, oaT[:, 4 * hq:4 * hq + 4, qs], r3(b.ap[:, :], 4), t)
                t_oa.append(b.free)
            t_pv = t_pt[-2:]
        gt = r3(Lb[:, 0:1024], 4)
        tmp2 = rel

        def gated(gsrc, wsrc, oT, nk, first, toks, gate):
            for n in range(2):
                tg = {}

                def evac(half, ps, t):
                    tg[half] = A.do(lambda e: e.activation(gate[:, 2 * half:2 * half + 2, :], r3(ps, 2), ACT.Sigmoid),
                                    t, V.last())
                    return tg[half]
                proj_t(chunk(gsrc[n]), hT, 8, evac)
                cks = [chunk(wsrc[n * (nk // 8) + i]) for i in range(nk // 8)]
                ws_ = [r3(c.ap, 8) for c in cks]
                for half in range(2):
                    t, k = branch([c.tok for c in cks], tmp,
                                  lambda blk: [(ws_[kk // 8][:, kk % 8, blk * 128:blk * 128 + 128], oT[:, kk, :])
                                               for kk in range(nk)],
                                  (2 * half, 2 * half + 1), gate[:, 2 * half:2 * half + 2, :], tg[half],
                                  4 * n + 2 * half, first, toks)
                for c in cks:
                    c.done = t
            return k

        tmp = r3(rel, 2)
        gated(w2[27:29], a["w_branch_a_2"], oaT, 8, True, t_oa, gt)

        toks = barrier()
        bq, bk, bb, bl, E, Gt = (ar(2048) for _ in range(6))
        bi, bg = r3(ar(2048), 2), r3(ar(2048), 2)
        acc = ar(2048)
        accx = ar(1024)
        masks = ar(8 * 128).bitcast(I32)
        lbt = ar(40)
        hg = ar(128)
        bls = ar(96)
        rel = ar(512)
        tmp = r3(rel, 2)
        sst = ar(96)
        g_b = group("hgrn")
        A.dma(g_b, lambda e: e.dma_start(masks, a["masks"]), toks)
        A.dma(g_b, lambda e: e.dma_start(lbt[:, 0:8], a["hgrn_lb_raw_2"]))
        t_gb = A.dma(g_b, lambda e: e.dma_start(hg, a["hgrn_norm_g_2"][0, :].partition_broadcast(P)))
        G.do(lambda e: e.memset(E, 1.0))
        t_rm = G.do(lambda e: e.memset(free_dims(E, [64, 32]), 0.0))
        G.do(lambda e: e.memset(acc, 0.0))
        V.do(lambda e: e.tensor_tensor(lbt[:, 8:16], lbt[:, 0:8], lbt[:, 0:8], ALU.subtract), t_gb)
        k = A.do(lambda e: e.activation(lbt[:, 16:24], lbt[:, 8:16], ACT.Exp), V.last())
        V.do(lambda e: e.reciprocal(lbt[:, 24:32], lbt[:, 16:24]), k)
        V.do(lambda e: e.tensor_tensor(lbt[:, 24:32], lbt[:, 24:32], lbt[:, 16:24], ALU.mult))
        V.do(lambda e: e.tensor_tensor(lbt[:, 24:32], lbt[:, 24:32], lbt[:, 24:32], ALU.subtract))
        V.do(lambda e: e.tensor_scalar(lbt[:, 32:40], lbt[:, 24:32], -1.0, 1.0, ALU.mult, ALU.add))
        t_bq, t_bf, t_bi, t_bg = [], [], [], []
        b3 = lambda ap: r3(ap, 8)
        to_sbuf_t(w2[9:11], b3(bk), t_bf, ACT.Sigmoid)
        to_sbuf_t(w2[7:9], b3(bq), t_bq)
        lb_b = free_dims(lbt[:, 24:32], [1, 8], [0, 256])
        om_b = free_dims(lbt[:, 32:40], [1, 8], [0, 256])
        V.do(lambda e: e.tensor_tensor(b3(bk), b3(bk), om_b, ALU.mult), t_bf)
        V.do(lambda e: e.tensor_tensor(b3(bk), b3(bk), lb_b, ALU.add))
        V.do(lambda e: e.tensor_scalar(bl, bk, 2.0 ** -63, None, ALU.max))
        k = A.do(lambda e: e.activation(bl, bl, ACT.Ln), V.last())
        V.do(lambda e: e.tensor_scalar(bk, bk, -1.0, 1.0, ALU.mult, ALU.add))
        t_b = V.do(lambda e: e.tensor_tensor_scan(bb, E, bl, 0.0, ALU.mult, ALU.add), k, t_rm)
        to_sbuf_n(w2[11:13], bi, t_bi)
        for n in range(2):
            def evac(tt, ps, t, n=n):
                d = bg[:, tt, n * 512:n * 512 + 512]
                k = A.do(lambda e: e.activation(d, ps, ACT.Sigmoid), t)
                k = V.do(lambda e: e.tensor_tensor(d, d, ps, ALU.mult), k)
                k = V.do(lambda e: e.tensor_tensor(r3(d, 4), r3(d, 4), free_dims(hg, [0, 4], [1, 128]), ALU.mult), t_gb)
                t_bg.append(k)
                return k
            proj_n(chunk(w2[13 + n]), hT, 8, evac)

        G3, acc3 = b3(Gt), r3(acc, 16)

        def pair_views(t, l):
            base = t[:, 0:1]
            even = free_dims(base, [2 * l, 1024 // l], [1, l])
            odd = free_dims(t[:, l:l + 1], [2 * l, 1024 // l], [1, l])
            return even, odd

        def products(m, lhs, rhs, k, first=False):
            last = None
            for q in range(4):
                b = bank()
                for j in range(4):
                    h, half = (4 * q + j) // 2, j % 2
                    sl = slice(half * 128, half * 128 + 128)
                    f = mm(b.ap[:, j * 128:j * 128 + 128], b3(lhs)[:, h, sl], b3(rhs)[:, h, sl], True, True)
                    if j == 3:
                        t = T.do(f)
                    else:
                        T.plain(f, b.free, k)
                b.free = V.do(lambda e, q=q, b=b: e.copy_predicated(
                    acc3[:, 4 * q:4 * q + 4, :], free_dims(masks[:, m * 128:m * 128 + 128], [0, 4], [1, 128]),
                    r3(b.ap[:, :], 4)), t, t_gb, G.last())
                last = b.free
            return t, last

        t_mm, t_acc = products(7, bk, bq, [t_b, t_bq])
        for lv in range(7):
            l = 1 << lv
            Ee, Eo = pair_views(E, l)
            be, bo = pair_views(bb, l)
            if l < 64:
                ref = free_dims(bb[:, l - 1:l], [2 * l, 1024 // l], [0, l])
                V.do(lambda e, Ee=Ee, ref=ref, be=be: e.tensor_tensor(Ee, ref, be, ALU.subtract), A.last())
                k = V.do(lambda e, Eo=Eo, ref=ref, bo=bo: e.tensor_tensor(Eo, bo, ref, ALU.subtract))
            else:
                ref = free_dims(bb[:, l - 1:l], [2 * l, 1024 // l], [0, l])
                V.do(lambda e, Ee=Ee, ref=ref, be=be: e.tensor_tensor(Ee, ref, be, ALU.subtract), A.last())
                k = V.do(lambda e, Eo=Eo, bo=bo: e.tensor_copy(Eo, bo))
            k = A.do(lambda e: e.activation(E, E, ACT.Exp), k)
            Ge, Go = pair_views(Gt, l)
            ke, _ = pair_views(bk, l)
            _, qo = pair_views(bq, l)
            V.do(lambda e, Ge=Ge, Ee=Ee, ke=ke: e.tensor_tensor(Ge, Ee, ke, ALU.mult), k, t_mm)
            k = V.do(lambda e, Go=Go, Eo=Eo, qo=qo: e.tensor_tensor(Go, Eo, qo, ALU.mult))
            t_mm, t_acc = products(lv, Gt, Gt, k)
        B4 = bb.rearrange("p (h c t) -> p h c t", h=8, c=4)
        E4 = E.rearrange("p (h c t) -> p h c t", h=8, c=4)
        lastc = lambda c: bb[:, c * 64 + 63:c * 64 + 64]
        v8 = lambda ap: free_dims(ap, [256, 8], [0, 64])
        V.do(lambda e: e.tensor_tensor(bls[:, 0:8], free_dims(lastc(0), [256, 8]), free_dims(lastc(1), [256, 8]), ALU.add))
        V.do(lambda e: e.tensor_tensor(E4[:, :, 0, :], free_dims(bls[:, 0:8], [1, 8], [0, 64]), B4[:, :, 0, :], ALU.subtract), A.last())
        V.do(lambda e: e.tensor_tensor(E4[:, :, 1, :], v8(lastc(1)), B4[:, :, 1, :], ALU.subtract))
        V.do(lambda e: e.tensor_copy(E4[:, :, 2, :], B4[:, :, 2, :]))
        k = V.do(lambda e: e.tensor_tensor(E4[:, :, 3, :], v8(lastc(2)), B4[:, :, 3, :], ALU.add))
        k = A.do(lambda e: e.activation(E, E, ACT.Exp), k)
        hv = lambda t, s: b3(t)[:, :, s * 128:s * 128 + 128]
        V.do(lambda e: e.tensor_tensor(hv(Gt, 0), hv(E, 0), hv(bk, 0), ALU.mult), k, t_mm)
        k = V.do(lambda e: e.tensor_tensor(hv(Gt, 1), hv(E, 1), hv(bq, 1), ALU.mult))
        accx3 = b3(accx)
        t_ax = []
        for q in range(2):
            b = bank()
            for j in range(4):
                h = 4 * q + j
                f = mm(b.ap[:, j * 128:j * 128 + 128], G3[:, h, 0:128], G3[:, h, 128:256], True, True)
                if j == 3:
                    t = T.do(f)
                else:
                    T.plain(f, b.free, k)
            b.free = copy_out(q, accx3[:, 4 * q:4 * q + 4, :], r3(b.ap[:, :], 4), t)
            t_ax.append(b.free)
        oN = r3(bq, 2)
        sqj = bk
        t_on = [T.last(), V.last()]
        for tt in range(2):
            for q in range(2):
                b = bank()
                for j in range(4):
                    h = 4 * q + j
                    o = b.ap[:, j * 128:j * 128 + 128]
                    v = slice(h * 128, h * 128 + 128)
                    if tt:
                        T.plain(mm(o, accx3[:, h, :], bi[:, 0, v], True, False), b.free, t_ax, t_bi)
                    f = mm(o, acc3[:, 2 * h + tt, :], bi[:, tt, v], tt == 0, True)
                    if j == 3:
                        t = T.do(f, t_acc)
                    else:
                        T.plain(f, b.free, t_acc, t_bi)
                t_o = copy_out(q, oN[:, tt, q * 512:q * 512 + 512], b.ap[:, :], t, t_on)
                b.free = t_o
                t_on = [t_on, t_o] if not isinstance(t_on, list) else t_on + [t_o]
        V.do(lambda e: e.tensor_tensor(sqj, bq, bq, ALU.mult), t_on)
        h_ss, h_ms, h_sq, h_r, h_t = (sst[:, 16 * i:16 * i + 16] for i in range(5))
        V.do(lambda e: e.tensor_reduce(h_ss, r3(sqj, 16), AX.X, ALU.add))
        k = V.do(lambda e: e.tensor_scalar(h_ms, h_ss, 1.0 / 128, 1e-6, ALU.mult, ALU.add))
        k = A.do(lambda e: e.activation(h_sq, h_ms, ACT.Sqrt), k)
        inv_sqrt(h_r, h_sq, h_ms, h_t, k)
        V.do(lambda e: e.tensor_tensor(r3(bq, 16), r3(bq, 16), free_dims(h_r, [1, 16], [0, 128]), ALU.mult))
        k = V.do(lambda e: e.tensor_tensor(oN, oN, bg, ALU.mult), t_bg)
        obT = b3(bb)
        t_ob = transposes(oN, obT, 8, k)
        gated(w2[29:31], a["w_branch_b_2"], obT, 8, False, t_ob, r3(E[:, 0:1024], 4))

        toks = barrier()
        cq, ck_, rq, rk = (ar(2048) for _ in range(4))
        ocT = r3(ar(16 * 256), 16)
        rel = ar(512)
        tmp = r3(rel, 2)
        rt1, rt2 = ar(1024), ar(1024)
        at0, at1 = r3(ar(1024), 4), r3(ar(512), 4)
        cv = [r3(ar(1024), 2) for _ in range(2)]
        cg = [r3(ar(1024), 2) for _ in range(2)]
        oc = [r3(ar(1024), 2) for _ in range(2)]
        tab = ar(1536)
        gt = r3(ar(1024), 4)
        sjunk = rt2[:, 0:512]
        cst_ = ar(40)
        g_t = group("ret")
        t_gt = A.dma(g_t, lambda e: e.dma_start(tab, a["cst"][:, C_COS:C_COS + 1536]), toks)
        cosb = free_dims(tab[:, 0:256], [0, 4], [1, 256])
        sinb = free_dims(tab[:, 256:512], [0, 4], [1, 256])
        dec = tab[:, 512:1536]
        t_rot = []
        for src, dst, eng, tp, ws_ in ((cq, rq, V, (rt1, rt2), w2[15:17]), (ck_, rk, V, (rt1, rt2), w2[17:19])):
            tk = []
            to_sbuf_t(ws_, b3(src), tk)
            ev = lambda t: t.rearrange("p (h e t) -> p h e t", h=4, e=2)
            s0, s1 = ev(src)[:, :, 0, :], ev(src)[:, :, 1, :]
            d0, d1 = ev(dst)[:, :, 0, :], ev(dst)[:, :, 1, :]
            u0, u1 = r3(tp[0], 4), r3(tp[1], 4)
            eng.do(lambda e, u0=u0, s0=s0: e.tensor_tensor(u0, s0, cosb, ALU.mult), tk, t_gt)
            eng.do(lambda e, u1=u1, s1=s1: e.tensor_tensor(u1, s1, sinb, ALU.mult))
            eng.do(lambda e, u0=u0, u1=u1, d0=d0: e.tensor_tensor(d0, u0, u1, ALU.subtract))
            eng.do(lambda e, u0=u0, s1=s1: e.tensor_tensor(u0, s1, cosb, ALU.mult))
            eng.do(lambda e, u1=u1, s0=s0: e.tensor_tensor(u1, s0, sinb, ALU.mult))
            t_rot.append(eng.do(lambda e, u0=u0, u1=u1, d1=d1: e.tensor_tensor(d1, u0, u1, ALU.add)))
        rq3, rk3 = b3(rq), b3(rk)
        t_at = []
        for h in range(4):
            b = bank()
            for e2 in range(2):
                T.plain(mm(b.ap[:, 0:256], rk3[:, 2 * h + e2, 0:128], rq3[:, 2 * h + e2, :], e2 == 0, e2 == 1),
                        b.free, t_rot)
            for e2 in range(2):
                f = mm(b.ap[:, 256:384], rk3[:, 2 * h + e2, 128:256], rq3[:, 2 * h + e2, 128:256], e2 == 0, e2 == 1)
                if e2:
                    t = T.do(f)
                else:
                    T.plain(f)
            V.do(lambda e, h=h, b=b: e.tensor_tensor(at0[:, h, :], b.ap[:, 0:256], dec[:, h * 256:h * 256 + 256], ALU.mult), t)
            b.free = V.do(lambda e, h=h, b=b: e.tensor_tensor(at1[:, h, :], b.ap[:, 256:384],
                                                              dec[:, h * 256:h * 256 + 128], ALU.mult))
            t_at.append(b.free)
        oc_free = [None, None]
        cv_free = [None, None]
        cg_free = [None, None]
        t_oc = []
        for h in range(4):
            i = h % 2
            tv, tg = [], []

            def evac_v(tt, ps, t):
                k = copy_out(tt, cv[i][:, tt, :], ps, t, cv_free[i])
                tv.append(k)
                return k

            def evac_g(tt, ps, t):
                k = A.do(lambda e, o=cg[i][:, tt, :]: e.activation(o, ps, ACT.Sigmoid), t, cg_free[i])
                k = V.do(lambda e, o=cg[i][:, tt, :]: e.tensor_tensor(o, o, ps, ALU.mult), k)
                tg.append(k)
                return k
            i_ = i
            proj_n(chunk(w2[19 + h]), hT, 8, evac_v)
            proj_n(chunk(w2[23 + h]), hT, 8, evac_g)
            o0 = cst_[:, 0:1]
            bs = []
            for tt in range(2):
                b = bank()
                if tt == 0:
                    t = T.do(mm(b.ap[:, :], at0[:, h, 0:128], cv[i][:, 0, :], True, True), b.free, tv, t_at)
                else:
                    T.plain(mm(b.ap[:, :], at0[:, h, 128:256], cv[i][:, 0, :], True, False), b.free)
                    t = T.do(mm(b.ap[:, :], at1[:, h, :], cv[i][:, 1, :], False, True))
                k = A.do(lambda e, b=b, tt=tt: e.activation(sjunk, b.ap[:, :], ACT.Square,
                                                            accum_out=cst_[:, tt:tt + 1]), t, V.last())
                bs.append(b)
            cv_free[i] = t
            ms, sq, r_, t_ = (cst_[:, 8 * q:8 * q + 2] for q in range(1, 5))
            k = V.do(lambda e, ms=ms: e.tensor_scalar(ms, cst_[:, 0:2], 1.0 / 512, 1e-6, ALU.mult, ALU.add), k)
            k = A.do(lambda e, ms=ms, sq=sq: e.activation(sq, ms, ACT.Sqrt), k)
            inv_sqrt(r_, sq, ms, t_, k)
            for tt in range(2):
                bs[tt].free = k = V.do(lambda e, tt=tt, i=i, b=bs[tt], r_=r_: e.scalar_tensor_tensor(
                    out=oc[i][:, tt, :], in0=b.ap[:, :], scalar=r_[:, tt:tt + 1], in1=cg[i][:, tt, :],
                    op0=ALU.mult, op1=ALU.mult), oc_free[i], tg)
            cg_free[i] = k
            t_oc += transposes(oc[i], ocT[:, 4 * h:4 * h + 4, :], 4, k)
            oc_free[i] = T.last()
        t_m = gated(w2[31:33], a["w_branch_c_2"], ocT, 16, False, t_oc, gt)

        k0 = row_load(A, g_r[0], 0, mod_d[2, :], V.last())
        for n in range(2):
            def evac(tt, ps, t, n=n):
                k = V.do(lambda e: e.tensor_tensor(rel, ps, grow[0][:, n * 512:n * 512 + 512], ALU.mult), t, k0)
                V.do(lambda e: e.tensor_tensor(x[:, tt, n * 512:n * 512 + 512], x[:, tt, n * 512:n * 512 + 512],
                                               rel, ALU.add))
                return k
            proj_n(chunk(a["w_out_2"][n]), mT, 8, evac, t_m)

        toks = barrier()
        Gb = ar(32 * 256)
        sgb = [ar(1024) for _ in range(2)]
        hg2 = [r3(ar(1024), 4) for _ in range(2)]
        hN = r3(ar(2048), 2)
        junk = ar(1024)
        rw = ar(8 * 36)
        rbb = ar(36)
        lg = ar(72)
        sc4 = ar(96)
        s8 = ar(200)
        gat = ar(64)
        gatT = ar(256)
        g_o = group("moe")
        A.dma(g_o, lambda e: e.dma_start(rw, a["rw"]), toks)
        t_go = A.dma(g_o, lambda e: e.dma_start(rbb, a["rb"][0, :].partition_broadcast(P)))
        ht = transposes(hN, hT, 8, modulated(a["norm2_g_2"][0, :], 4, 3, hN, junk))
        b = bank()
        rw3 = r3(rw, 8)
        for tt in range(2):
            for k in range(8):
                f = mm(b.ap[:, tt * 36:tt * 36 + 36], hT[:, k, tt * 128:tt * 128 + 128], rw3[:, k, :], k == 0, k == 7)
                if tt and k == 7:
                    t = T.do(f)
                else:
                    T.plain(f, b.free, ht, t_go)
        lg3 = r3(lg, 2)
        b.free = V.do(lambda e, b=b: e.tensor_tensor(lg3, r3(b.ap[:, 0:72], 2), free_dims(rbb, [0, 2], [1, 36]), ALU.add), t, t_go)
        gl = lg3[:, :, 0:4]
        vv = lambda o, n: free_dims(sc4[:, o:o + 1], [n, 2], [1, n])
        vb = lambda o, n: free_dims(sc4[:, o:o + 1], [1, 2], [0, n])
        gmx, gsum, gp = sc4[:, 0:2], sc4[:, 2:4], sc4[:, 4:6]
        eqg, ohg = vv(8, 4), vv(16, 4)

        def first_one(dst, src, mx_o, n, tmp_o):
            V.do(lambda e: e.tensor_reduce(sc4[:, mx_o:mx_o + 2], src, AX.X, ALU.max))
            V.do(lambda e: e.tensor_tensor(dst, src, vb(mx_o, n), ALU.is_equal))
            rank = free_dims(iota[:, 0:1], [0, 2], [1, n])
            V.do(lambda e: e.scalar_tensor_tensor(out=dst, in0=rank, scalar=-16.0, in1=dst, op0=ALU.add, op1=ALU.mult))
            V.do(lambda e: e.tensor_reduce(sc4[:, tmp_o:tmp_o + 2], dst, AX.X, ALU.min))
            return V.do(lambda e: e.tensor_tensor(dst, dst, vb(tmp_o, n), ALU.is_equal))

        first_one(ohg, gl, 0, 4, 24)
        V.do(lambda e: e.tensor_tensor(eqg, gl, vb(0, 4), ALU.subtract))
        k = A.do(lambda e: e.activation(sc4[:, 8:16], sc4[:, 8:16], ACT.Exp), V.last())
        V.do(lambda e: e.tensor_reduce(gsum, eqg, AX.X, ALU.add), k)
        V.do(lambda e: e.reciprocal(gp, gsum))
        el = free_dims(lg[:, 4:5], [36, 2], [1, 8], [8, 4])
        prod = s8[:, 0:64]
        V.do(lambda e: e.tensor_tensor(free_dims(prod, [32, 2], [4, 8], [1, 4]), el,
                                       free_dims(sc4[:, 16:17], [4, 2], [0, 8], [1, 4]), ALU.mult))
        ing = r3(s8[:, 64:80], 2)
        V.do(lambda e: e.tensor_reduce(s8[:, 64:80], free_dims(prod, [4, 16], [1, 4]), AX.X, ALU.add))
        oh1, oh2, in2 = r3(s8[:, 80:96], 2), r3(s8[:, 96:112], 2), r3(s8[:, 112:128], 2)
        first_one(oh1, ing, 26, 8, 28)
        V.do(lambda e: e.scalar_tensor_tensor(out=in2, in0=oh1, scalar=-BIG, in1=ing, op0=ALU.mult, op1=ALU.add))
        first_one(oh2, in2, 30, 8, 32)
        gex, den, w1 = sc4[:, 34:36], sc4[:, 36:38], sc4[:, 38:40]
        k = V.do(lambda e: e.tensor_tensor(gex, sc4[:, 30:32], sc4[:, 26:28], ALU.subtract))
        k = A.do(lambda e: e.activation(gex, gex, ACT.Exp), k)
        V.do(lambda e: e.tensor_scalar(den, gex, 1.0, None, ALU.add), k)
        V.do(lambda e: e.reciprocal(w1, den))
        V.do(lambda e: e.tensor_tensor(w1, w1, gp, ALU.mult))
        V.do(lambda e: e.tensor_tensor(gex, gex, w1, ALU.mult))
        V.do(lambda e: e.tensor_tensor(oh1, oh1, vb(38, 8), ALU.mult))
        V.do(lambda e: e.tensor_tensor(oh2, oh2, vb(34, 8), ALU.mult))
        V.do(lambda e: e.tensor_tensor(oh1, oh1, oh2, ALU.add))
        k = V.do(lambda e: e.tensor_tensor(free_dims(gat, [32, 2], [8, 4], [1, 8]),
                                           free_dims(sc4[:, 16:17], [4, 2], [1, 4], [0, 8]),
                                           free_dims(s8[:, 80:81], [8, 2], [0, 4], [1, 8]), ALU.mult))
        b = bank()
        for tt in range(2):
            f = (lambda e, tt=tt, b=b: e.transpose(b.ap[0:32, tt * 128:tt * 128 + 128], gat[:, tt * 32:tt * 32 + 32], ident))
            if tt:
                t = T.do(f)
            else:
                T.plain(f, b.free, k)
        b.free = k = V.do(lambda e, b=b: e.tensor_copy(gatT[0:32, :], b.ap[0:32, 0:256]), t)
        t_gg = []
        for e2 in range(16):
            b = bank()
            for j in range(2):
                f = mm(b.ap[:, j * 256:j * 256 + 256], free_dims(ident[0:32, 2 * e2 + j:2 * e2 + j + 1], [0, 128]),
                       gatT[0:32, :], True, True)
                if j:
                    t = T.do(f)
                else:
                    T.plain(f, b.free, k)
            b.free = copy_out(e2, Gb[:, e2 * 512:e2 * 512 + 512], b.ap[:, :], t)
            t_gg.append(b.free)
        t_gg = t_gg[-2:]

        y = [banks[4 + i] for i in range(4)]
        yfree = [q.free for q in y]
        usable[:] = [0, 1, 2, 3]
        t_down = {}

        def up(ex):
            cg_, cu_ = chunk(a["eg"][ex]), chunk(a["eu"][ex])
            wg, wu = r3(cg_.ap, 8), r3(cu_.ap, 8)
            s, h = sgb[ex % 2], hg2[ex % 2]
            toks = []
            for half in range(2):
                bg_, bu_ = bank(), bank()
                for b, w, c in ((bg_, wg, cg_), (bu_, wu, cu_)):
                    for j in range(2):
                        blk = 2 * half + j
                        for k in range(8):
                            f = mm(b.ap[:, j * 256:j * 256 + 256], w[:, k, blk * 128:blk * 128 + 128],
                                   hT[:, k, :], k == 0, k == 7)
                            if j and k == 7:
                                c.done = T.do(f)
                            else:
                                T.plain(f, c.tok, b.free)
                sh = s[:, half * 512:half * 512 + 512]
                bg_.free = k = A.do(lambda e, bg_=bg_, sh=sh: e.activation(sh, bg_.ap[:, :], ACT.Silu), cg_.done,
                                    (t_down.get((ex, half))))
                bu_.free = V.do(lambda e, bu_=bu_, sh=sh: e.tensor_tensor(sh, sh, bu_.ap[:, :], ALU.mult), k, cu_.done)
                k = V.do(lambda e, sh=sh, h=h, half=half: e.tensor_tensor(
                    h[:, 2 * half:2 * half + 2, :], r3(sh, 2),
                    free_dims(Gb[:, ex * 256:ex * 256 + 256], [0, 2], [1, 256]), ALU.mult), t_gg, t_down.get(ex - 2))
                t_down[ex + 2, half] = k
                toks.append(k)
            return toks

        def down(ex, toks):
            c = chunk(a["ed"][ex])
            w = r3(c.ap, 4)
            h = hg2[ex % 2]
            for tt in range(2):
                for n in range(2):
                    b = y[2 * tt + n]
                    for k in range(4):
                        f = mm(b.ap[:, :], h[:, k, tt * 128:tt * 128 + 128], w[:, k, n * 512:n * 512 + 512],
                               ex == 0 and k == 0, ex == 31 and k == 3)
                        if k == 3 and tt and n:
                            c.done = T.do(f)
                        else:
                            T.plain(f, c.tok, toks, yfree)
            t_down[ex] = c.done

        prev = up(0)
        for ex in range(32):
            nxt = up(ex + 1) if ex < 31 else None
            down(ex, prev)
            prev = nxt
        k0 = row_load(A, g_r[0], 0, mod_d[5, :], V.last())
        k1 = row_load(A, g_r[1], 1, a["final_norm_g_2"], V.last())
        for tt in range(2):
            for n in range(2):
                V.do(lambda e, tt=tt, n=n: e.tensor_tensor(junk[:, 0:512], y[2 * tt + n].ap[:, :],
                                                           grow[0][:, n * 512:n * 512 + 512], ALU.mult), k0, t_down[31])
                t_x = V.do(lambda e, tt=tt, n=n: e.tensor_tensor(
                    x[:, tt, n * 512:n * 512 + 512], x[:, tt, n * 512:n * 512 + 512], junk[:, 0:512], ALU.add))
        t_f = rmsnorm(x, grow[1][:, :], hN, junk, 1024, t_x, k1)
        g_out = group("out")
        t_out = A.dma(g_out, lambda e: e.dma_start(out.rearrange("b (t p) d -> p (b t) d", p=P), hN), t_f)
        A.wait(t_out)

        block = ctx.enter_context(nc.Block())

        @block.sync
        def _(e):
            for c in chunks:
                if c.n >= RING:
                    e.wait_ge(*chunks[c.n - RING].done)
                e.dma_start(ring[c.slot][:, 0:c.cols], c.src).then_inc(c.tok[0], 16)

        @block.tensor
        def _(e):
            for f in T.ops:
                f(e)

        @block.vector
        def _(e):
            for f in V.ops:
                f(e)

        @block.scalar
        def _(e):
            for f in A.ops:
                f(e)

        @block.gpsimd
        def _(e):
            for f in G.ops:
                f(e)


def top16(V, src, tmp, vals, idx, *toks):
    V.do(lambda e: e.max(vals[:, 0:8], src), *toks)
    V.do(lambda e: e.max_index(idx[:, 0:8], vals[:, 0:8], src))
    V.do(lambda e: e.match_replace(tmp, vals[:, 0:8], src, -BIG))
    V.do(lambda e: e.max(vals[:, 8:16], tmp))
    V.do(lambda e: e.max_index(idx[:, 8:16], vals[:, 8:16], tmp))


def constants():
    c = np.zeros((P, C_END), np.float32)
    c[:, C_ID:C_ID + 128] = np.eye(128)
    c[:, C_IOTA:C_IOTA + 16] = np.arange(16)
    pos = np.arange(256, dtype=np.float32)
    theta = (np.float32(1.0) / np.power(np.float32(10000.0), np.linspace(0.0, 1.0, 128, dtype=np.float32))).astype(np.float32)
    ang = (theta[:, None] * pos[None, :]).astype(np.float32).astype(np.float64)
    c[:, C_COS:C_COS + 256] = np.cos(ang)
    c[:, C_SIN:C_SIN + 256] = np.sin(ang)
    s, t = np.arange(128)[:, None], np.arange(256)[None, :]
    for h in range(4):
        g = np.log(1.0 - 2.0 ** (-5.0 - h))
        d = np.where(t >= s, np.exp((t - s) * g), 0.0) * (256.0 ** -0.5)
        c[:, C_DEC + h * 256:C_DEC + h * 256 + 256] = d
    for g, w in enumerate((2, 4, 8, 16)):
        c[:, C_INV + g * 256:C_INV + g * 256 + 256] = 1.0 / np.minimum(np.arange(256) + 1, w)
    rel = np.maximum(255 - np.arange(512), 0)
    relf = np.maximum(rel, 1).astype(np.float32)
    large = 16 + (np.log(relf / np.float32(16)) / np.float32(np.log(8.0)) * np.float32(16)).astype(np.int32)
    bucket = np.where(rel < 16, rel, np.minimum(large, 31))
    c[bucket, C_OH + np.arange(512)] = 1.0
    c[:, C_OH + 512:C_OH + 640] = np.eye(128)[::-1]
    m = np.zeros((P, 8, 128), np.int32)
    s, t = np.arange(128)[:, None], np.arange(128)[None, :]
    for lv in range(7):
        l = 1 << lv
        m[:, lv, :] = (s // (2 * l) == t // (2 * l)) & ((s // l) % 2 == 0) & ((t // l) % 2 == 1)
    m[:, 7, :] = s == t
    return c, m.reshape(P, 1024)


def kernel(**inputs):
    import concourse.bacc as bacc
    from concourse.bass_utils import run_bass_kernel_spmd

    i = {k: np.asarray(v) for k, v in inputs.items()}

    def cols(w, cw=512):
        k, n = w.shape
        return w.reshape(k // 128, 128, n // cw, cw).transpose(2, 1, 0, 3).reshape(n // cw, 128, -1)

    def rows(w):
        k, n = w.shape
        return w.reshape(k // 128, 128, n).transpose(1, 0, 2).reshape(128, -1)

    w2 = i["w_in_2"][0]
    offs = np.cumsum([0, 1024, 1024, 1024, 512, 64, 8] + [1024] * 4 + [1024, 1024, 2048, 2048] + [1024] * 3)
    aq, ak, av, iq, ik, iw, bq, bf, bi, bg, cq, ck, cv, cg, ga, gb, gc = (
        w2[:, offs[n]:offs[n + 1]] for n in range(17))
    pairs = lambda w: w.reshape(1024, 4, 128, 2).transpose(0, 1, 3, 2).reshape(1024, 1024)
    big = np.concatenate([aq, ak, iq, av, bq, bf, bi, bg, pairs(cq), pairs(ck), cv, cg, ga, gb, gc], axis=1)
    wc = i["w_branch_c_2"][0]
    cst, masks = constants()
    arrays = {
        "x": i["x"], "cst": cst, "masks": masks,
        "g_mix": i["g_mix"], "g_ffn": i["g_ffn"], "g_final": i["g_final"],
        "w_in": cols(i["w_in"][0]),
        "pgw": i["pool_group_w"][0].transpose(1, 0, 2).reshape(128, 512),
        "pcs": i["pool_scale"][0].reshape(4, 128).T,
        "cvw": i["conv_w"][0].reshape(3, 4, 128).transpose(2, 0, 1).reshape(128, 12),
        "wbp": rows(i["w_branch_pool"][0]), "wbc": rows(i["w_branch_conv"][0]),
        "w_out": cols(i["w_out"][0]), "w_q": cols(i["w_q"][0]),
        "skT": i["sub_keys"][0].transpose(3, 0, 1, 2).reshape(128, 2048),
        "expert_u": i["expert_u"][0], "expert_v": i["expert_v"][0],
        "c_2": i["c_2"].reshape(8, 128).T, "ada_w_2": cols(i["ada_w_2"][0]), "ada_b_2": i["ada_b_2"],
        "norm1_g_2": i["norm1_g_2"], "norm2_g_2": i["norm2_g_2"], "final_norm_g_2": i["final_norm_g_2"],
        "w_in_2": cols(big), "w_small": rows(np.concatenate([ik, ik, iw], axis=1)),
        "rel_bias_2": i["rel_bias_2"],
        "hgrn_lb_raw_2": i["hgrn_lb_raw_2"].reshape(8, 128).T, "hgrn_norm_g_2": i["hgrn_norm_g_2"],
        "w_branch_a_2": cols(i["w_branch_a_2"][0]), "w_branch_b_2": cols(i["w_branch_b_2"][0]),
        "w_branch_c_2": np.concatenate([cols(wc[0:1024]), cols(wc[1024:2048])], axis=1).reshape(4, 128, 4096),
        "w_out_2": cols(i["w_out_2"][0]),
        "rw": rows(np.concatenate([i["router_group_w_2"][0], i["router_expert_w_2"][0]], axis=1)),
        "rb": np.concatenate([i["router_group_b_2"], i["router_expert_b_2"]], axis=1),
        "eg": i["expert_w_gate_2"][0].reshape(32, 8, 128, 512).transpose(0, 2, 1, 3).reshape(32, 128, 4096),
        "eu": i["expert_w_up_2"][0].reshape(32, 8, 128, 512).transpose(0, 2, 1, 3).reshape(32, 128, 4096),
        "ed": i["expert_w_down_2"][0].reshape(32, 4, 128, 1024).transpose(0, 2, 1, 3).reshape(32, 128, 4096),
    }
    nc = bacc.Bacc("TRN2", target_bir_lowering=False, num_devices=1)
    feed, aps = {}, {}
    for name, v in arrays.items():
        feed["in_" + name] = np.ascontiguousarray(v)
        aps[name] = nc.dram_tensor("in_" + name, v.shape, mybir.dt.from_np(v.dtype), kind="ExternalInput").ap()
    out = nc.dram_tensor("out_0", (1, 256, 1024), F32, kind="ExternalOutput").ap()
    build(nc, aps, out)
    r = run_bass_kernel_spmd(nc, [feed], core_ids=[0])
    return r.results[0]["out_0"]
```

```python
from contextlib import ExitStack

import numpy as np
import concourse.bass as bass
from concourse import mybir

F32 = mybir.dt.float32
F32R = mybir.dt.float32r
U32 = mybir.dt.uint32
I32 = mybir.dt.int32
ALU = mybir.AluOpType
ACT = mybir.ActivationFunctionType
AX = mybir.AxisListType

P = 128
RING = 3
PARTS = 4
NGB = 9
CAP = 128
BIG = 3.0e38
IDX_SCALE = float(512) ** -0.5
ATT_SCALE = float(128) ** -0.5

C_ID, C_IOTA = 0, 128
C_COS, C_SIN, C_DEC, C_INV, C_OH = 144, 400, 656, 1680, 2704
C_MOE = 2704 + 640
C_END = C_MOE + 384


class Queue:

    def __init__(self, sem, linked):
        self.sem, self.linked = sem, linked
        self.count, self.ops, self.met = 0, [], {}

    def wait(self, *tokens):
        for t in tokens:
            if not t:
                continue
            if isinstance(t, list):
                self.wait(*t)
                continue
            sem, value = t
            if self.met.get(sem.name, 0) < value:
                self.met[sem.name] = value
                self.ops.append(lambda e, s=sem, v=value: e.wait_ge(s, v))

    def last(self):
        return (self.sem, self.count) if self.count else None

    def do(self, fn, *tokens):
        if self.linked:
            self.wait(self.last())
        self.wait(*tokens)
        self.count += 1
        self.ops.append(lambda e: fn(e).then_inc(self.sem, 1))
        return (self.sem, self.count)

    def plain(self, fn, *tokens):
        self.wait(*tokens)
        self.ops.append(fn)

    def dma(self, group, fn, *tokens):
        self.wait(*tokens)
        group.count += 16
        self.ops.append(lambda e: fn(e).then_inc(group.sem, 16))
        return (group.sem, group.count)


class Group:

    def __init__(self, sem):
        self.sem, self.count = sem, 0


class Chunk:

    def __init__(self, n, src, cols, sems):
        self.n, self.src, self.cols, self.slot = n, src, cols, n % RING
        self.tok = (sems[n % RING], 16 * (n // RING + 1))
        self.done = None


class Bank:
    def __init__(self, ap):
        self.ap, self.free = ap, None


class Part:

    def __init__(self, chunk, view, last, eng):
        self.chunk, self.view, self.last, self.eng = chunk, view, last, eng


class Splitter:

    def __init__(self, T, A, chunk, bufs):
        self.T, self.A, self.chunk, self.bufs = T, A, chunk, bufs
        self.free = [None] * len(bufs)
        self.parts, self.taken, self.made = [], 0, 0

    def expect(self, src, engines, cut):
        c = self.chunk(src)
        c.done = []
        for q in range(4):
            if cut == "cols":
                v = c.ap.rearrange("p (k n) -> p k n", k=8)[:, :, q * 128:q * 128 + 128]
            else:
                v = c.ap[:, q * 1024:q * 1024 + 1024]
            self.parts.append(Part(c, v, q == 3, engines[q % len(engines)]))

    def ahead(self, n):
        while self.made < min(n, len(self.parts)):
            self.split(self.made)
            self.made += 1

    def take(self):
        n = self.taken
        self.taken += 1
        self.ahead(n + PARTS)
        return self.parts[n]

    def split(self, n):
        p, i = self.parts[n], n % PARTS
        hi, lo = self.bufs[i]
        if p.view.ndim == 3:
            hi, lo = (t.rearrange("p (k n) -> p k n", k=8) for t in (hi, lo))
        p.hi, p.lo = hi, lo
        a = self.A.do(lambda e: e.activation(hi, p.view, ACT.Copy), p.chunk.tok, self.free[i])
        p.tok = p.eng.do(lambda e: e.tensor_tensor(lo, p.view, hi.bitcast(F32), ALU.subtract), a, p.chunk.tok,
                         self.free[i])
        p.chunk.done = [a, p.tok] + p.chunk.done[:3]

    def give(self, p, token):
        self.free[self.parts.index(p) % PARTS] = token


def free_dims(ap, *dims):
    return bass.AP(tensor=ap.tensor, offset=ap.offset, ap=[list(ap.ap[0])] + [list(d) for d in dims])


def build(nc, a, out):
    ctx = ExitStack()
    with ctx:
        def sb(name, n, dt=F32):
            return ctx.enter_context(nc.sbuf_tensor(name, [P, n], dt))

        def sem(name):
            return ctx.enter_context(nc.semaphore(name))

        ring = [sb(f"ring{i}", 4096) for i in range(RING)]
        x_t = sb("x", 2048)
        grow = [sb(f"g{i}", 1024) for i in range(4)]
        cid = sb("cid", 144)
        st = sb("st", 64)
        banks = [Bank(ctx.enter_context(nc.psum_tensor(f"ps{i}", [P, 512], F32))[:, :]) for i in range(8)]
        mod_d = nc.dram_tensor("mod_scratch", [6, 1024], F32, kind="Internal").ap()
        rr_d = nc.dram_tensor("rr_scratch", [8, 512], F32, kind="Internal").ap()

        ring_sems = [sem(f"s_ring{i}") for i in range(RING)]
        V = Queue(sem("s_dve"), True)
        A = Queue(sem("s_act"), True)
        G = Queue(sem("s_pool"), True)
        T = Queue(sem("s_pe"), False)

        def group(name):
            return Group(sem("d_" + name))

        chunks = []

        def chunk(src, cols=4096):
            c = Chunk(len(chunks), src, cols, ring_sems)
            chunks.append(c)
            c.ap = ring[c.slot][:, 0:cols]
            return c

        usable = list(range(8))
        turn = [0]

        def bank():
            b = banks[usable[turn[0] % len(usable)]]
            turn[0] += 1
            return b

        scopes = [ExitStack()]
        names = [0]

        def ar(n, dt=F32):
            names[0] += 1
            return scopes[-1].enter_context(nc.sbuf_tensor(f"t{names[0]}", [P, n], dt))[:, :]

        def inner():
            scopes.append(ExitStack())

        def leave():
            scopes.pop().close()

        def barrier():
            toks = [q.last() for q in (T, A, V, G)]
            for q in (T, A, V, G):
                q.wait(*toks)
            return toks

        def split_bufs():
            return [(ar(1024, F32R), ar(1024, F32R)) for _ in range(PARTS)]

        def r3(ap, n):
            return ap.rearrange("p (a b) -> p a b", a=n)

        def mm(o, l, r, start, stop):
            return lambda e: e.matmul(o, l, r, start=start, stop=stop)

        x = r3(x_t[:, :], 2)
        ident = cid[:, C_ID:C_ID + 128]
        iota = cid[:, C_IOTA:C_IOTA + 16]

        g_c, g_x = group("const"), group("x")
        A.dma(g_x, lambda e: e.dma_start(x, a["x"].rearrange("b (t p) d -> p (b t) d", p=P)))
        A.dma(g_x, lambda e: e.dma_start(cid[:, :], a["cst"][:, 0:144]))
        def row_load(q, grp, i, src, *toks):
            return q.dma(grp, lambda e: e.dma_start(grow[i][:, :], src.partition_broadcast(P)), *toks)

        t_x0 = row_load(A, g_x, 0, a["g_mix"][0, :])
        inner()
        hold = ar(2048)
        inner()
        pgw = ar(512)
        invc = ar(1024)
        pcs = ar(4)
        cvw = ar(12)
        A.dma(g_c, lambda e: e.dma_start(pgw, a["pgw"]))
        A.dma(g_c, lambda e: e.dma_start(invc, a["cst"][:, C_INV:C_INV + 1024]))
        A.dma(g_c, lambda e: e.dma_start(pcs, a["pcs"]))
        A.dma(g_c, lambda e: e.dma_start(cvw, a["cvw"]))

        row_load(A, g_c, 1, a["g_ffn"][0, :])
        cs, csg, one = ar(8), ar(8), ar(1)
        adab = ar(512)
        row_load(A, g_c, 2, a["g_final"])
        A.dma(g_c, lambda e: e.dma_start(cs, a["c_2"]))
        c_tok = A.dma(g_c, lambda e: e.dma_start(adab[0:12, :], a["ada_b_2"].rearrange("o (n c) -> (o n) c", n=12)))

        def rmsnorm(src, g, dst, junk, cols, *toks, tiles=(0, 1)):
            first, end = tiles[0], tiles[-1] + 1
            ss, (ms, sq, r, t) = st[:, 0:2], (st[:, 2 * i + first:2 * i + end] for i in range(1, 5))
            for tt in tiles:
                s = A.do(lambda e, tt=tt: e.activation(junk, src[:, tt, :], ACT.Square,
                                                       accum_out=ss[:, tt:tt + 1]), *toks)
            m = V.do(lambda e: e.tensor_scalar(ms, ss[:, first:end], 1.0 / cols, 1e-6, ALU.mult, ALU.add), s)
            s = A.do(lambda e: e.activation(sq, ms, ACT.Sqrt), m)
            inv_sqrt(r, sq, ms, t, s)
            for tt in tiles:
                k = V.do(lambda e, tt=tt: e.scalar_tensor_tensor(
                    out=dst[:, tt, :], in0=src[:, tt, :], scalar=st[:, 6 + tt:7 + tt], in1=g,
                    op0=ALU.mult, op1=ALU.mult), *toks)
            return k

        def inv_sqrt(r, sq, ms, t, *toks):
            V.do(lambda e: e.reciprocal(r, sq), *toks)
            V.do(lambda e: e.tensor_tensor(t, r, r, ALU.mult))
            V.do(lambda e: e.tensor_tensor(t, t, ms, ALU.mult))
            V.do(lambda e: e.tensor_scalar(t, t, -0.5, 1.5, ALU.mult, ALU.add))
            return V.do(lambda e: e.tensor_tensor(r, r, t, ALU.mult))

        def copy_out(n, dst, src, *toks):
            if n % 2:
                return A.do(lambda e: e.activation(dst, src, ACT.Copy), *toks)
            return V.do(lambda e: e.tensor_copy(dst, src), *toks)

        def transposes(src, dst, nk, *toks):
            got = []
            for kp in range(nk // 2):
                b = bank()
                for kk in range(2):
                    for tt in range(2):
                        o = b.ap[:, kk * 256 + tt * 128:kk * 256 + tt * 128 + 128]
                        i = src[:, tt, (2 * kp + kk) * 128:(2 * kp + kk + 1) * 128]
                        f = (lambda e, o=o, i=i: e.transpose(o, i, ident))
                        if kk and tt:
                            t = T.do(f, *toks)
                        else:
                            T.plain(f, b.free, *toks)
                k = copy_out(kp, dst[:, 2 * kp:2 * kp + 2, :], r3(b.ap[:, :], 2), t)
                b.free = k
                got.append(k)
            return got[-2:]

        def transposes_split(src, hi, lo, nk, *toks):
            got = []
            for kp in range(nk // 2):
                b = bank()
                for kk in range(2):
                    for tt in range(2):
                        o = b.ap[:, kk * 256 + tt * 128:kk * 256 + tt * 128 + 128]
                        i = src[:, tt, (2 * kp + kk) * 128:(2 * kp + kk + 1) * 128]
                        f = (lambda e, o=o, i=i: e.transpose(o, i, ident))
                        if kk and tt:
                            t = T.do(f, *toks)
                        else:
                            T.plain(f, b.free, *toks)
                h, l, ps = hi[:, 2 * kp:2 * kp + 2, :], lo[:, 2 * kp:2 * kp + 2, :], r3(b.ap, 2)
                k = A.do(lambda e, h=h, ps=ps: e.activation(h, ps, ACT.Copy), t)
                b.free = V.do(lambda e, h=h, l=l, ps=ps: e.tensor_tensor(l, ps, h.bitcast(F32), ALU.subtract), k)
                got.append(b.free)
            return got[-1]

        def proj_t(sp, rhs, evac, *toks):
            xh, xl = rhs
            for half in range(2):
                b = bank()
                for j in range(2):
                    p = sp.take()
                    o = b.ap[:, j * 256:j * 256 + 256]
                    for k in range(8):
                        T.plain(mm(o, p.lo[:, k, :], xh[:, k, :], k == 0, False), p.tok, b.free, *toks)
                    for k in range(8):
                        T.plain(mm(o, p.hi[:, k, :], xl[:, k, :], False, False))
                    for k in range(8):
                        f = mm(o, p.hi[:, k, :], xh[:, k, :], False, k == 7)
                        if k == 7:
                            t = T.do(f)
                        else:
                            T.plain(f)
                    sp.give(p, t)
                    if j == 1:
                        b.free = evac(half, b.ap, t)
                    yield

        def proj_n(sp, lhs, evac, *toks):
            xh, xl = lhs
            bs = [bank(), bank()]
            for q in range(4):
                p = sp.take()
                ts = []
                for tt in range(2):
                    rows = slice(tt * 128, tt * 128 + 128)
                    for kk in range(2):
                        k, w = 2 * q + kk, slice(kk * 512, kk * 512 + 512)
                        T.plain(mm(bs[tt].ap, xh[:, k, rows], p.hi[:, w], k == 0, False), p.tok, bs[tt].free, *toks)
                        T.plain(mm(bs[tt].ap, xl[:, k, rows], p.hi[:, w], False, False))
                        f = mm(bs[tt].ap, xh[:, k, rows], p.lo[:, w], False, k == 7)
                        if kk == 1:
                            ts.append(T.do(f))
                        else:
                            T.plain(f)
                sp.give(p, ts[1])
                if q == 3:
                    for tt in range(2):
                        bs[tt].free = evac(tt, bs[tt].ap, ts[tt])
                yield

        def go(gen, beside=lambda: None):
            for _ in gen:
                beside()

        hT = (r3(ar(2048, F32R), 8), r3(ar(2048, F32R), 8))
        hN_f = ar(2048)
        hN = r3(hN_f, 2)
        pf_f = ar(1024)
        pp = [r3(ar(n * 272), n) for n in (4, 4, 3, 2, 1)]
        cu = r3(ar(4 * 258), 4)
        zb, zv, aT, bT = (r3(ar(1024), 4) for _ in range(4))
        pf, cy = r3(pf_f, 4), zv
        mT = r3(ar(2048), 8)
        tmp = r3(ar(512), 2)
        sp = Splitter(T, A, chunk, split_bufs())
        msum = [ar(512) for _ in range(2)]
        modr = [ar(512) for _ in range(2)]
        c_ada = []

        def ada_chunk():
            c_ada.append(chunk(a["ada_w_2"][len(c_ada)]))

        for n in range(6):
            sp.expect(a["w_in"][n], [G, V], "cols")
            ada_chunk()
        c_wbp = chunk(a["wbp"])
        for n in range(6, 8):
            sp.expect(a["w_in"][n], [G, V], "cols")
            ada_chunk()
        c_wbc = chunk(a["wbc"])
        ada_chunk()
        ada_chunk()
        c_wo = []
        for n in range(2):
            c_wo.append(chunk(a["w_out"][n]))
            ada_chunk()
        t_ones = G.do(lambda e: e.memset(one, 1.0))
        z1 = G.do(lambda e: e.memset(pp[0][:, :, 0:16], 0.0))
        z2 = G.do(lambda e: e.memset(cu[:, :, 0:2], 0.0))
        ht = transposes_split(hN, hT[0], hT[1], 8, rmsnorm(x, grow[0][:, :], hN, pf_f, 1024, t_x0))
        k = A.do(lambda e: e.activation(csg, cs, ACT.Sigmoid), c_tok)
        t_cs = V.do(lambda e: e.tensor_tensor(csg, csg, cs, ALU.mult), k)
        g_md = [group(f"mod{i}") for i in range(2)]
        t_om = [None, None]

        def modulation():
            t_am = [None, None]
            ended = []

            def summed(n, i):
                b = bank()
                T.plain(mm(b.ap[0:1, :], one, msum[i], True, False), c_ada[n].done, b.free, t_ones)
                t_am[i] = T.do(mm(b.ap[0:1, :], ident[0:12, n:n + 1], adab[0:12, :], False, True))
                return b

            def stored(n, i, b):
                b.free = A.do(lambda e: e.activation(modr[i][0:1, :], b.ap[0:1, :], ACT.Copy), t_am[i], t_om[i])
                t_om[i] = A.dma(g_md[i], lambda e: e.dma_start(
                    mod_d[n // 2:n // 2 + 1, n % 2 * 512:n % 2 * 512 + 512], modr[i][0:1, :]), b.free)

            for n, c in enumerate(c_ada):
                i, w = n % 2, r3(c.ap, 8)
                V.do(lambda e, i=i, w=w: e.tensor_scalar(msum[i], w[:, 0, :], csg[:, 0:1], None, ALU.mult),
                     c.tok, t_cs, t_am[i])
                yield
                for k in range(1, 8):
                    c.done = V.do(lambda e, i=i, w=w, k=k: e.scalar_tensor_tensor(
                        out=msum[i], in0=w[:, k, :], scalar=csg[:, k:k + 1], in1=msum[i], op0=ALU.mult, op1=ALU.add))
                    if n and k == 3:
                        ended.append(summed(n - 1, 1 - i))
                    if n and k == 6:
                        stored(n - 1, 1 - i, ended.pop())
                    yield
            yield
            yield
            b = summed(11, 1)
            yield
            stored(11, 1, b)

        ada = modulation()

        def pour(n=2):
            for _ in range(n):
                next(ada, None)

        pre = {}
        for name, dst, off in (("p", pp[0], 16), ("c", cu, 2), ("b", zb, 0), ("v", zv, 0)):
            def evac(half, ps, t, dst=dst, off=off, name=name):
                k = copy_out(1, dst[:, 2 * half:2 * half + 2, off:off + 256], r3(ps, 2), t)
                pre.setdefault(name, []).append(k)
                return k
            go(proj_t(sp, hT, evac, ht), pour)

        for lv in range(4):
            d = 1 << lv
            lo = 2 * d - 1
            V.do(lambda e, lv=lv, d=d, lo=lo: e.tensor_tensor(
                pp[lv + 1][:, :, lo:272], pp[lv][:, lv > 0:, lo:272], pp[lv][:, lv > 0:, lo - d:272 - d], ALU.add),
                pre["p"], z1)
            V.do(lambda e, lv=lv: e.tensor_tensor(pf[:, lv, :], pp[lv + 1][:, 0, 16:272],
                                                  invc[:, lv * 256:lv * 256 + 256], ALU.mult))
        t_pf = V.do(lambda e: e.tensor_tensor(pf, pf, pp[0][:, :, 16:272], ALU.subtract))
        t_a = []
        for half in range(2):
            b = bank()
            for j in range(2):
                g = 2 * half + j
                f = mm(b.ap[:, j * 256:j * 256 + 256], pgw[:, g * 128:g * 128 + 128], pf[:, g, :], True, True)
                if j:
                    t = T.do(f)
                else:
                    T.plain(f, t_pf, b.free)
            for j in range(2):
                g = 2 * half + j
                k = A.do(lambda e, g=g, j=j, b=b: e.activation(aT[:, g, :], b.ap[:, j * 256:j * 256 + 256],
                                                               ACT.Copy, scale=pcs[:, g:g + 1]), t)
            b.free = k
            t_a.append(k)
        V.do(lambda e: e.tensor_tensor(cu[:, :, 2:258], cu[:, :, 2:258], zv, ALU.mult), pre["c"], pre["v"], z2)
        for g in range(4):
            V.do(lambda e, g=g: e.tensor_scalar(cy[:, g, :], cu[:, g, 0:256], cvw[:, g:g + 1], None, ALU.mult))
            for k in (1, 2):
                V.do(lambda e, g=g, k=k: e.scalar_tensor_tensor(
                    out=cy[:, g, :], in0=cu[:, g, k:k + 256], scalar=cvw[:, 4 * k + g:4 * k + g + 1],
                    in1=cy[:, g, :], op0=ALU.mult, op1=ALU.add))
        t_b = V.do(lambda e: e.tensor_tensor(bT, cy, zb, ALU.mult), pre["b"])

        sg = r3(hN_f, 8)

        def gates(sp, dst, free, *toks):
            got = []

            def make():
                for n in range(2):
                    def evac(half, ps, t, n=n):
                        k = A.do(lambda e: e.activation(dst[:, 4 * n + 2 * half:4 * n + 2 * half + 2, :], r3(ps, 2),
                                                        ACT.Sigmoid), t, free)
                        got.append(k)
                        return k
                    yield from proj_t(sp, hT, evac, *toks)
            return got, make()

        def branch(c, tmp, kts, blks, sgs, tsg, m0, first, *toks):
            m_ = mT[:, m0:m0 + 2, :]
            """Two blocks of 128 columns of a branch at a time, gated, into mT."""
            b = bank()
            for j, blk in enumerate(blks):
                for n, (l, r) in enumerate(kts(blk)):
                    f = mm(b.ap[:, j * 256:j * 256 + 256], l, r, n == 0, n == len(kts(blk)) - 1)
                    if j == 1 and n == len(kts(blk)) - 1:
                        t = T.do(f)
                    else:
                        T.plain(f, c, b.free, *toks)
            if first:
                k = V.do(lambda e: e.tensor_tensor(m_, sgs, r3(b.ap[:, :], 2), ALU.mult), t, tsg)
                b.free = k
            else:
                b.free = V.do(lambda e: e.tensor_tensor(tmp, sgs, r3(b.ap[:, :], 2), ALU.mult), t, tsg)
                k = V.do(lambda e: e.tensor_tensor(m_, m_, tmp, ALU.add))
            return t, k

        t_m = None
        for br, (c, rhs, toks) in enumerate(((c_wbp, aT, t_a), (c_wbc, bT, t_b))):
            t_sg, make = gates(sp, sg, t_m)
            go(make, pour)
            w = r3(c.ap, 4)
            for q in range(4):
                t, t_m = branch(c.tok, tmp,
                                lambda blk, w=w, rhs=rhs: [(w[:, k, blk * 128:blk * 128 + 128], rhs[:, k, :])
                                                           for k in range(4)],
                                (2 * q, 2 * q + 1), sg[:, 2 * q:2 * q + 2, :], t_sg[q],
                                2 * q, br == 0, toks)
                if br:
                    pour(4)
            c.done = t

        for tt in range(2):
            for n in range(2):
                b = bank()
                w = r3(c_wo[n].ap, 8)
                for k in range(8):
                    f = mm(b.ap, mT[:, k, tt * 128:tt * 128 + 128], w[:, k, :], k == 0, k == 7)
                    if k == 7:
                        c_wo[n].done = t = T.do(f)
                    else:
                        T.plain(f, c_wo[n].tok, b.free, t_m)
                xs = x[:, tt, n * 512:n * 512 + 512]
                b.free = V.do(lambda e, b=b, xs=xs: e.tensor_tensor(xs, xs, b.ap, ALU.add), t)
            t_h2 = rmsnorm(x, grow[1][:, :], r3(hold, 2), pf_f, 1024, V.last(), tiles=(tt,))
            pour(8)
        pour(100)
        t_md = list(t_om)

        barrier()
        leave()
        inner()
        hN = r3(hold, 2)
        idx_u = ar(256).bitcast(U32)
        wts = ar(256)
        act = ar(256)
        S_f = ar(2 * 16 * 128)
        S = S_f.rearrange("p (t h k) -> p t h k", t=2, h=16)
        S2 = ar(256)
        tops = ar(512).rearrange("p (t h k) -> p t h k", t=2, h=16)
        topi = ar(512).bitcast(U32).rearrange("p (t h k) -> p t h k", t=2, h=16)
        topf = ar(512).rearrange("p (t h k) -> p t h k", t=2, h=16)
        cand = ar(2048)
        oh = cand
        junk = cand[:, 0:1024]
        fs = ar(256)
        fp = ar(256).bitcast(U32)
        fa = ar(256).bitcast(U32)
        faf = ar(256)
        ab = [ar(256) for _ in range(2)]
        sm = ar(64)
        qT_f = ar(4096)
        qT = r3(qT_f, 16)
        inner()
        hT = (r3(ar(2048, F32R), 8), r3(ar(2048, F32R), 8))
        rb, ohb, rrs = ar(8), ar(512), ar(512)
        sp = Splitter(T, A, chunk, split_bufs())
        sk_f = ar(2048)
        for n in range(4):
            sp.expect(a["w_q"][n], [G], "cols")
        g_rr, g_rb, g_sk = group("rr"), group("rb"), group("sk")
        t_sk = A.dma(g_sk, lambda e: e.dma_start(sk_f, a["skT"]))
        A.dma(g_rb, lambda e: e.dma_start(rb[0:32, :], a["rel_bias_2"]))
        t_rb = A.dma(g_rb, lambda e: e.dma_start(ohb, a["cst"][:, C_OH:C_OH + 512]))
        gbs = [group(f"gb{i}") for i in range(NGB)]
        ht = transposes_split(hN, hT[0], hT[1], 8, t_h2)

        def bc(ap2, off, *dims):
            return free_dims(ap2[:, off:off + 1], *dims)

        flat = lambda ap: ap.rearrange("p t h k -> p (t h k)")
        tops_f, topi_f, topf_f = flat(tops), flat(topi), flat(topf)
        t_idx = {}

        def picks(tt, q):
            o, first = tt * 256 + 64 * q, tt * 128 + 32 * q
            fr = slice(first, first + 32)
            cq = cand[:, 512 * q:512 * q + 512]
            grid = free_dims(cq, [256, 2], [16, 16], [1, 16])
            steps = []

            def v(fn, *toks):
                steps.append(lambda: V.do(fn, *toks))

            def top16(src, tmp, vals, idx, *toks):
                v(lambda e: e.max(vals[:, 0:8], src), *toks)
                v(lambda e: e.max_index(idx[:, 0:8], vals[:, 0:8], src))
                v(lambda e: e.match_replace(tmp, vals[:, 0:8], src, -BIG))
                v(lambda e: e.max(vals[:, 8:16], tmp))
                v(lambda e: e.max_index(idx[:, 8:16], vals[:, 8:16], tmp))

            for hp in range(4 * q, 4 * q + 4):
                top16(S[:, tt, hp, :], S2[:, 0:128], tops[:, tt, hp, :], topi[:, tt, hp, :], t_s[tt, q])
            v(lambda e: e.tensor_copy(topf_f[:, o:o + 64], topi_f[:, o:o + 64]))
            v(lambda e: e.tensor_tensor(grid, bc(tops_f, o, [32, 2], [1, 16], [0, 16]),
                                        bc(tops_f, o + 16, [32, 2], [0, 16], [1, 16]), ALU.add))
            for h in range(2):
                f0 = first + h * 16
                top16(cq[:, h * 256:h * 256 + 256], S2, fs[:, f0:f0 + 16], fp[:, f0:f0 + 16])
            for half in range(2):
                if half == 0:
                    v(lambda e: e.tensor_scalar(fa[:, fr], fp[:, fr], 4, None, ALU.logical_shift_right))
                else:
                    v(lambda e: e.tensor_scalar(fa[:, fr], fp[:, fr], 15, None, ALU.bitwise_and))
                v(lambda e: e.tensor_copy(faf[:, fr], fa[:, fr]))
                v(lambda e: e.tensor_tensor(grid, bc(faf, first, [16, 2], [1, 16], [0, 16]),
                                            bc(iota, 0, [0, 2], [0, 16], [1, 16]), ALU.is_equal), c_tok)
                v(lambda e, half=half: e.tensor_tensor(
                    grid, grid, bc(topf_f, o + 16 * half, [32, 2], [0, 16], [1, 16]), ALU.mult))
                v(lambda e, half=half: e.tensor_reduce(ab[half][:, fr], free_dims(cq, [16, 32], [1, 16]), AX.X, ALU.add))
            v(lambda e: e.scalar_tensor_tensor(out=ab[0][:, fr], in0=ab[0][:, fr], scalar=128.0, in1=ab[1][:, fr],
                                               op0=ALU.mult, op1=ALU.add))

            def index():
                t_idx[tt, q] = V.do(lambda e: e.tensor_copy(idx_u[:, fr], ab[0][:, fr]))
            steps.append(index)
            return steps

        def softmax(tt):
            fr = slice(tt * 128, tt * 128 + 128)
            w3, f3 = r3(wts[:, fr], 8), r3(fs[:, fr], 8)
            s0 = 32 * tt
            t = V.do(lambda e: e.tensor_tensor(w3, f3, free_dims(fs[:, tt * 128:tt * 128 + 1], [16, 8], [0, 16]),
                                               ALU.subtract))
            k = A.do(lambda e: e.activation(wts[:, fr], wts[:, fr], ACT.Exp), t)
            V.do(lambda e: e.tensor_reduce(sm[:, s0:s0 + 8], w3, AX.X, ALU.add), k)
            V.do(lambda e: e.reciprocal(sm[:, s0 + 8:s0 + 16], sm[:, s0:s0 + 8]))
            V.do(lambda e: e.tensor_tensor(w3, w3, free_dims(sm[:, s0 + 8:s0 + 9], [1, 8], [0, 16]), ALU.mult))

        t_q, t_s = {}, {}
        sk = r3(sk_f, 16)

        def scores(q):
            for tt in range(2):
                b = bank()
                for j in range(4):
                    hp = 4 * q + j
                    f = mm(b.ap[:, j * 128:j * 128 + 128], qT[:, hp, tt * 128:tt * 128 + 128], sk[:, hp, :], True, True)
                    if j == 3:
                        t = T.do(f)
                    else:
                        T.plain(f, t_sk, b.free, t_q[q])
                t_s[tt, q] = b.free = A.do(lambda e, tt=tt, b=b: e.activation(
                    S[:, tt, 4 * q:4 * q + 4, :], r3(b.ap, 4), ACT.Copy), t)

        now = []
        for n in range(4):
            t_q[n] = []

            def evac(half, ps, t, n=n):
                k = A.do(lambda e: e.activation(qT[:, 4 * n + 2 * half:4 * n + 2 * half + 2, :], r3(ps, 2), ACT.Copy), t)
                t_q[n].append(k)
                return k
            for part, _ in enumerate(proj_t(sp, hT, evac, ht)):
                if n and part == 0:
                    scores(n - 1)
                    now += picks(0, n - 1)
                for step in now[:16]:
                    step()
                now = now[16:]
        scores(3)
        t_qT = T.last()
        for step in now + picks(0, 3):
            step()
        softmax(0)
        b = bank()
        t = T.do(mm(b.ap[0:8, :], rb[0:32, :], ohb[0:32, :], True, True), t_rb, b.free)
        b.free = t_bt = A.do(lambda e, b=b: e.activation(rrs[0:8, :], b.ap[0:8, :], ACT.Copy), t)
        t_rr = A.dma(g_rr, lambda e: e.dma_start(rr_d, rrs[0:8, :]), b.free)
        leave()
        gb = [qT_f[:, 0:2048], qT_f[:, 2048:4096], S_f[:, 0:2048]] + [ar(2048) for _ in range(NGB - 3)]
        diag = [ar(128) for _ in range(4)]
        t_S0 = V.last()
        g_r = [group(f"row{i}") for i in range(4)]
        k0 = row_load(A, g_r[0], 0, a["norm1_g_2"][0, :], t_h2)
        k1 = row_load(A, g_r[1], 1, mod_d[1, :], t_h2, t_md)
        t_sh = row_load(A, g_r[3], 3, mod_d[0, :], t_md)

        def scale_rows(s_row, g_row, *toks):
            return V.do(lambda e: e.scalar_tensor_tensor(
                out=grow[s_row][:, :], in0=grow[s_row][:, :], scalar=1.0, in1=grow[g_row][:, :],
                op0=ALU.add, op1=ALU.mult), *toks)

        scale_rows(1, 0, k0, k1)

        def finish(tt):
            rmsnorm(x, grow[2][:, :], x, junk, 1024, V.last(), tiles=(tt,))
            rmsnorm(x, grow[1][:, :], hN, junk, 1024, V.last(), tiles=(tt,))
            rows = hN[:, tt, :]
            return V.do(lambda e: e.tensor_tensor(rows, rows, grow[3][:, :], ALU.add), t_sh)

        gfree = [[t_qT], [t_qT], [t_S0]] + [[t_qT, t_rr]] * (NGB - 3)
        ng = [0]
        got = {}

        def gather(col):
            s = ng[0] % NGB
            ng[0] += 1
            t = G.dma(gbs[s], lambda e: e.indirect_dma_start(
                out=gb[s], out_offset=None, in_=a["expert_uv"],
                in_offset=bass.IndirectOffsetOnAxis(ap=idx_u[:, col:col + 1], axis=0)), t_idx[col // 128, col % 128 // 32], gfree[s])
            got[col] = (s, t)

        def dots(c0):
            for col in range(c0, c0 + 2):
                gather(col)
                s, t = got[col]
                V.do(lambda e, s=s, col=col, hN=hN: e.tensor_tensor_reduce(
                    out=gb[s][:, 0:1024], in0=gb[s][:, 0:1024], in1=hN[:, col // 128, :], scale=1.0, scalar=0.0,
                    op0=ALU.mult, op1=ALU.add, accum_out=act[:, col:col + 1]), t)
            got["act", c0] = A.do(lambda e: e.activation(act[:, c0:c0 + 2], act[:, c0:c0 + 2], ACT.Gelu), V.last())

        def add_picks(tt):
            for n in range(2):
                xs, b = x[:, tt, n * 512:n * 512 + 512], sums[tt][n]
                b.free = V.do(lambda e, b=b, xs=xs: e.tensor_tensor(xs, xs, b.ap, ALU.add), T.last())

        sums = [[bank(), bank()] for _ in range(2)]
        free = {bk: bk.free for bks in sums for bk in bks}
        later = [step for q in range(4) for step in picks(1, q)] + [lambda: softmax(1)]
        n_later = len(later)
        t_dg = [t_rr] * 4
        dots(0)
        for c0 in range(0, 256, 2):
            while later and len(later) > n_later - n_later * (c0 + 2) // 120:
                later.pop(0)()
            if c0 + 2 < 256:
                dots(c0 + 2)
            k = V.do(lambda e, c0=c0: e.tensor_tensor(wts[:, c0:c0 + 2], wts[:, c0:c0 + 2], act[:, c0:c0 + 2], ALU.mult),
                     got["act", c0])
            for col in range(c0, c0 + 2):
                s, i, tt = got[col][0], col % 4, col // 128
                d = A.do(lambda e, i=i, col=col: e.activation(diag[i], ident, ACT.Copy, scale=wts[:, col:col + 1]),
                         k, t_dg[i])
                T.plain(mm(sums[tt][0].ap, diag[i], gb[s][:, 1024:1536], col % 128 == 0, col % 128 == 127),
                        d, [free[bk] for bk in sums[tt]])
                gfree[s] = t_dg[i] = T.do(mm(sums[tt][1].ap, diag[i], gb[s][:, 1536:2048], col % 128 == 0, col % 128 == 127))
            if c0 % 128 == 126:
                add_picks(c0 // 128)
                t_hold = finish(c0 // 128)

        w2 = a["w_in_2"]
        barrier()
        leave()
        inner()
        hT = (r3(ar(2048, F32R), 8), r3(ar(2048, F32R), 8))
        mT = r3(ar(2048), 8)
        sg = r3(hold, 8)
        rel = ar(512)
        tmp = r3(rel, 2)
        sp = Splitter(T, A, chunk, split_bufs())

        def run_t(dst, n, toks_out, fn=ACT.Copy):
            def evac(half, ps, t):
                d = dst[:, 4 * n + 2 * half:4 * n + 2 * half + 2, :]
                k = A.do(lambda e: e.activation(d, r3(ps, 2), fn), t)
                toks_out.append(k)
                return k
            return proj_t(sp, hT, evac, ht)

        def run_n(dst, n, toks_out):
            def evac(tt, ps, t):
                d = dst[:, tt, n * 512:n * 512 + 512]
                k = A.do(lambda e: e.activation(d, ps, ACT.Copy), t)
                toks_out.append(k)
                return k
            return proj_n(sp, hT, evac, ht)

        def run_silu(dst, toks_out, free, fix=None):
            def evac(tt, ps, t):
                d = dst[tt]
                k = A.do(lambda e: e.activation(d, ps, ACT.Sigmoid), t, free)
                k = V.do(lambda e: e.tensor_tensor(d, d, ps, ALU.mult), k)
                k2 = V.do(lambda e: e.tensor_tensor(r3(d, 4), r3(d, 4), fix, ALU.mult)) if fix is not None else k
                toks_out.append(k2)
                return k
            return proj_n(sp, hT, evac, ht)

        def wire(names):
            raw = {}
            for name in names:
                kind, src = name[0], name[1]
                if kind == "t":
                    sp.expect(src, name[2], "cols")
                elif kind == "n":
                    sp.expect(src, name[2], "rows")
                else:
                    raw.setdefault(name[2], []).append(chunk(src))
            return raw

        GV, GG = [G, V], [G]
        wa, wb, wc = a["w_branch_a_2"], a["w_branch_b_2"], a["w_branch_c_2"]
        raw = wire([("t", w2[4], GV)] + [("t", w2[n], GG) for n in range(4)] + [("n", w2[5], GG), ("n", w2[6], GG)]
                   + [("t", w2[27], GG), ("t", w2[28], GV)] + [("raw", wa[n], "a") for n in range(2)]
                   + [("t", w2[n], GV) for n in (9, 10, 7, 8)] + [("n", w2[n], GV) for n in (11, 12)]
                   + [("n", w2[n], GG) for n in (13, 14)] + [("t", w2[n], GG) for n in (29, 30)]
                   + [("raw", wb[n], "b") for n in range(2)]
                   + [("t", w2[n], GV) for n in range(15, 19)]
                   + [("n", w2[b0 + h], GV) for h in range(4) for b0 in (19, 23)]
                   + [("t", w2[31], GV), ("t", w2[32], GV)] + [("raw", wc[n], "c") for n in range(4)]
                   + [("raw", a["w_out_2"][n], "o") for n in range(2)])

        def merge(cks, oT, nk, first, toks, t_sg):
            for n in range(2):
                cs_ = cks[n * (nk // 8):(n + 1) * (nk // 8)]
                ws_ = [r3(c.ap, 8) for c in cs_]
                for half in range(2):
                    t, k = branch([c.tok for c in cs_], tmp,
                                  lambda blk: [(ws_[kk // 8][:, kk % 8, blk * 128:blk * 128 + 128], oT[:, kk, :])
                                               for kk in range(nk)],
                                  (2 * half, 2 * half + 1), sg[:, 4 * n + 2 * half:4 * n + 2 * half + 2, :],
                                  t_sg[2 * n + half], 4 * n + 2 * half, first, toks)
                for c in cs_:
                    c.done = t
            return k

        inner()
        toks = [T.last(), A.last(), V.last(), G.last()]
        t_gt1 = row_load(A, g_r[0], 0, mod_d[2, :], toks)
        k1 = row_load(A, g_r[1], 1, mod_d[4, :], toks)
        t_sh = row_load(A, g_r[2], 2, mod_d[3, :], toks)
        k3 = row_load(A, g_r[3], 3, a["norm2_g_2"][0, :], toks)
        aq_f, ak_f = ar(2048), ar(2048)
        aq, ak = r3(aq_f, 8), r3(ak_f, 8)
        iq = r3(ar(1024), 4)
        ikE, ikO = ar(256), ar(256)
        iw = r3(ar(16), 2)
        bias = [r3(ar(8 * 128), 8), r3(ar(8 * 256), 8)]
        Ls = [ar(8 * 128), ar(8 * 256)]
        sc = [ar(128), ar(256)]
        sc2 = [ar(128), ar(256)]
        m8 = ar(8)
        mx = ar(48)
        inner()
        wsm = ar(8 * 136)
        wsh, wsl = ar(8 * 136, F32R), ar(8 * 136, F32R)
        flip = ar(128)
        g_a = group("att")
        A.dma(g_a, lambda e: e.dma_start(wsm, a["w_small"]), toks)
        t_ga = A.dma(g_a, lambda e: e.dma_start(flip, a["cst"][:, C_OH + 512:C_OH + 640]))
        ht = transposes_split(r3(hold, 2), hT[0], hT[1], 8, t_hold)
        z1 = G.do(lambda e: e.memset(ikE, 0.0))
        z2 = G.do(lambda e: e.memset(ikO, 0.0))
        g_rev = group("rev")
        k = A.do(lambda e: e.activation(wsh, wsm, ACT.Copy), t_ga)
        t_ws = V.do(lambda e: e.tensor_tensor(wsl, wsm, wsh.bitcast(F32), ALU.subtract), k)
        for tt in range(2):
            n = 128 * (tt + 1)
            for h in range(8):
                t_rev = A.dma(g_rev, lambda e, tt=tt, n=n, h=h: e.dma_start(
                    bias[tt][:, h, :], bass.AP(tensor=rr_d.tensor, offset=h * 512 + 128 - tt * 128,
                                               ap=[[1, 128], [1, n]])), t_rr)
        t_aq, t_av, t_iq, t_oa = [], [], [], []
        t_rows = scale_rows(1, 3, k1, k3)
        t_gf = row_load(A, g_r[3], 3, a["final_norm_g_2"], t_rows)
        go(run_t(iq, 0, t_iq))
        w3h, w3l = r3(wsh, 8), r3(wsl, 8)
        b = bank()
        for k in range(8):
            o = b.ap[:, 0:256]
            T.plain(mm(o, w3h[:, k, 0:128], hT[0][:, k, :], k == 0, False), t_ws, b.free)
            T.plain(mm(o, w3h[:, k, 0:128], hT[1][:, k, :], False, False))
            f = mm(o, w3l[:, k, 0:128], hT[0][:, k, :], False, k == 7)
            if k == 7:
                t = T.do(f)
            else:
                T.plain(f)
        A.do(lambda e, b=b: e.activation(ikE[0:64, :], b.ap[0:64, 0:256], ACT.Copy), t, z1)
        b.free = t_ik = A.do(lambda e, b=b: e.activation(ikO[64:128, :], b.ap[64:128, 0:256], ACT.Copy), t, z2)
        b = bank()
        for tt in range(2):
            o = b.ap[:, tt * 8:tt * 8 + 8]
            for k in range(8):
                xs = slice(tt * 128, tt * 128 + 128)
                T.plain(mm(o, hT[0][:, k, xs], w3h[:, k, 128:136], k == 0, False), b.free)
                T.plain(mm(o, hT[1][:, k, xs], w3h[:, k, 128:136], False, False))
                f = mm(o, hT[0][:, k, xs], w3l[:, k, 128:136], False, k == 7)
                if k == 7 and tt:
                    t = T.do(f)
                else:
                    T.plain(f)
        b.free = t_iw = V.do(lambda e, b=b: e.tensor_scalar(iw, r3(b.ap[:, 0:16], 2), IDX_SCALE, None, ALU.mult), t)

        for tt in range(2):
            n = 128 * (tt + 1)
            qs = slice(tt * 128, tt * 128 + 128)
            rl3 = r3(Ls[tt], 8)
            for hp in range(4):
                b = bank()
                for j in range(2):
                    f = mm(b.ap[:, j * 256:j * 256 + n], iq[:, hp, qs], (ikO if j else ikE)[:, 0:n], True, True)
                    if j:
                        t = T.do(f)
                    else:
                        T.plain(f, b.free, t_ik, t_iq)
                rl = rl3[:, 2 * hp:2 * hp + 2, :]
                b.free = k = A.do(lambda e, b=b, n=n, rl=rl: e.activation(rl, r3(b.ap[:, :], 2)[:, :, 0:n], ACT.Relu), t)
                for j in range(2):
                    h = 2 * hp + j
                    if h == 0:
                        V.do(lambda e, rl=rl, tt=tt, h=h: e.tensor_scalar(
                            sc[tt], rl[:, 0, :], iw[:, tt, h:h + 1], None, ALU.mult), k, t_iw)
                    else:
                        V.do(lambda e, rl=rl, tt=tt, h=h, j=j: e.scalar_tensor_tensor(
                            out=sc[tt], in0=rl[:, j, :], scalar=iw[:, tt, h:h + 1], in1=sc[tt],
                            op0=ALU.mult, op1=ALU.add), k)
            t_af = G.do(lambda e, tt=tt, n=n: e.affine_select(
                out=sc[tt], in_=sc[tt], pattern=[[-1, n]], compare_op=ALU.is_ge, fill=-BIG,
                base=tt * 128, channel_multiplier=1), V.last())
            V.do(lambda e, tt=tt: e.max(m8, sc[tt]), t_af)
            V.do(lambda e, tt=tt: e.match_replace(sc2[tt], m8, sc[tt], -BIG))
            for _ in range(7):
                V.do(lambda e, tt=tt: e.max(m8, sc2[tt]))
                V.do(lambda e, tt=tt: e.match_replace(sc2[tt], m8, sc2[tt], -BIG))
            V.do(lambda e, tt=tt: e.tensor_tensor(sc2[tt], sc2[tt], sc[tt], ALU.is_equal))
        for n in range(2):
            go(run_t(aq, n, t_aq))
        t_bias = []
        for tt in range(2):
            hs = 4 >> tt
            for hq in range(8 // hs):
                b = bank()
                bs = bias[tt][:, hq * hs:hq * hs + hs, :]
                t = T.do(mm(b.ap[:, :], flip, bs, True, True), t_rev, t_ga, b.free)
                b.free = A.do(lambda e, b=b, bs=bs, hs=hs: e.activation(bs, r3(b.ap[:, :], hs), ACT.Copy), t)
        t_bias = b.free
        leave()
        av = r3(ar(2048), 2)
        for n in range(2):
            go(run_t(ak, n, t_aq))
        for tt in range(2):
            n = 128 * (tt + 1)
            qs = slice(tt * 128, tt * 128 + 128)
            L3 = r3(Ls[tt], 8)
            for hp in range(4):
                b = bank()
                for j in range(2):
                    h = 2 * hp + j
                    f = mm(b.ap[:, j * 256:j * 256 + n], aq[:, h, qs], ak[:, h, 0:n], True, True)
                    if j:
                        t = T.do(f)
                    else:
                        T.plain(f, b.free, t_aq)
                Lh = L3[:, 2 * hp:2 * hp + 2, :]
                b.free = V.do(lambda e, b=b, Lh=Lh, tt=tt, hp=hp, n=n: e.scalar_tensor_tensor(
                    out=Lh, in0=r3(b.ap[:, :], 2)[:, :, 0:n], scalar=ATT_SCALE,
                    in1=bias[tt][:, 2 * hp:2 * hp + 2, :], op0=ALU.mult, op1=ALU.add), t, t_bias)
            V.do(lambda e, L3=L3, n=n, tt=tt: e.scalar_tensor_tensor(
                out=L3, in0=free_dims(sc2[tt], [0, 8], [1, n]), scalar=-1e30, in1=L3, op0=ALU.mult, op1=ALU.add))
            V.do(lambda e, L3=L3, tt=tt: e.tensor_reduce(mx[:, 24 * tt:24 * tt + 8], L3, AX.X, ALU.max))
            t_L = V.do(lambda e, L3=L3, n=n, tt=tt: e.tensor_tensor(
                L3, L3, free_dims(mx[:, 24 * tt:24 * tt + 8], [1, 8], [0, n]), ALU.subtract))
        t_lg = T.last()
        t_sm = {}
        t_sg, make_a = gates(sp, sg, None, ht)
        for tt in range(2):
            go(run_n(av, tt, t_av))
            n = 128 * (tt + 1)
            L, L3, o = Ls[tt], r3(Ls[tt], 8), 24 * tt
            k = A.do(lambda e, L=L: e.activation(L, L, ACT.Exp), t_L)
            V.do(lambda e, L3=L3, o=o: e.tensor_reduce(mx[:, o + 8:o + 16], L3, AX.X, ALU.add), k)
            V.do(lambda e, o=o: e.reciprocal(mx[:, o + 16:o + 24], mx[:, o + 8:o + 16]))
            t_sm[tt] = V.do(lambda e, L3=L3, n=n, o=o: e.tensor_tensor(
                L3, L3, free_dims(mx[:, o + 16:o + 24], [1, 8], [0, n]), ALU.mult))
        go(make_a)
        PT = [[r3(aq_f[:, 0:1024], 8), None], [r3(aq_f[:, 1024:2048], 8), r3(Ls[0], 8)]]
        oaT = r3(ak_f, 8)
        for tt in range(2):
            L3 = r3(Ls[tt], 8)
            t_pt = []
            for s in range(tt + 1):
                for hq in range(2):
                    b = bank()
                    for j in range(4):
                        f = (lambda e, b=b, j=j, hq=hq, s=s, L3=L3: e.transpose(
                            b.ap[:, j * 128:j * 128 + 128], L3[:, 4 * hq + j, s * 128:s * 128 + 128], ident))
                        if j == 3:
                            t = T.do(f)
                        else:
                            T.plain(f, b.free, t_sm[tt])
                    b.free = copy_out(hq, PT[tt][s][:, 4 * hq:4 * hq + 4, :], r3(b.ap[:, :], 4), t, t_lg)
                    t_pt.append(b.free)
            for hq in range(2):
                b = bank()
                for j in range(4):
                    h = 4 * hq + j
                    for s in range(tt + 1):
                        f = mm(b.ap[:, j * 128:j * 128 + 128], av[:, s, h * 128:h * 128 + 128], PT[tt][s][:, h, :],
                               s == 0, s == tt)
                        if j == 3 and s == tt:
                            t = T.do(f)
                        else:
                            T.plain(f, b.free, t_pt, t_av)
                b.free = copy_out(hq, oaT[:, 4 * hq:4 * hq + 4, tt * 128:tt * 128 + 128], r3(b.ap[:, :], 4), t, t_lg)
                t_oa.append(b.free)
        t_m = merge(raw["a"], oaT, 8, True, t_oa, t_sg)

        toks = barrier()
        leave()
        inner()
        bq, bk, bb, E, Gt = (ar(2048) for _ in range(5))
        bl = Gt
        bi, bg = r3(ar(2048), 2), r3(ar(2048), 2)
        acc = ar(2048)
        accx = E[:, 0:1024]
        masks = ar(8 * 128).bitcast(I32)
        lbt = ar(40)
        hg = ar(128)
        bls = ar(8)
        sst = ar(80)
        g_b = group("hgrn")
        A.dma(g_b, lambda e: e.dma_start(masks, a["masks"]), toks)
        A.dma(g_b, lambda e: e.dma_start(lbt[:, 0:8], a["hgrn_lb_raw_2"]))
        t_gb = A.dma(g_b, lambda e: e.dma_start(hg, a["hgrn_norm_g_2"][0, :].partition_broadcast(P)))
        t_bq, t_bf, t_bi, t_bg = [], [], [], []
        b3 = lambda ap: r3(ap, 8)
        go(run_t(b3(bk), 0, t_bf, ACT.Sigmoid))
        G.do(lambda e, E=E: e.memset(E, 1.0))
        t_rm = G.do(lambda e, E=E: e.memset(free_dims(E, [64, 32]), 0.0))
        t_az = G.do(lambda e, acc=acc: e.memset(acc, 0.0))
        V.do(lambda e: e.tensor_tensor(lbt[:, 8:16], lbt[:, 0:8], lbt[:, 0:8], ALU.subtract), t_gb)
        k = A.do(lambda e: e.activation(lbt[:, 16:24], lbt[:, 8:16], ACT.Exp), V.last())
        V.do(lambda e: e.reciprocal(lbt[:, 24:32], lbt[:, 16:24]), k)
        V.do(lambda e: e.tensor_tensor(lbt[:, 24:32], lbt[:, 24:32], lbt[:, 16:24], ALU.mult))
        V.do(lambda e: e.tensor_tensor(lbt[:, 24:32], lbt[:, 24:32], lbt[:, 24:32], ALU.subtract))
        V.do(lambda e: e.tensor_scalar(lbt[:, 32:40], lbt[:, 24:32], -1.0, 1.0, ALU.mult, ALU.add))
        go(run_t(b3(bk), 1, t_bf, ACT.Sigmoid))
        lb_b = free_dims(lbt[:, 24:32], [1, 8], [0, 256])
        om_b = free_dims(lbt[:, 32:40], [1, 8], [0, 256])
        V.do(lambda e, bk=bk: e.tensor_tensor(b3(bk), b3(bk), om_b, ALU.mult), t_bf)
        V.do(lambda e, bk=bk: e.tensor_tensor(b3(bk), b3(bk), lb_b, ALU.add))
        t_f = V.do(lambda e, bl=bl, bk=bk: e.tensor_scalar(bl, bk, 2.0 ** -63, None, ALU.max))
        V.do(lambda e, bk=bk: e.tensor_scalar(bk, bk, -1.0, 1.0, ALU.mult, ALU.add))
        go(run_t(b3(bq), 0, t_bq))
        k = A.do(lambda e, bl=bl: e.activation(bl, bl, ACT.Ln), t_f)
        t_b = V.do(lambda e, bb=bb, E=E, bl=bl: e.tensor_tensor_scan(bb, E, bl, 0.0, ALU.mult, ALU.add), k, t_rm)
        go(run_t(b3(bq), 1, t_bq))
        G3, acc3 = b3(Gt), r3(acc, 16)

        t_sg, make_b = gates(sp, sg, t_m, ht)

        def filling():
            for n in range(2):
                yield from run_n(bi, n, t_bi)
            for n in range(2):
                yield from run_silu([bg[:, tt, n * 512:n * 512 + 512] for tt in range(2)], t_bg, None,
                                    free_dims(hg, [0, 4], [1, 128]))
            yield from make_b
        filler = filling()

        def fill(n):
            for _ in range(n):
                next(filler, None)

        def pair_views(t, l):
            even = free_dims(t[:, 0:1], [2 * l, 1024 // l], [1, l])
            odd = free_dims(t[:, l:l + 1], [2 * l, 1024 // l], [1, l])
            return even, odd

        def products(m, lhs, rhs, k):
            for q in range(4):
                b = bank()
                for j in range(4):
                    h, half = (4 * q + j) // 2, j % 2
                    sl = slice(half * 128, half * 128 + 128)
                    f = mm(b.ap[:, j * 128:j * 128 + 128], b3(lhs)[:, h, sl], b3(rhs)[:, h, sl], True, True)
                    if j == 3:
                        t = T.do(f)
                    else:
                        T.plain(f, b.free, k)
                b.free = V.do(lambda e, q=q, b=b, acc3=acc3, masks=masks: e.copy_predicated(
                    acc3[:, 4 * q:4 * q + 4, :], free_dims(masks[:, m * 128:m * 128 + 128], [0, 4], [1, 128]),
                    r3(b.ap[:, :], 4)), t, t_gb, t_az)
            return t, b.free

        t_mm, t_acc = products(7, bk, bq, [t_b, t_bq])
        for lv in range(7):
            l = 1 << lv
            Ee, Eo = pair_views(E, l)
            be, bo = pair_views(bb, l)
            ref = free_dims(bb[:, l - 1:l], [2 * l, 1024 // l], [0, l])
            V.do(lambda e, Ee=Ee, ref=ref, be=be: e.tensor_tensor(Ee, ref, be, ALU.subtract), A.last())
            if l < 64:
                t_e = V.do(lambda e, Eo=Eo, ref=ref, bo=bo: e.tensor_tensor(Eo, bo, ref, ALU.subtract))
            else:
                t_e = V.do(lambda e, Eo=Eo, bo=bo: e.tensor_copy(Eo, bo))
            fill(1)
            k = A.do(lambda e, E=E: e.activation(E, E, ACT.Exp), t_e)
            Ge, Go = pair_views(Gt, l)
            ke, _ = pair_views(bk, l)
            _, qo = pair_views(bq, l)
            V.do(lambda e, Ge=Ge, Ee=Ee, ke=ke: e.tensor_tensor(Ge, Ee, ke, ALU.mult), k, t_mm)
            k = V.do(lambda e, Go=Go, Eo=Eo, qo=qo: e.tensor_tensor(Go, Eo, qo, ALU.mult))
            fill(2)
            t_mm, t_acc = products(lv, Gt, Gt, k)
        B4 = bb.rearrange("p (h c t) -> p h c t", h=8, c=4)
        E4 = E.rearrange("p (h c t) -> p h c t", h=8, c=4)
        lastc = lambda c: bb[:, c * 64 + 63:c * 64 + 64]
        v8 = lambda ap: free_dims(ap, [256, 8], [0, 64])
        V.do(lambda e: e.tensor_tensor(bls[:, 0:8], free_dims(lastc(0), [256, 8]), free_dims(lastc(1), [256, 8]), ALU.add))
        V.do(lambda e: e.tensor_tensor(E4[:, :, 0, :], free_dims(bls[:, 0:8], [1, 8], [0, 64]), B4[:, :, 0, :], ALU.subtract), A.last())
        V.do(lambda e: e.tensor_tensor(E4[:, :, 1, :], v8(lastc(1)), B4[:, :, 1, :], ALU.subtract))
        V.do(lambda e: e.tensor_copy(E4[:, :, 2, :], B4[:, :, 2, :]))
        t_e = V.do(lambda e: e.tensor_tensor(E4[:, :, 3, :], v8(lastc(2)), B4[:, :, 3, :], ALU.add))
        fill(2)
        k = A.do(lambda e, E=E: e.activation(E, E, ACT.Exp), t_e)
        hv = lambda t, s: b3(t)[:, :, s * 128:s * 128 + 128]
        V.do(lambda e, E=E, Gt=Gt, bk=bk: e.tensor_tensor(hv(Gt, 0), hv(E, 0), hv(bk, 0), ALU.mult), k, t_mm)
        k = V.do(lambda e, E=E, Gt=Gt, bq=bq: e.tensor_tensor(hv(Gt, 1), hv(E, 1), hv(bq, 1), ALU.mult))
        accx3 = b3(accx)
        t_ax = []
        for q in range(2):
            b = bank()
            for j in range(4):
                h = 4 * q + j
                f = mm(b.ap[:, j * 128:j * 128 + 128], G3[:, h, 0:128], G3[:, h, 128:256], True, True)
                if j == 3:
                    t = T.do(f)
                else:
                    T.plain(f, b.free, k)
            b.free = copy_out(q, accx3[:, 4 * q:4 * q + 4, :], r3(b.ap[:, :], 4), t, k)
            t_ax.append(b.free)
        oN = r3(bq, 2)
        sqj = bk
        t_fin = [T.last(), V.last()]
        t_on = []
        for tt in range(2):
            for q in range(2):
                b = bank()
                for j in range(4):
                    h = 4 * q + j
                    o = b.ap[:, j * 128:j * 128 + 128]
                    v = slice(h * 128, h * 128 + 128)
                    if tt:
                        T.plain(mm(o, accx3[:, h, :], bi[:, 0, v], True, False), b.free, t_ax, t_bi)
                    f = mm(o, acc3[:, 2 * h + tt, :], bi[:, tt, v], tt == 0, True)
                    if j == 3:
                        t = T.do(f, t_acc)
                    else:
                        T.plain(f, b.free, t_acc, t_bi)
                b.free = copy_out(q, oN[:, tt, q * 512:q * 512 + 512], b.ap[:, :], t, t_fin)
                t_on.append(b.free)
        V.do(lambda e, sqj=sqj, bq=bq: e.tensor_tensor(sqj, bq, bq, ALU.mult), t_on)
        h_ss, h_ms, h_sq, h_r, h_t = (sst[:, 16 * i:16 * i + 16] for i in range(5))
        V.do(lambda e, sqj=sqj: e.tensor_reduce(h_ss, r3(sqj, 16), AX.X, ALU.add))
        t_e = V.do(lambda e: e.tensor_scalar(h_ms, h_ss, 1.0 / 128, 1e-6, ALU.mult, ALU.add))
        for _ in filler:
            pass
        k = A.do(lambda e: e.activation(h_sq, h_ms, ACT.Sqrt), t_e)
        inv_sqrt(h_r, h_sq, h_ms, h_t, k)
        V.do(lambda e, bq=bq: e.tensor_tensor(r3(bq, 16), r3(bq, 16), free_dims(h_r, [1, 16], [0, 128]), ALU.mult))
        k = V.do(lambda e, oN=oN, bg=bg: e.tensor_tensor(oN, oN, bg, ALU.mult), t_bg)
        obT = b3(bb)
        t_ob = transposes(oN, obT, 8, k)
        t_m = merge(raw["b"], obT, 8, False, t_ob, t_sg)

        toks = barrier()
        leave()
        inner()
        cq, ck_ = ar(2048), ar(2048)
        ocT = r3(ar(16 * 256), 16)
        rt1, rt2 = ar(1024), ar(1024)
        at0, at1 = r3(ar(1024), 4), r3(ar(512), 4)
        cv = [r3(ar(1024), 2) for _ in range(2)]
        cg = [r3(ar(1024), 2) for _ in range(2)]
        oc = [r3(rt1, 2), r3(rt2, 2)]
        tab = ar(1536)
        cst_ = ar(40)
        sjunk = rel
        g_t = group("ret")
        t_gt = A.dma(g_t, lambda e: e.dma_start(tab, a["cst"][:, C_COS:C_COS + 1536]), toks)
        cosb = free_dims(tab[:, 0:256], [0, 4], [1, 256])
        sinb = free_dims(tab[:, 256:512], [0, 4], [1, 256])
        dec = tab[:, 512:1536]
        t_rot = []
        u0, u1 = r3(rt1, 4), r3(rt2, 4)
        for src in (cq, ck_):
            tk = []
            for n in range(2):
                go(run_t(b3(src), n, tk))
            ev = src.rearrange("p (h e t) -> p h e t", h=4, e=2)
            s0, s1 = ev[:, :, 0, :], ev[:, :, 1, :]
            V.do(lambda e, s0=s0: e.tensor_tensor(u0, s0, cosb, ALU.mult), tk, t_gt)
            V.do(lambda e, s0=s0: e.tensor_tensor(u1, s0, sinb, ALU.mult))
            V.do(lambda e, s0=s0, s1=s1: e.tensor_tensor(s0, s1, sinb, ALU.mult))
            V.do(lambda e, s0=s0: e.tensor_tensor(s0, u0, s0, ALU.subtract))
            V.do(lambda e, s1=s1: e.tensor_tensor(s1, s1, cosb, ALU.mult))
            t_rot.append(V.do(lambda e, s1=s1: e.tensor_tensor(s1, s1, u1, ALU.add)))
        rq3, rk3 = b3(cq), b3(ck_)
        t_at = []
        oc_free, cv_free, cg_free = [None, None], [None, None], [None, None]
        t_oc = []
        turned = None
        t_cv, t_cg = {}, {}

        def values(h):
            i = h % 2
            t_cv[h], t_cg[h] = [], []

            def evac_v(tt, ps, t):
                k = A.do(lambda e, o=cv[i][:, tt, :]: e.activation(o, ps, ACT.Copy), t, cv_free[i])
                t_cv[h].append(k)
                return k
            go(proj_n(sp, hT, evac_v))
            go(run_silu([cg[i][:, tt, :] for tt in range(2)], t_cg[h], cg_free[i]))

        values(0)
        for h in range(4):
            b = bank()
            for e2 in range(2):
                T.plain(mm(b.ap[:, 0:256], rk3[:, 2 * h + e2, 0:128], rq3[:, 2 * h + e2, :], e2 == 0, e2 == 1),
                        b.free, t_rot)
            for e2 in range(2):
                f = mm(b.ap[:, 256:384], rk3[:, 2 * h + e2, 128:256], rq3[:, 2 * h + e2, 128:256], e2 == 0, e2 == 1)
                if e2:
                    t = T.do(f)
                else:
                    T.plain(f)
            V.do(lambda e, h=h, b=b: e.tensor_tensor(at0[:, h, :], b.ap[:, 0:256], dec[:, h * 256:h * 256 + 256], ALU.mult), t)
            b.free = V.do(lambda e, h=h, b=b: e.tensor_tensor(at1[:, h, :], b.ap[:, 256:384],
                                                              dec[:, h * 256:h * 256 + 128], ALU.mult))
            t_at.append(b.free)
        for h in range(4):
            i = h % 2
            if h < 3:
                values(h + 1)
            bs = []
            for tt in range(2):
                b = bank()
                if tt == 0:
                    t = T.do(mm(b.ap[:, :], at0[:, h, 0:128], cv[i][:, 0, :], True, True), b.free, t_cv[h], t_at)
                else:
                    T.plain(mm(b.ap[:, :], at0[:, h, 128:256], cv[i][:, 0, :], True, False), b.free)
                    t = T.do(mm(b.ap[:, :], at1[:, h, :], cv[i][:, 1, :], False, True))
                k = A.do(lambda e, b=b, tt=tt: e.activation(sjunk, b.ap[:, :], ACT.Square,
                                                            accum_out=cst_[:, tt:tt + 1]), t, V.last())
                bs.append(b)
            cv_free[i] = t
            ms, sq, r_, t_ = (cst_[:, 8 * q:8 * q + 2] for q in range(1, 5))
            k = V.do(lambda e, ms=ms: e.tensor_scalar(ms, cst_[:, 0:2], 1.0 / 512, 1e-6, ALU.mult, ALU.add), k)
            k = A.do(lambda e, ms=ms, sq=sq: e.activation(sq, ms, ACT.Sqrt), k)
            inv_sqrt(r_, sq, ms, t_, k)
            for tt in range(2):
                bs[tt].free = k = V.do(lambda e, tt=tt, i=i, b=bs[tt], r_=r_: e.scalar_tensor_tensor(
                    out=oc[i][:, tt, :], in0=b.ap[:, :], scalar=r_[:, tt:tt + 1], in1=cg[i][:, tt, :],
                    op0=ALU.mult, op1=ALU.mult), oc_free[i], t_cg[h])
            cg_free[i] = k
            t_oc += transposes(oc[i], ocT[:, 4 * h:4 * h + 4, :], 4, k)
            oc_free[i] = T.last()
        t_sg, make_c = gates(sp, sg, t_m, ht)
        go(make_c)
        t_m = merge(raw["c"], ocT, 16, False, t_oc, t_sg)

        hN = r3(hold, 2)
        for tt in range(2):
            for n in range(2):
                b = bank()
                c, w = raw["o"][n], r3(raw["o"][n].ap, 8)
                for k in range(8):
                    f = mm(b.ap, mT[:, k, tt * 128:tt * 128 + 128], w[:, k, :], k == 0, k == 7)
                    if k == 7:
                        c.done = t = T.do(f)
                    else:
                        T.plain(f, c.tok, b.free, t_m)
                xs = x[:, tt, n * 512:n * 512 + 512]
                b.free = V.do(lambda e, b=b, n=n: e.tensor_tensor(
                    rel, b.ap, grow[0][:, n * 512:n * 512 + 512], ALU.mult), t, t_gt1)
                V.do(lambda e, xs=xs: e.tensor_tensor(xs, xs, rel, ALU.add))
            rmsnorm(x, grow[1][:, :], hN, rt1, 1024, V.last(), tiles=(tt,))
            t_hn = V.do(lambda e, tt=tt: e.tensor_tensor(hN[:, tt, :], hN[:, tt, :], grow[2][:, :], ALU.add), t_sh)
        t_g2 = row_load(A, g_r[0], 0, mod_d[5, :], V.last())
        leave()

        toks = barrier()
        leave()
        inner()
        hT = r3(ar(2048), 8)
        junk = ar(1024)
        rw = ar(8 * 36)
        rbb = ar(36)
        lg = ar(72)
        sc4 = ar(96)
        s8 = ar(200)
        cm = ar(384)
        pos = ar(16)
        cnt = ar(16)
        many = ar(1).bitcast(I32)
        sel = ar(1024)
        selT = ar(1024)
        xg = (r3(ar(4096, F32R), 8), r3(ar(4096, F32R), 8))
        gsel = ar(32)
        sgb = [ar(512) for _ in range(2)]
        hge = [ar(512) for _ in range(2)]
        hgT = [(r3(ar(512, F32R), 4), r3(ar(512, F32R), 4)) for _ in range(2)]
        bufs = split_bufs()
        yg = [ar(1024) for _ in range(2)]
        ytmp = ar(512)
        ctx.callback(leave)
        ctx.callback(leave)
        g_o = group("moe")
        A.dma(g_o, lambda e: e.dma_start(rw, a["rw"]), toks)
        A.dma(g_o, lambda e: e.dma_start(cm, a["cst"][:, C_MOE:C_MOE + 384]))
        t_go = A.dma(g_o, lambda e: e.dma_start(rbb, a["rb"][0, :].partition_broadcast(P)))
        ht = transposes(hN, hT, 8, t_hn)

        def weights(T, A, chunk, engines, at_first):
            sp = Splitter(T, A, chunk, bufs)
            for src, ex in ([("eg", 0), ("eu", 0)] + [(src, ex + (src != "ed")) for ex in range(32)
                                                      for src in ("eg", "eu", "ed") if ex + (src != "ed") < 32]):
                sp.expect(a[src][ex], engines if sp.parts else at_first, "rows")
            sp.ahead(PARTS)
            return sp

        sp = weights(T, A, chunk, [V], [G])
        b = bank()
        rw3 = r3(rw, 8)
        for tt in range(2):
            for k in range(8):
                f = mm(b.ap[:, tt * 36:tt * 36 + 36], hT[:, k, tt * 128:tt * 128 + 128], rw3[:, k, :], k == 0, k == 7)
                if tt and k == 7:
                    t = T.do(f)
                else:
                    T.plain(f, b.free, ht, t_go)
        lg3 = r3(lg, 2)
        b.free = V.do(lambda e, b=b: e.tensor_tensor(lg3, r3(b.ap[:, 0:72], 2), free_dims(rbb, [0, 2], [1, 36]), ALU.add), t, t_go)
        gl = lg3[:, :, 0:4]
        vv = lambda o, n: free_dims(sc4[:, o:o + 1], [n, 2], [1, n])
        vb = lambda o, n: free_dims(sc4[:, o:o + 1], [1, 2], [0, n])
        gsum, gp = sc4[:, 2:4], sc4[:, 4:6]
        eqg, ohg = vv(8, 4), vv(16, 4)

        def first_one(dst, src, mx_o, n, tmp_o):
            rank = free_dims(iota[:, 0:1], [0, 2], [1, n])
            return [lambda fn=fn: V.do(fn) for fn in (
                lambda e: e.tensor_reduce(sc4[:, mx_o:mx_o + 2], src, AX.X, ALU.max),
                lambda e: e.tensor_tensor(dst, src, vb(mx_o, n), ALU.is_equal),
                lambda e: e.scalar_tensor_tensor(out=dst, in0=rank, scalar=-16.0, in1=dst, op0=ALU.add, op1=ALU.mult),
                lambda e: e.tensor_reduce(sc4[:, tmp_o:tmp_o + 2], dst, AX.X, ALU.min),
                lambda e: e.tensor_tensor(dst, dst, vb(tmp_o, n), ALU.is_equal))]

        for step in first_one(ohg, gl, 0, 4, 24):
            t_oh = step()
        b = bank()
        tri, ones = cm[:, 128:256], cm[:, 256:384]
        T.plain(mm(b.ap[:, 0:4], tri, sc4[:, 16:20], True, True), b.free, t_oh, t_go)
        T.plain(mm(b.ap[:, 4:8], ones, sc4[:, 16:20], True, False))
        T.plain(mm(b.ap[:, 4:8], tri, sc4[:, 20:24], False, True))
        T.plain(mm(b.ap[:, 8:12], ones, sc4[:, 16:20], True, False))
        t = T.do(mm(b.ap[:, 8:12], ones, sc4[:, 20:24], False, True))
        V.do(lambda e, b=b: e.tensor_scalar(pos[:, 0:8], b.ap[:, 0:8], 1.0, None, ALU.add), t)
        V.do(lambda e: e.tensor_tensor(pos[:, 0:8], pos[:, 0:8], sc4[:, 16:24], ALU.mult))
        V.do(lambda e: e.tensor_scalar(pos[:, 0:8], pos[:, 0:8], -1.0, None, ALU.add))
        b.free = V.do(lambda e, b=b: e.tensor_reduce(cnt[:, 0:1], b.ap[:, 8:12], AX.X, ALU.max))
        t_many = V.do(lambda e: e.tensor_copy(many, cnt[:, 0:1]))
        def gating():
            steps = []

            def v(fn):
                steps.append(lambda: V.do(fn))

            def expo(d):
                def f():
                    k = A.do(lambda e: e.activation(d, d, ACT.Exp), V.last())
                    V.wait(k)
                steps.append(f)

            v(lambda e: e.tensor_tensor(eqg, gl, vb(0, 4), ALU.subtract))
            expo(sc4[:, 8:16])
            v(lambda e: e.tensor_reduce(gsum, eqg, AX.X, ALU.add))
            v(lambda e: e.reciprocal(gp, gsum))
            el = free_dims(lg[:, 4:5], [36, 2], [1, 8], [8, 4])
            prod = s8[:, 0:64]
            v(lambda e: e.tensor_tensor(free_dims(prod, [32, 2], [4, 8], [1, 4]), el,
                                           free_dims(sc4[:, 16:17], [4, 2], [0, 8], [1, 4]), ALU.mult))
            ing = r3(s8[:, 64:80], 2)
            v(lambda e: e.tensor_reduce(s8[:, 64:80], free_dims(prod, [4, 16], [1, 4]), AX.X, ALU.add))
            oh1, oh2, in2 = r3(s8[:, 80:96], 2), r3(s8[:, 96:112], 2), r3(s8[:, 112:128], 2)
            steps += first_one(oh1, ing, 26, 8, 28)
            v(lambda e: e.scalar_tensor_tensor(out=in2, in0=oh1, scalar=-BIG, in1=ing, op0=ALU.mult, op1=ALU.add))
            steps += first_one(oh2, in2, 30, 8, 32)
            gex, den, w1 = sc4[:, 34:36], sc4[:, 36:38], sc4[:, 38:40]
            v(lambda e: e.tensor_tensor(gex, sc4[:, 30:32], sc4[:, 26:28], ALU.subtract))
            expo(gex)
            v(lambda e: e.tensor_scalar(den, gex, 1.0, None, ALU.add))
            v(lambda e: e.reciprocal(w1, den))
            v(lambda e: e.tensor_tensor(w1, w1, gp, ALU.mult))
            v(lambda e: e.tensor_tensor(gex, gex, w1, ALU.mult))
            v(lambda e: e.tensor_tensor(oh1, oh1, vb(38, 8), ALU.mult))
            v(lambda e: e.tensor_tensor(oh2, oh2, vb(34, 8), ALU.mult))
            v(lambda e: e.tensor_tensor(oh1, oh1, oh2, ALU.add))
            return steps

        y = [[banks[4], banks[5]], [banks[6], banks[7]]]
        usable[:] = [0, 1, 2, 3]

        t_gate = []
        gate_steps = gating()

        def experts(T, V, A, sp, first):
            done = {}
            for g in range(4):
                for tt in range(2):
                    t_sel = V.do(lambda e, g=g, tt=tt: e.tensor_scalar(
                        sel[:, tt * 512 + g * 128:tt * 512 + g * 128 + 128], cm[:, 0:128], float(first),
                        pos[:, 4 * tt + g:4 * tt + g + 1], ALU.add, ALU.is_equal), t_go, T.last())
            if CAP < 128:
                t_sel = V.do(lambda e: e.memset(sel.rearrange("p (a b) -> p a b", b=128)[:, :, CAP:128], 0.0))
            t_xg = []
            for k in range(8):
                b = bank()
                T.plain(mm(b.ap[:, :], hN[:, 0, k * 128:k * 128 + 128], sel[:, 0:512], True, False), b.free, t_sel, t_hn)
                t = T.do(mm(b.ap[:, :], hN[:, 1, k * 128:k * 128 + 128], sel[:, 512:1024], False, True))
                q = A.do(lambda e, k=k, b=b: e.activation(xg[0][:, k, :], b.ap, ACT.Copy), t)
                b.free = V.do(lambda e, k=k, b=b: e.tensor_tensor(xg[1][:, k, :], b.ap, xg[0][:, k, :].bitcast(F32),
                                                                  ALU.subtract), q)
                t_xg.append(b.free)
                for step in gate_steps[:7]:
                    step()
                del gate_steps[:7]
            if not t_gate:
                for step in gate_steps:
                    step()
                t_gate.append(V.last())
            def places():
                b = bank()
                for g in range(4):
                    for tt in range(2):
                        f = mm(b.ap[:, g * 8:g * 8 + 8], sel[:, tt * 512 + g * 128:tt * 512 + g * 128 + 128],
                               s8[:, 80 + 8 * tt:88 + 8 * tt], tt == 0, tt == 1)
                        if g == 3 and tt:
                            t = T.do(f)
                        else:
                            T.plain(f, b.free, t_gate)
                b.free = done["gs"] = V.do(lambda e, b=b: e.tensor_copy(gsel, b.ap[:, 0:32]), t)
                for q in range(2):
                    b = bank()
                    for j in range(4):
                        g, tt = 2 * q + j // 2, j % 2
                        f = (lambda e, b=b, j=j, g=g, tt=tt: e.transpose(
                            b.ap[:, j * 128:j * 128 + 128], sel[:, tt * 512 + g * 128:tt * 512 + g * 128 + 128], ident))
                        if j == 3:
                            t = T.do(f)
                        else:
                            T.plain(f, b.free)
                    b.free = done["st"] = V.do(lambda e, q=q, b=b: e.tensor_copy(selT[:, q * 512:q * 512 + 512], b.ap[:, :]), t)

            def up(ex, between):
                g = ex // 8
                hb, sb_ = hge[ex % 2], sgb[ex % 2]
                got = []
                rows = slice(g * 128, g * 128 + 128)
                for part in range(2):
                    if part:
                        (bg_, tg), = got
                        bg_.free = k_s = A.do(lambda e: e.activation(sb_, bg_.ap, ACT.Silu), tg, done.get(("h", ex - 2)))
                        between()
                    b = bank()
                    for q in range(4):
                        p = sp.take()
                        for kk in range(2):
                            k, w = 2 * q + kk, slice(kk * 512, kk * 512 + 512)
                            T.plain(mm(b.ap, xg[0][:, k, rows], p.hi[:, w], k == 0, False), p.tok, b.free, t_xg)
                            T.plain(mm(b.ap, xg[1][:, k, rows], p.hi[:, w], False, False))
                            f = mm(b.ap, xg[0][:, k, rows], p.lo[:, w], False, k == 7)
                            if kk:
                                t = T.do(f)
                            else:
                                T.plain(f)
                        sp.give(p, t)
                    got.append((b, t))
                bu_, tu = got[1]
                bu_.free = done["h", ex] = V.do(lambda e: e.scalar_tensor_tensor(
                    out=hb, in0=sb_, scalar=gsel[:, ex:ex + 1], in1=bu_.ap[:, :], op0=ALU.mult, op1=ALU.mult),
                    k_s, tu, done["gs"], done.get(("t", ex - 2)))

            def turned(ex):
                b = bank()
                for j in range(4):
                    f = (lambda e, b=b, j=j: e.transpose(b.ap[:, j * 128:j * 128 + 128],
                                                         hge[ex % 2][:, j * 128:j * 128 + 128], ident))
                    if j == 3:
                        done["t", ex] = T.do(f)
                    else:
                        T.plain(f, b.free, done["h", ex])
                hh, hl = hgT[ex % 2]
                k = A.do(lambda e, b=b: e.activation(hh, r3(b.ap, 4), ACT.Copy), done["t", ex], done.get(("d", ex - 2)))
                b.free = done["hT", ex] = V.do(lambda e, b=b: e.tensor_tensor(
                    hl, r3(b.ap, 4), hh.bitcast(F32), ALU.subtract), k, done.get(("d", ex - 2)))

            def down(ex):
                g = ex // 8
                hh, hl = hgT[ex % 2]
                t_h = done["hT", ex]
                for k in range(4):
                    p = sp.take()
                    for n in range(2):
                        yb = y[g % 2][n]
                        w = slice(n * 512, n * 512 + 512)
                        T.plain(mm(yb.ap, hh[:, k, :], p.hi[:, w], ex % 8 == 0 and k == 0, False),
                                p.tok, t_h, yb.free if ex % 8 == 0 else None)
                        T.plain(mm(yb.ap, hl[:, k, :], p.hi[:, w], False, False))
                        f = mm(yb.ap, hh[:, k, :], p.lo[:, w], False, ex % 8 == 7 and k == 3)
                        if n:
                            t = T.do(f)
                        else:
                            T.plain(f)
                    sp.give(p, t)
                done["d", ex] = t
                if ex % 8 == 7:
                    for n in range(2):
                        y[g % 2][n].free = done["y", g] = A.do(lambda e, n=n: e.activation(
                            yg[g % 2][:, n * 512:n * 512 + 512], y[g % 2][n].ap[:, :], ACT.Copy),
                            done["d", ex], done.get(("s", g - 2)))

            def back(g):
                for tt in range(2):
                    for n in range(2):
                        b = bank()
                        done["s", g] = t = T.do(mm(
                            b.ap[:, :], selT[:, g * 256 + tt * 128:g * 256 + tt * 128 + 128],
                            yg[g % 2][:, n * 512:n * 512 + 512], True, True), b.free, done["y", g], done["st"])
                        xs = x[:, tt, n * 512:n * 512 + 512]
                        b.free = V.do(lambda e, b=b, n=n: e.tensor_tensor(
                            ytmp, b.ap[:, :], grow[0][:, n * 512:n * 512 + 512], ALU.mult), t, t_g2)
                        V.do(lambda e, xs=xs: e.tensor_tensor(xs, xs, ytmp, ALU.add))

            up(0, places)
            for ex in range(32):
                if ex < 31:
                    up(ex + 1, lambda: turned(ex))
                else:
                    turned(ex)
                down(ex)
                if ex % 8 == 1 and ex > 8:
                    back(ex // 8 - 1)
            back(3)

        experts(T, V, A, sp, 0)
        rest = []
        for p in range(1, 256 // CAP):
            marks = [q.last() for q in (T, V, A, G)]
            T2, V2, A2 = (Queue(sem(f"s_{n}{p}"), n != "pe") for n in ("pe", "dve", "act"))
            for q in (T2, V2, A2):
                q.wait(*marks)
            sems2 = [sem(f"s_ring{i}_{p}") for i in range(RING)]
            more = []

            def chunk2(src, more=more, sems2=sems2):
                c = Chunk(len(more), src, 4096, sems2)
                more.append(c)
                c.ap = ring[c.slot][:, :]
                return c

            frees = [(b, b.free) for b in banks]
            for b in banks:
                b.free = None
            experts(T2, V2, A2, weights(T2, A2, chunk2, [V2], [V2]), p * CAP)
            for b, f in frees:
                b.free = f
            for q in (T2, V2, A2):
                q.wait(T2.last(), V2.last(), A2.last())
            rest.append((p, T2, V2, A2, more, marks))
            for q, q2 in ((T, T2), (V, V2), (A, A2)):
                q.ops.append((p, q2.ops))
        t_x = V.last()
        t_f = rmsnorm(x, grow[3][:, :], hN, junk, 1024, t_x, t_gf)
        g_out = group("out")
        t_out = A.dma(g_out, lambda e: e.dma_start(out.rearrange("b (t p) d -> p (b t) d", p=P), hN), t_f)
        A.wait(t_out)

        block = ctx.enter_context(nc.Block())

        def run(e, ops):
            for f in ops:
                if isinstance(f, tuple):
                    p, inner = f
                    e.wait_ge(*t_many)
                    with e.If(e.value_load(many[0:1, 0:1], min_val=0, max_val=256) > p * CAP):
                        run(e, inner)
                else:
                    f(e)

        def load(e, cs, before):
            for c in cs:
                if c.n >= RING:
                    done = cs[c.n - RING].done
                    for t in (done if isinstance(done, list) else [done]):
                        e.wait_ge(*t)
                elif before:
                    for t in before:
                        e.wait_ge(*t)
                e.dma_start(ring[c.slot][:, 0:c.cols], c.src).then_inc(c.tok[0], 16)

        @block.sync
        def _(e):
            load(e, chunks, [t_x0])
            for p, _, _, _, more, marks in rest:
                e.wait_ge(*t_many)
                with e.If(e.value_load(many[0:1, 0:1], min_val=0, max_val=256) > p * CAP):
                    load(e, more, marks)

        @block.tensor
        def _(e):
            run(e, T.ops)

        @block.vector
        def _(e):
            run(e, V.ops)

        @block.scalar
        def _(e):
            run(e, A.ops)

        @block.gpsimd
        def _(e):
            run(e, G.ops)


def constants():
    c = np.zeros((P, C_END), np.float32)
    c[:, C_ID:C_ID + 128] = np.eye(128)
    c[:, C_IOTA:C_IOTA + 16] = np.arange(16)
    pos = np.arange(256, dtype=np.float32)
    theta = (np.float32(1.0) / np.power(np.float32(10000.0), np.linspace(0.0, 1.0, 128, dtype=np.float32))).astype(np.float32)
    ang = (theta[:, None] * pos[None, :]).astype(np.float32).astype(np.float64)
    c[:, C_COS:C_COS + 256] = np.cos(ang)
    c[:, C_SIN:C_SIN + 256] = np.sin(ang)
    s, t = np.arange(128)[:, None], np.arange(256)[None, :]
    for h in range(4):
        g = np.log(1.0 - 2.0 ** (-5.0 - h))
        d = np.where(t >= s, np.exp((t - s) * g), 0.0) * (256.0 ** -0.5)
        c[:, C_DEC + h * 256:C_DEC + h * 256 + 256] = d
    for g, w in enumerate((2, 4, 8, 16)):
        c[:, C_INV + g * 256:C_INV + g * 256 + 256] = 1.0 / np.minimum(np.arange(256) + 1, w)
    rel = np.maximum(255 - np.arange(512), 0)
    relf = np.maximum(rel, 1).astype(np.float32)
    large = 16 + (np.log(relf / np.float32(16)) / np.float32(np.log(8.0)) * np.float32(16)).astype(np.int32)
    bucket = np.where(rel < 16, rel, np.minimum(large, 31))
    c[bucket, C_OH + np.arange(512)] = 1.0
    c[:, C_OH + 512:C_OH + 640] = np.eye(128)[::-1]
    c[:, C_MOE:C_MOE + 128] = np.arange(128)
    c[:, C_MOE + 128:C_MOE + 256] = np.triu(np.ones((128, 128)), 1)
    c[:, C_MOE + 256:C_MOE + 384] = 1.0
    m = np.zeros((P, 8, 128), np.int32)
    s, t = np.arange(128)[:, None], np.arange(128)[None, :]
    for lv in range(7):
        l = 1 << lv
        m[:, lv, :] = (s // (2 * l) == t // (2 * l)) & ((s // l) % 2 == 0) & ((t // l) % 2 == 1)
    m[:, 7, :] = s == t
    return c, m.reshape(P, 1024)


def kernel(**inputs):
    import concourse.bacc as bacc
    from concourse.bass_utils import run_bass_kernel_spmd

    i = {k: np.asarray(v) for k, v in inputs.items()}

    def cols(w, cw=512):
        k, n = w.shape
        return w.reshape(k // 128, 128, n // cw, cw).transpose(2, 1, 0, 3).reshape(n // cw, 128, -1)

    def rows(w):
        k, n = w.shape
        return w.reshape(k // 128, 128, n).transpose(1, 0, 2).reshape(128, -1)

    w2 = i["w_in_2"][0]
    offs = np.cumsum([0, 1024, 1024, 1024, 512, 64, 8] + [1024] * 4 + [1024, 1024, 2048, 2048] + [1024] * 3)
    aq, ak, av, iq, ik, iw, bq, bf, bi, bg, cq, ck, cv, cg, ga, gb, gc = (
        w2[:, offs[n]:offs[n + 1]] for n in range(17))
    pairs = lambda w: w.reshape(1024, 4, 128, 2).transpose(0, 1, 3, 2).reshape(1024, 1024)
    big = np.concatenate([aq, ak, iq, av, bq, bf, bi, bg, pairs(cq), pairs(ck), cv, cg, ga, gb, gc], axis=1)
    wc = i["w_branch_c_2"][0]
    cst, masks = constants()
    arrays = {
        "x": i["x"], "cst": cst, "masks": masks,
        "g_mix": i["g_mix"], "g_ffn": i["g_ffn"], "g_final": i["g_final"],
        "w_in": cols(i["w_in"][0]),
        "pgw": i["pool_group_w"][0].transpose(1, 0, 2).reshape(128, 512),
        "pcs": i["pool_scale"][0].reshape(4, 128).T,
        "cvw": i["conv_w"][0].reshape(3, 4, 128).transpose(2, 0, 1).reshape(128, 12),
        "wbp": rows(i["w_branch_pool"][0]), "wbc": rows(i["w_branch_conv"][0]),
        "w_out": cols(i["w_out"][0]), "w_q": cols(i["w_q"][0]),
        "skT": i["sub_keys"][0].transpose(3, 0, 1, 2).reshape(128, 2048),
        "expert_uv": np.concatenate([i["expert_u"][0], i["expert_v"][0]], axis=1),
        "c_2": i["c_2"].reshape(8, 128).T, "ada_w_2": cols(i["ada_w_2"][0]), "ada_b_2": i["ada_b_2"],
        "norm1_g_2": i["norm1_g_2"], "norm2_g_2": i["norm2_g_2"], "final_norm_g_2": i["final_norm_g_2"],
        "w_in_2": cols(big), "w_small": rows(np.concatenate([ik, ik, iw], axis=1)),
        "rel_bias_2": i["rel_bias_2"],
        "hgrn_lb_raw_2": i["hgrn_lb_raw_2"].reshape(8, 128).T, "hgrn_norm_g_2": i["hgrn_norm_g_2"],
        "w_branch_a_2": cols(i["w_branch_a_2"][0]), "w_branch_b_2": cols(i["w_branch_b_2"][0]),
        "w_branch_c_2": np.concatenate([cols(wc[0:1024]), cols(wc[1024:2048])], axis=1).reshape(4, 128, 4096),
        "w_out_2": cols(i["w_out_2"][0]),
        "rw": rows(np.concatenate([i["router_group_w_2"][0], i["router_expert_w_2"][0]], axis=1)),
        "rb": np.concatenate([i["router_group_b_2"], i["router_expert_b_2"]], axis=1),
        "eg": i["expert_w_gate_2"][0].reshape(32, 8, 128, 512).transpose(0, 2, 1, 3).reshape(32, 128, 4096),
        "eu": i["expert_w_up_2"][0].reshape(32, 8, 128, 512).transpose(0, 2, 1, 3).reshape(32, 128, 4096),
        "ed": i["expert_w_down_2"][0].reshape(32, 4, 128, 1024).transpose(0, 2, 1, 3).reshape(32, 128, 4096),
    }
    nc = bacc.Bacc("TRN2", target_bir_lowering=False, num_devices=1)
    feed, aps = {}, {}
    for name, v in arrays.items():
        feed["in_" + name] = np.ascontiguousarray(v)
        aps[name] = nc.dram_tensor("in_" + name, v.shape, mybir.dt.from_np(v.dtype), kind="ExternalInput").ap()
    out = nc.dram_tensor("out_0", (1, 256, 1024), F32, kind="ExternalOutput").ap()
    build(nc, aps, out)
    r = run_bass_kernel_spmd(nc, [feed], core_ids=[0])
    return r.results[0]["out_0"]
```

```python
from contextlib import ExitStack

import numpy as np
import concourse.bass as bass
from concourse import mybir

F32 = mybir.dt.float32
F32R = mybir.dt.float32r
U32 = mybir.dt.uint32
I32 = mybir.dt.int32
ALU = mybir.AluOpType
ACT = mybir.ActivationFunctionType
AX = mybir.AxisListType

P = 128
RING = 6
HALF = 2048
PARTS = 4
NGB = 9
CAP = 128
BIG = 3.0e38
IDX_SCALE = float(512) ** -0.5
ATT_SCALE = float(128) ** -0.5

C_ID, C_IOTA = 0, 128
C_COS, C_SIN, C_DEC, C_INV, C_OH = 144, 400, 656, 1680, 2704
C_MOE = 2704 + 640
C_END = C_MOE + 384


class Queue:

    def __init__(self, sem, linked):
        self.sem, self.linked = sem, linked
        self.count, self.ops, self.met = 0, [], {}

    def wait(self, *tokens):
        for t in tokens:
            if not t:
                continue
            if isinstance(t, list):
                self.wait(*t)
                continue
            sem, value = t
            if self.met.get(sem.name, 0) < value:
                self.met[sem.name] = value
                self.ops.append(lambda e, s=sem, v=value: e.wait_ge(s, v))

    def last(self):
        return (self.sem, self.count) if self.count else None

    def do(self, fn, *tokens):
        if self.linked:
            self.wait(self.last())
        self.wait(*tokens)
        self.count += 1
        self.ops.append(lambda e: fn(e).then_inc(self.sem, 1))
        return (self.sem, self.count)

    def plain(self, fn, *tokens):
        self.wait(*tokens)
        self.ops.append(fn)

    def dma(self, group, fn, *tokens):
        self.wait(*tokens)
        group.count += 16
        self.ops.append(lambda e: fn(e).then_inc(group.sem, 16))
        return (group.sem, group.count)


class Group:

    def __init__(self, sem):
        self.sem, self.count = sem, 0


class Chunk:

    def __init__(self, n, src, sems):
        self.n, self.src, self.slot = n, src, n % RING
        self.tok = (sems[n % RING], 16 * (n // RING + 1))
        self.done = None


class Bank:
    def __init__(self, ap):
        self.ap, self.free = ap, None


class Part:

    def __init__(self, chunk, view, eng):
        self.chunk, self.view, self.eng = chunk, view, eng


class Splitter:

    def __init__(self, T, A, chunk, bufs):
        self.T, self.A, self.chunk, self.bufs = T, A, chunk, bufs
        self.free = [None] * len(bufs)
        self.parts, self.taken, self.made = [], 0, 0

    def expect(self, srcs, engines, cut):
        for src in srcs:
            c = self.chunk(src)
            c.done = []
            for q in range(2):
                if cut == "cols":
                    v = c.ap.rearrange("p (k n) -> p k n", k=8)[:, :, q * 128:q * 128 + 128]
                elif cut == "wide":
                    v = c.ap.rearrange("p (k n) -> p k n", k=4)[:, :, q * 256:q * 256 + 256]
                else:
                    v = c.ap[:, q * 1024:q * 1024 + 1024]
                self.parts.append(Part(c, v, engines[len(self.parts) % len(engines)]))

    def ahead(self, n):
        while self.made < min(n, len(self.parts)):
            self.split(self.made)
            self.made += 1

    def take(self):
        n = self.taken
        self.taken += 1
        self.ahead(n + PARTS)
        return self.parts[n]

    def split(self, n):
        p, i = self.parts[n], n % PARTS
        hi, lo = self.bufs[i]
        if p.view.ndim == 3:
            hi, lo = (t.rearrange("p (k n) -> p k n", k=p.view.shape[1]) for t in (hi, lo))
        p.hi, p.lo = hi, lo
        a = self.A.do(lambda e: e.activation(hi, p.view, ACT.Copy), p.chunk.tok, self.free[i])
        p.tok = p.eng.do(lambda e: e.tensor_tensor(lo, p.view, hi.bitcast(F32), ALU.subtract), a, p.chunk.tok,
                         self.free[i])
        p.chunk.done += [a, p.tok]

    def give(self, p, token):
        self.free[self.parts.index(p) % PARTS] = token


def free_dims(ap, *dims):
    return bass.AP(tensor=ap.tensor, offset=ap.offset, ap=[list(ap.ap[0])] + [list(d) for d in dims])


def build(nc, a, out):
    ctx = ExitStack()
    with ctx:
        def sb(name, n, dt=F32):
            return ctx.enter_context(nc.sbuf_tensor(name, [P, n], dt))

        def sem(name):
            return ctx.enter_context(nc.semaphore(name))

        ring = [sb(f"ring{i}", HALF) for i in range(RING)]
        x_t = sb("x", 2048)
        grow = [sb(f"g{i}", 1024) for i in range(4)]
        cid = sb("cid", 144)
        st = sb("st", 64)
        banks = [Bank(ctx.enter_context(nc.psum_tensor(f"ps{i}", [P, 512], F32))[:, :]) for i in range(8)]
        mod_d = nc.dram_tensor("mod_scratch", [6, 1024], F32, kind="Internal").ap()
        rr_d = nc.dram_tensor("rr_scratch", [8, 512], F32, kind="Internal").ap()

        ring_sems = [sem(f"s_ring{i}") for i in range(RING)]
        V = Queue(sem("s_dve"), True)
        A = Queue(sem("s_act"), True)
        G = Queue(sem("s_pool"), True)
        T = Queue(sem("s_pe"), False)

        def group(name):
            return Group(sem("d_" + name))

        chunks = []

        def chunk(src):
            c = Chunk(len(chunks), src, ring_sems)
            chunks.append(c)
            c.ap = ring[c.slot][:, :]
            return c

        def halves(src):
            return [src[:, 0:HALF], src[:, HALF:2 * HALF]]

        def pair(src, n):
            return [src[2 * n], src[2 * n + 1]]

        usable = list(range(8))
        turn = [0]

        def bank():
            b = banks[usable[turn[0] % len(usable)]]
            turn[0] += 1
            return b

        scopes = [ExitStack()]
        names = [0]

        def ar(n, dt=F32):
            names[0] += 1
            return scopes[-1].enter_context(nc.sbuf_tensor(f"t{names[0]}", [P, n], dt))[:, :]

        def inner():
            scopes.append(ExitStack())

        def leave():
            scopes.pop().close()

        def barrier():
            toks = [q.last() for q in (T, A, V, G)]
            for q in (A, V, G):
                q.wait(*toks)
            return toks

        def split_bufs():
            return [(ar(1024, F32R), ar(1024, F32R)) for _ in range(PARTS)]

        def r3(ap, n):
            return ap.rearrange("p (a b) -> p a b", a=n)

        def mm(o, l, r, start, stop):
            return lambda e: e.matmul(o, l, r, start=start, stop=stop)

        x = r3(x_t[:, :], 2)
        ident = cid[:, C_ID:C_ID + 128]
        iota = cid[:, C_IOTA:C_IOTA + 16]

        g_c, g_x = group("const"), group("x")
        A.dma(g_x, lambda e: e.dma_start(x, a["x"].rearrange("b (t p) d -> p (b t) d", p=P)))
        A.dma(g_x, lambda e: e.dma_start(cid[:, :], a["cst"][:, 0:144]))
        def row_load(q, grp, i, src, *toks):
            return q.dma(grp, lambda e: e.dma_start(grow[i][:, :], src.partition_broadcast(P)), *toks)

        t_x0 = row_load(A, g_x, 0, a["g_mix"][0, :])
        inner()
        hold = ar(2048)
        inner()
        pgw = ar(512)
        invc = ar(1024)
        pcs = ar(4)
        cvw = ar(12)
        cs, csg, one = st[:, 16:24], st[:, 24:32], st[:, 32:33]
        adab = ar(512)
        g_s = group("small")
        A.dma(g_s, lambda e: e.dma_start(cs, a["c_2"]))
        t_sm0 = A.dma(g_s, lambda e: e.dma_start(adab[0:12, :], a["ada_b_2"].rearrange("o (n c) -> (o n) c", n=12)))

        def rmsnorm(src, g, dst, junk, cols, *toks, tiles=(0, 1)):
            first, end = tiles[0], tiles[-1] + 1
            ss, (ms, sq, r, t) = st[:, 0:2], (st[:, 2 * i + first:2 * i + end] for i in range(1, 5))
            for tt in tiles:
                s = A.do(lambda e, tt=tt: e.activation(junk, src[:, tt, :], ACT.Square,
                                                       accum_out=ss[:, tt:tt + 1]), *toks)
            m = V.do(lambda e: e.tensor_scalar(ms, ss[:, first:end], 1.0 / cols, 1e-6, ALU.mult, ALU.add), s)
            s = A.do(lambda e: e.activation(sq, ms, ACT.Sqrt), m)
            inv_sqrt(r, sq, ms, t, s)
            for tt in tiles:
                k = V.do(lambda e, tt=tt: e.scalar_tensor_tensor(
                    out=dst[:, tt, :], in0=src[:, tt, :], scalar=st[:, 6 + tt:7 + tt], in1=g,
                    op0=ALU.mult, op1=ALU.mult), *toks)
            return k

        def inv_sqrt(r, sq, ms, t, *toks):
            V.do(lambda e: e.reciprocal(r, sq), *toks)
            V.do(lambda e: e.tensor_tensor(t, r, r, ALU.mult))
            V.do(lambda e: e.tensor_tensor(t, t, ms, ALU.mult))
            V.do(lambda e: e.tensor_scalar(t, t, -0.5, 1.5, ALU.mult, ALU.add))
            return V.do(lambda e: e.tensor_tensor(r, r, t, ALU.mult))

        def copy_out(n, dst, src, *toks):
            if n % 2:
                return A.do(lambda e: e.activation(dst, src, ACT.Copy), *toks)
            return V.do(lambda e: e.tensor_copy(dst, src), *toks)

        def transposes(src, dst, nk, *toks):
            got = []
            for kp in range(nk // 2):
                b = bank()
                for kk in range(2):
                    for tt in range(2):
                        o = b.ap[:, kk * 256 + tt * 128:kk * 256 + tt * 128 + 128]
                        i = src[:, tt, (2 * kp + kk) * 128:(2 * kp + kk + 1) * 128]
                        f = (lambda e, o=o, i=i: e.transpose(o, i, ident))
                        if kk and tt:
                            t = T.do(f, *toks)
                        else:
                            T.plain(f, b.free, *toks)
                k = copy_out(kp, dst[:, 2 * kp:2 * kp + 2, :], r3(b.ap[:, :], 2), t)
                b.free = k
                got.append(k)
            return got[-2:]

        def transposes_split(src, hi, lo, nk, *toks):
            got = []
            for kp in range(nk // 2):
                b = bank()
                for kk in range(2):
                    for tt in range(2):
                        o = b.ap[:, kk * 256 + tt * 128:kk * 256 + tt * 128 + 128]
                        i = src[:, tt, (2 * kp + kk) * 128:(2 * kp + kk + 1) * 128]
                        f = (lambda e, o=o, i=i: e.transpose(o, i, ident))
                        if kk and tt:
                            t = T.do(f, *toks)
                        else:
                            T.plain(f, b.free, *toks)
                h, l, ps = hi[:, 2 * kp:2 * kp + 2, :], lo[:, 2 * kp:2 * kp + 2, :], r3(b.ap, 2)
                k = A.do(lambda e, h=h, ps=ps: e.activation(h, ps, ACT.Copy), t)
                b.free = V.do(lambda e, h=h, l=l, ps=ps: e.tensor_tensor(l, ps, h.bitcast(F32), ALU.subtract), k)
                got.append(b.free)
            return got[-1]

        def proj_t(sp, rhs, evac, *toks):
            xh, xl = rhs
            for half in range(2):
                b = bank()
                for j in range(2):
                    p = sp.take()
                    o = b.ap[:, j * 256:j * 256 + 256]
                    for k in range(8):
                        T.plain(mm(o, p.lo[:, k, :], xh[:, k, :], k == 0, False), p.tok, b.free, *toks)
                    for k in range(8):
                        T.plain(mm(o, p.hi[:, k, :], xl[:, k, :], False, False))
                    for k in range(8):
                        f = mm(o, p.hi[:, k, :], xh[:, k, :], False, k == 7)
                        if k == 7:
                            t = T.do(f)
                        else:
                            T.plain(f)
                    sp.give(p, t)
                    if j == 1:
                        b.free = evac(half, b.ap, t)
                    yield

        def proj_n(sp, lhs, evac, *toks):
            xh, xl = lhs
            bs = [bank(), bank()]
            for q in range(4):
                p = sp.take()
                ts = []
                for tt in range(2):
                    rows = slice(tt * 128, tt * 128 + 128)
                    for kk in range(2):
                        k, w = 2 * q + kk, slice(kk * 512, kk * 512 + 512)
                        T.plain(mm(bs[tt].ap, xh[:, k, rows], p.hi[:, w], k == 0, False), p.tok, bs[tt].free, *toks)
                        T.plain(mm(bs[tt].ap, xl[:, k, rows], p.hi[:, w], False, False))
                        f = mm(bs[tt].ap, xh[:, k, rows], p.lo[:, w], False, k == 7)
                        if kk == 1:
                            ts.append(T.do(f))
                        else:
                            T.plain(f)
                sp.give(p, ts[1])
                if q == 3:
                    for tt in range(2):
                        bs[tt].free = evac(tt, bs[tt].ap, ts[tt])
                yield

        def go(gen, beside=lambda: None):
            for _ in gen:
                beside()

        hT = (r3(ar(2048, F32R), 8), r3(ar(2048, F32R), 8))
        hN_f = ar(2048)
        hN = r3(hN_f, 2)
        pf_f = ar(1024)
        pp = [r3(ar(n * 272), n) for n in (4, 4, 3, 2, 1)]
        cu = r3(ar(4 * 258), 4)
        zb, zv = (r3(ar(1024), 4) for _ in range(2))
        abT = tuple(r3(ar(1024, F32R), 4) for _ in range(2))
        pf, cy = r3(pf_f, 4), zv
        mT = r3(ar(2048), 8)
        tmp = r3(ar(512), 2)
        sp = Splitter(T, A, chunk, split_bufs())
        msum = [ar(512) for _ in range(2)]
        modr = [ar(512) for _ in range(2)]
        c_ada = []

        def ada_chunks(n):
            return [chunk(src) for src in halves(a["ada_w_2"][n])]

        c_ada = []
        for n in range(6):
            sp.expect(pair(a["w_in"], n), [G] if n in (0, 4) else [G, V], "cols")
            c_ada.append(ada_chunks(n))
        sp.expect(pair(a["wbp"], 0), [G, V], "wide")
        for n in range(6, 8):
            sp.expect(pair(a["w_in"], n), [G, V], "cols")
            c_ada.append(ada_chunks(n))
        sp.expect(pair(a["wbc"], 0), [G, V], "wide")
        c_wo = [[chunk(src) for src in halves(a["w_out"][n])] for n in range(2)]
        t_ones = G.do(lambda e: e.memset(one, 1.0))
        z1 = G.do(lambda e: e.memset(pp[0][:, :, 0:16], 0.0))
        z2 = G.do(lambda e: e.memset(cu[:, :, 0:2], 0.0))
        k = rmsnorm(x, grow[0][:, :], hN, pf_f, 1024, t_x0)
        sp.ahead(2)
        ht = transposes_split(hN, hT[0], hT[1], 8, k)
        A.dma(g_c, lambda e: e.dma_start(pgw, a["pgw"]))
        A.dma(g_c, lambda e: e.dma_start(invc, a["cst"][:, C_INV:C_INV + 1024]))
        A.dma(g_c, lambda e: e.dma_start(pcs, a["pcs"]))
        A.dma(g_c, lambda e: e.dma_start(cvw, a["cvw"]))
        row_load(A, g_c, 1, a["g_ffn"][0, :])
        c_tok = row_load(A, g_c, 2, a["g_final"])
        k = A.do(lambda e: e.activation(csg, cs, ACT.Sigmoid), t_sm0)
        t_cs = V.do(lambda e: e.tensor_tensor(csg, csg, cs, ALU.mult), k)
        g_md = [group(f"mod{i}") for i in range(2)]
        t_om = [None, None]

        def modulation(first, c_ada, msum, modr, adab, *toks):
            t_am = [None, None]
            ended = []

            def summed(n, i):
                b = bank()
                T.plain(mm(b.ap[0:1, :], one, msum[i], True, False), c_ada[n - first][1].done, b.free, t_ones)
                t_am[i] = T.do(mm(b.ap[0:1, :], ident[0:12, n:n + 1], adab[0:12, :], False, True), *toks)
                return b

            def stored(n, i, b):
                b.free = A.do(lambda e: e.activation(modr[i][0:1, :], b.ap[0:1, :], ACT.Copy), t_am[i], t_om[i])
                t_om[i] = A.dma(g_md[i], lambda e: e.dma_start(
                    mod_d[n // 2:n // 2 + 1, n % 2 * 512:n % 2 * 512 + 512], modr[i][0:1, :]), b.free)

            for n, cs_ in enumerate(c_ada, first):
                i = n % 2
                for k in range(8):
                    c = cs_[k // 4]
                    w = r3(c.ap, 4)[:, k % 4, :]
                    if k == 0:
                        V.do(lambda e, i=i, w=w: e.tensor_scalar(msum[i], w, csg[:, 0:1], None, ALU.mult),
                             c.tok, t_cs, t_am[i], *toks)
                    else:
                        c.done = V.do(lambda e, i=i, w=w, k=k: e.scalar_tensor_tensor(
                            out=msum[i], in0=w, scalar=csg[:, k:k + 1], in1=msum[i], op0=ALU.mult, op1=ALU.add), c.tok)
                    if n > first and k == 3:
                        ended.append(summed(n - 1, 1 - i))
                    if n > first and k == 6:
                        stored(n - 1, 1 - i, ended.pop())
                    yield
            yield
            yield
            b = summed(n, i)
            yield
            stored(n, i, b)

        ada = modulation(0, c_ada, msum, modr, adab, t_sm0)

        def pour(n=2):
            for _ in range(n):
                next(ada, None)

        pre = {}
        for name, dst, off in (("p", pp[0], 16), ("c", cu, 2), ("b", zb, 0), ("v", zv, 0)):
            def evac(half, ps, t, dst=dst, off=off, name=name):
                k = copy_out(1, dst[:, 2 * half:2 * half + 2, off:off + 256], r3(ps, 2), t)
                pre.setdefault(name, []).append(k)
                return k
            go(proj_t(sp, hT, evac, ht), pour)

        for lv in range(4):
            d = 1 << lv
            lo = 2 * d - 1
            V.do(lambda e, lv=lv, d=d, lo=lo: e.tensor_tensor(
                pp[lv + 1][:, :, lo:272], pp[lv][:, lv > 0:, lo:272], pp[lv][:, lv > 0:, lo - d:272 - d], ALU.add),
                pre["p"], z1, c_tok)
            V.do(lambda e, lv=lv: e.tensor_tensor(pf[:, lv, :], pp[lv + 1][:, 0, 16:272],
                                                  invc[:, lv * 256:lv * 256 + 256], ALU.mult))
        t_pf = V.do(lambda e: e.tensor_tensor(pf, pf, pp[0][:, :, 16:272], ALU.subtract))
        V.do(lambda e: e.tensor_tensor(cu[:, :, 2:258], cu[:, :, 2:258], zv, ALU.mult), pre["c"], pre["v"], z2)
        for g in range(4):
            V.do(lambda e, g=g: e.tensor_scalar(cy[:, g, :], cu[:, g, 0:256], cvw[:, g:g + 1], None, ALU.mult))
            for k in (1, 2):
                V.do(lambda e, g=g, k=k: e.scalar_tensor_tensor(
                    out=cy[:, g, :], in0=cu[:, g, k:k + 256], scalar=cvw[:, 4 * k + g:4 * k + g + 1],
                    in1=cy[:, g, :], op0=ALU.mult, op1=ALU.add))
        t_b = V.do(lambda e: e.tensor_tensor(cy, cy, zb, ALU.mult), pre["b"])

        sg = r3(hN_f, 8)

        def gates(sp, dst, free, *toks):
            got = []

            def make():
                for n in range(2):
                    def evac(half, ps, t, n=n):
                        k = A.do(lambda e: e.activation(dst[:, 4 * n + 2 * half:4 * n + 2 * half + 2, :], r3(ps, 2),
                                                        ACT.Sigmoid), t, free)
                        got.append(k)
                        return k
                    yield from proj_t(sp, hT, evac, *toks)
            return got, make()

        def pooled():
            got = []
            for half in range(2):
                b = bank()
                for j in range(2):
                    g = 2 * half + j
                    f = mm(b.ap[:, j * 256:j * 256 + 256], pgw[:, g * 128:g * 128 + 128], pf[:, g, :], True, True)
                    if j:
                        t = T.do(f)
                    else:
                        T.plain(f, t_pf, b.free)
                views = [(2 * half + j, b.ap[:, j * 256:j * 256 + 256], pcs[:, 2 * half + j:2 * half + j + 1])
                         for j in range(2)]
                for g, ps, sc in views:
                    k = A.do(lambda e, g=g, ps=ps, sc=sc: e.activation(abT[0][:, g, :], ps, ACT.Copy, scale=sc), t)
                for g, ps, sc in views:
                    b.free = V.do(lambda e, g=g, ps=ps, sc=sc: e.scalar_tensor_tensor(
                        out=abT[1][:, g, :], in0=ps, scalar=sc, in1=abT[0][:, g, :].bitcast(F32),
                        op0=ALU.mult, op1=ALU.subtract), k)
                got.append(b.free)
            return got

        def conved(*toks):
            k = A.do(lambda e: e.activation(abT[0], cy, ACT.Copy), *toks)
            return [V.do(lambda e: e.tensor_tensor(abT[1], cy, abT[0].bitcast(F32), ALU.subtract), k)]

        def block_pair(p, outs, xs, first, last, *toks):
            xh, xl = xs
            terms = [(p.lo, xh), (p.hi, xl), (p.hi, xh)]
            for j in range(2):
                o, cs_ = outs[j], slice(j * 128, j * 128 + 128)
                for i, (w, y) in enumerate(terms):
                    for k in range(4):
                        f = mm(o, w[:, k, cs_], y[:, k, :], first and i == 0 and k == 0, last and i == 2 and k == 3)
                        if j == 1 and i == 2 and k == 3:
                            t = T.do(f)
                        else:
                            T.plain(f, p.tok, *toks)
            return t

        def gated(b, t, m0, sgs, tsg, first):
            m_, add = mT[:, m0:m0 + 2, :], tmp
            if first:
                b.free = k = V.do(lambda e: e.tensor_tensor(m_, sgs, r3(b.ap, 2), ALU.mult), t, tsg)
            else:
                b.free = V.do(lambda e: e.tensor_tensor(add, sgs, r3(b.ap, 2), ALU.mult), t, tsg)
                k = V.do(lambda e: e.tensor_tensor(m_, m_, add, ALU.add))
            return k

        t_m = None
        for br in range(2):
            t_sg, make = gates(sp, sg, t_m)
            if br:
                toks = conved(T.last(), t_b)
            for part, _ in enumerate(make):
                pour()
                if part == 4 and not br:
                    toks = pooled()
            for q in range(4):
                b, p = bank(), sp.take()
                t = block_pair(p, [b.ap[:, 0:256], b.ap[:, 256:512]], abT, True, True, toks, b.free)
                sp.give(p, t)
                t_m = gated(b, t, 2 * q, sg[:, 2 * q:2 * q + 2, :], t_sg[q], br == 0)
                if br:
                    pour(1)

        for tt in range(2):
            for n in range(2):
                b = bank()
                for k in range(8):
                    c = c_wo[n][k // 4]
                    f = mm(b.ap, mT[:, k, tt * 128:tt * 128 + 128], r3(c.ap, 4)[:, k % 4, :], k == 0, k == 7)
                    T.wait(c.tok, b.free, t_m)
                    if k % 4 == 3:
                        c.done = t = T.do(f)
                    else:
                        T.plain(f)
                xs = x[:, tt, n * 512:n * 512 + 512]
                b.free = V.do(lambda e, b=b, xs=xs: e.tensor_tensor(xs, xs, b.ap, ALU.add), t)
            t_h2 = rmsnorm(x, grow[1][:, :], r3(hold, 2), pf_f, 1024, V.last(), tiles=(tt,))
        pour(100)
        t_md = list(t_om)

        barrier()
        leave()
        inner()
        hN = r3(hold, 2)
        idx_u = ar(256).bitcast(U32)
        wts = ar(256)
        act = ar(256)
        S_f = ar(2 * 16 * 128)
        S = S_f.rearrange("p (t h k) -> p t h k", t=2, h=16)
        S2 = ar(256)
        tops = ar(512).rearrange("p (t h k) -> p t h k", t=2, h=16)
        topi = ar(512).bitcast(U32).rearrange("p (t h k) -> p t h k", t=2, h=16)
        topf = ar(512).rearrange("p (t h k) -> p t h k", t=2, h=16)
        cand = ar(2048)
        junk = cand[:, 0:1024]
        fs = ar(256)
        fp = ar(256).bitcast(U32)
        fa = ar(256).bitcast(U32)
        faf = ar(256)
        ab = [ar(256) for _ in range(2)]
        sm = ar(64)
        qT_f = ar(4096)
        qT = r3(qT_f, 16)
        inner()
        hT = (r3(ar(2048, F32R), 8), r3(ar(2048, F32R), 8))
        rb, ohb, rrs = ar(8), ar(512), ar(512)
        sp = Splitter(T, A, chunk, split_bufs())
        sk_f = ar(2048)
        for n in range(4):
            sp.expect(pair(a["w_q"], n), [G], "cols")
        c_ada = [ada_chunks(n) for n in range(8, 12)]
        g_rr, g_rb, g_sk = group("rr"), group("rb"), group("sk")
        t_sk = A.dma(g_sk, lambda e: e.dma_start(sk_f, a["skT"]))
        A.dma(g_rb, lambda e: e.dma_start(rb[0:32, :], a["rel_bias_2"]))
        t_rb = A.dma(g_rb, lambda e: e.dma_start(ohb, a["cst"][:, C_OH:C_OH + 512]))
        gbs = [group(f"gb{i}") for i in range(NGB)]
        ht = transposes_split(hN, hT[0], hT[1], 8, t_h2)

        def bc(ap2, off, *dims):
            return free_dims(ap2[:, off:off + 1], *dims)

        flat = lambda ap: ap.rearrange("p t h k -> p (t h k)")
        tops_f, topi_f, topf_f = flat(tops), flat(topi), flat(topf)
        t_idx = {}

        def picks(tt, q):
            o, first = tt * 256 + 64 * q, tt * 128 + 32 * q
            fr = slice(first, first + 32)
            cq = cand[:, 512 * q:512 * q + 512]
            grid = free_dims(cq, [256, 2], [16, 16], [1, 16])
            steps = []

            def v(fn, *toks):
                steps.append(lambda: V.do(fn, *toks))

            def top16(src, tmp, vals, idx, *toks):
                v(lambda e: e.max(vals[:, 0:8], src), *toks)
                v(lambda e: e.max_index(idx[:, 0:8], vals[:, 0:8], src))
                v(lambda e: e.match_replace(tmp, vals[:, 0:8], src, -BIG))
                v(lambda e: e.max(vals[:, 8:16], tmp))
                v(lambda e: e.max_index(idx[:, 8:16], vals[:, 8:16], tmp))

            for hp in range(4 * q, 4 * q + 4):
                top16(S[:, tt, hp, :], S2[:, 0:128], tops[:, tt, hp, :], topi[:, tt, hp, :], t_s[tt, q])
            v(lambda e: e.tensor_copy(topf_f[:, o:o + 64], topi_f[:, o:o + 64]))
            v(lambda e: e.tensor_tensor(grid, bc(tops_f, o, [32, 2], [1, 16], [0, 16]),
                                        bc(tops_f, o + 16, [32, 2], [0, 16], [1, 16]), ALU.add))
            for h in range(2):
                f0 = first + h * 16
                top16(cq[:, h * 256:h * 256 + 256], S2, fs[:, f0:f0 + 16], fp[:, f0:f0 + 16])
            for half in range(2):
                if half == 0:
                    v(lambda e: e.tensor_scalar(fa[:, fr], fp[:, fr], 4, None, ALU.logical_shift_right))
                else:
                    v(lambda e: e.tensor_scalar(fa[:, fr], fp[:, fr], 15, None, ALU.bitwise_and))
                v(lambda e: e.tensor_copy(faf[:, fr], fa[:, fr]))
                v(lambda e: e.tensor_tensor(grid, bc(faf, first, [16, 2], [1, 16], [0, 16]),
                                            bc(iota, 0, [0, 2], [0, 16], [1, 16]), ALU.is_equal), c_tok)
                v(lambda e, half=half: e.tensor_tensor(
                    grid, grid, bc(topf_f, o + 16 * half, [32, 2], [0, 16], [1, 16]), ALU.mult))
                v(lambda e, half=half: e.tensor_reduce(ab[half][:, fr], free_dims(cq, [16, 32], [1, 16]), AX.X, ALU.add))
            v(lambda e: e.scalar_tensor_tensor(out=ab[0][:, fr], in0=ab[0][:, fr], scalar=128.0, in1=ab[1][:, fr],
                                               op0=ALU.mult, op1=ALU.add))

            def index():
                t_idx[tt, q] = V.do(lambda e: e.tensor_copy(idx_u[:, fr], ab[0][:, fr]))
            steps.append(index)
            return steps

        def softmax(tt, q):
            first = tt * 128 + 32 * q
            fr = slice(first, first + 32)
            w3, f3 = r3(wts[:, fr], 2), r3(fs[:, fr], 2)
            tot, inv = (sm[:, 32 * tt + o + 2 * q:32 * tt + o + 2 * q + 2] for o in (0, 8))
            k = []
            return [
                lambda: V.do(lambda e: e.tensor_tensor(w3, f3, free_dims(fs[:, first:first + 1], [16, 2], [0, 16]),
                                                       ALU.subtract)),
                lambda: k.append(A.do(lambda e: e.activation(wts[:, fr], wts[:, fr], ACT.Exp), V.last())),
                lambda: V.do(lambda e: e.tensor_reduce(tot, w3, AX.X, ALU.add), k),
                lambda: V.do(lambda e: e.reciprocal(inv, tot)),
                lambda: V.do(lambda e: e.tensor_tensor(w3, w3, free_dims(inv, [1, 2], [0, 16]), ALU.mult))]

        t_q, t_s = {}, {}
        sk = r3(sk_f, 16)

        def scores(q):
            for tt in range(2):
                b = bank()
                for j in range(4):
                    hp = 4 * q + j
                    f = mm(b.ap[:, j * 128:j * 128 + 128], qT[:, hp, tt * 128:tt * 128 + 128], sk[:, hp, :], True, True)
                    if j == 3:
                        t = T.do(f)
                    else:
                        T.plain(f, t_sk, b.free, t_q[q])
                t_s[tt, q] = b.free = A.do(lambda e, tt=tt, b=b: e.activation(
                    S[:, tt, 4 * q:4 * q + 4, :], r3(b.ap, 4), ACT.Copy), t)

        now = []
        for n in range(4):
            t_q[n] = []

            def evac(half, ps, t, n=n):
                k = A.do(lambda e: e.activation(qT[:, 4 * n + 2 * half:4 * n + 2 * half + 2, :], r3(ps, 2), ACT.Copy), t)
                t_q[n].append(k)
                return k
            for part, _ in enumerate(proj_t(sp, hT, evac, ht)):
                if n and part == 0:
                    scores(n - 1)
                    if n < 3:
                        now += picks(0, n - 1)
                for step in now[:16]:
                    step()
                now = now[16:]
        scores(3)
        t_qT = T.last()
        b = bank()
        t = T.do(mm(b.ap[0:8, :], rb[0:32, :], ohb[0:32, :], True, True), t_rb, b.free)
        b.free = A.do(lambda e, b=b: e.activation(rrs[0:8, :], b.ap[0:8, :], ACT.Copy), t)
        t_rr = A.dma(g_rr, lambda e: e.dma_start(rr_d, rrs[0:8, :]), b.free)
        for step in softmax(0, 0) + softmax(0, 1):
            step()
        leave()
        gb = [qT_f[:, 0:2048], qT_f[:, 2048:4096]] + [ar(2048) for _ in range(NGB - 2)]
        diag = [ar(128) for _ in range(4)]
        biases = ar(512)
        msum, modr = ([ar(512) for _ in range(2)] for _ in range(2))
        g_ab = group("adab")
        t_ab = A.dma(g_ab, lambda e: e.dma_start(biases[0:12, :], a["ada_b_2"].rearrange("o (n c) -> (o n) c", n=12)),
                     t_qT, t_rr)
        ada = modulation(8, c_ada, msum, modr, biases, t_ab)
        g_r = [group(f"row{i}") for i in range(4)]
        k0 = row_load(A, g_r[0], 0, a["norm1_g_2"][0, :], t_h2)
        k1 = row_load(A, g_r[1], 1, mod_d[1, :], t_h2, t_md)
        t_sh = row_load(A, g_r[3], 3, mod_d[0, :], t_md)

        def scale_rows(s_row, g_row, *toks):
            return V.do(lambda e: e.scalar_tensor_tensor(
                out=grow[s_row][:, :], in0=grow[s_row][:, :], scalar=1.0, in1=grow[g_row][:, :],
                op0=ALU.add, op1=ALU.mult), *toks)

        scale_rows(1, 0, k0, k1)

        def finish(tt):
            xs, rows, c = x[:, tt, :], hN[:, tt, :], 34 + 12 * tt
            ss, ms, sq, r, t, rr = (st[:, c + 2 * q:c + 2 * q + 2] for q in range(6))
            k = V.do(lambda e: e.tensor_tensor(rows, xs, grow[2][:, :], ALU.mult))
            A.do(lambda e, junk=junk: e.activation(junk, xs, ACT.Square, accum_out=ss[:, 0:1]), V.last())
            k = A.do(lambda e, junk=junk: e.activation(junk, rows, ACT.Square, accum_out=ss[:, 1:2]), k)
            V.do(lambda e: e.tensor_scalar(ms, ss, 1.0 / 1024, None, ALU.mult), k)
            V.do(lambda e: e.tensor_scalar(ms[:, 0:1], ms[:, 0:1], 1e-6, None, ALU.add))
            V.do(lambda e: e.reciprocal(rr[:, 0:1], ms[:, 0:1]))
            V.do(lambda e: e.tensor_tensor(ms[:, 1:2], ms[:, 1:2], rr[:, 0:1], ALU.mult))
            k = V.do(lambda e: e.tensor_scalar(ms[:, 1:2], ms[:, 1:2], 1e-6, None, ALU.add))
            k = A.do(lambda e: e.activation(sq, ms, ACT.Sqrt), k)
            inv_sqrt(r, sq, ms, t, k)
            V.do(lambda e: e.tensor_tensor(rr[:, 1:2], r[:, 0:1], r[:, 1:2], ALU.mult))
            V.do(lambda e: e.scalar_tensor_tensor(out=rows, in0=rows, scalar=rr[:, 1:2], in1=grow[1][:, :],
                                                  op0=ALU.mult, op1=ALU.mult))
            done = V.do(lambda e: e.tensor_tensor(rows, rows, grow[3][:, :], ALU.add), t_sh)
            V.do(lambda e: e.scalar_tensor_tensor(out=xs, in0=xs, scalar=r[:, 0:1], in1=grow[2][:, :],
                                                  op0=ALU.mult, op1=ALU.mult))
            return done

        gfree = [[t_qT]] * 2 + [[t_qT, t_rr]] * (NGB - 2)
        ng = [0]
        got = {}

        def gather(col):
            s = ng[0] % NGB
            ng[0] += 1
            t = G.dma(gbs[s], lambda e: e.indirect_dma_start(
                out=gb[s], out_offset=None, in_=a["expert_uv"],
                in_offset=bass.IndirectOffsetOnAxis(ap=idx_u[:, col:col + 1], axis=0)), t_idx[col // 128, col % 128 // 32], gfree[s])
            got[col] = (s, t)

        def dots(c0):
            for col in range(c0, c0 + 2):
                gather(col)
                s, t = got[col]
                V.do(lambda e, s=s, col=col, hN=hN: e.tensor_tensor_reduce(
                    out=gb[s][:, 0:1024], in0=gb[s][:, 0:1024], in1=hN[:, col // 128, :], scale=1.0, scalar=0.0,
                    op0=ALU.mult, op1=ALU.add, accum_out=act[:, col:col + 1]), t)
            got["act", c0] = A.do(lambda e: e.activation(act[:, c0:c0 + 2], act[:, c0:c0 + 2], ACT.Gelu), V.last())

        t_sum = {}

        def add_picks(tt):
            for n in range(2):
                xs, b = x[:, tt, n * 512:n * 512 + 512], sums[tt][n]
                b.free = V.do(lambda e, b=b, xs=xs: e.tensor_tensor(xs, xs, b.ap, ALU.add), t_sum[tt])

        sums = [[bank(), bank()] for _ in range(2)]
        free = {bk: bk.free for bks in sums for bk in bks}
        usable[:] = [i for i in range(8) if banks[i] not in free]
        def work(*ps):
            return [step for tt, q in ps for step in picks(tt, q) + softmax(tt, q)]

        plan = [(0, 48, work((0, 2))), (48, 80, work((0, 3))), (80, 112, work((1, 0))), (112, 140, work((1, 1))),
                (140, 170, work((1, 2))), (170, 200, work((1, 3))), (200, 236, [pour] * 18)]
        t_dg = [t_rr] * 4
        dots(0)
        for c0 in range(0, 256, 2):
            for begin, end, steps in plan:
                if begin <= c0 < end:
                    each = -(-len(steps) // ((end - c0) // 2))
                    for step in steps[:each]:
                        step()
                    del steps[:each]
            if c0 + 2 < 256:
                dots(c0 + 2)
            k = V.do(lambda e, c0=c0: e.tensor_tensor(wts[:, c0:c0 + 2], wts[:, c0:c0 + 2], act[:, c0:c0 + 2], ALU.mult),
                     got["act", c0])
            for col in range(c0, c0 + 2):
                s, i, tt = got[col][0], col % 4, col // 128
                d = A.do(lambda e, i=i, col=col: e.activation(diag[i], ident, ACT.Copy, scale=wts[:, col:col + 1]),
                         k, t_dg[i])
                T.plain(mm(sums[tt][0].ap, diag[i], gb[s][:, 1024:1536], col % 128 == 0, col % 128 == 127),
                        d, [free[bk] for bk in sums[tt]])
                gfree[s] = t_dg[i] = T.do(mm(sums[tt][1].ap, diag[i], gb[s][:, 1536:2048], col % 128 == 0, col % 128 == 127))
            if c0 % 128 == 126:
                t_sum[c0 // 128] = T.last()
            if c0 in (134, 254):
                add_picks(c0 // 200)
                t_hold = finish(c0 // 200)
        usable[:] = range(8)
        t_md = list(t_om)

        w2 = a["w_in_2"]
        barrier()
        leave()
        inner()
        hT = (r3(ar(2048, F32R), 8), r3(ar(2048, F32R), 8))
        mT = r3(ar(2048), 8)
        sg = r3(hold, 8)
        rel = ar(512)
        tmp = r3(rel, 2)
        sp = Splitter(T, A, chunk, split_bufs())

        def run_t(dst, n, toks_out, fn=ACT.Copy):
            def evac(half, ps, t):
                d = dst[:, 4 * n + 2 * half:4 * n + 2 * half + 2, :]
                k = A.do(lambda e: e.activation(d, r3(ps, 2), fn), t)
                toks_out.append(k)
                return k
            return proj_t(sp, hT, evac, ht)

        def run_n(dst, n, toks_out):
            def evac(tt, ps, t):
                d = dst[:, tt, n * 512:n * 512 + 512]
                k = A.do(lambda e: e.activation(d, ps, ACT.Copy), t)
                toks_out.append(k)
                return k
            return proj_n(sp, hT, evac, ht)

        def run_silu(dst, toks_out, free):
            def evac(tt, ps, t):
                d = dst[tt]
                k = A.do(lambda e: e.activation(d, ps, ACT.Sigmoid), t, free)
                k = V.do(lambda e: e.tensor_tensor(d, d, ps, ALU.mult), k)
                toks_out.append(k)
                return k
            return proj_n(sp, hT, evac, ht)

        def wire(names):
            raw = {}
            for name in names:
                kind, src = name[0], name[1]
                if kind == "t":
                    sp.expect(src, name[2], "cols")
                elif kind == "n":
                    sp.expect(src, name[2], "rows")
                elif kind == "w":
                    sp.expect(src, name[2], "wide")
                else:
                    raw.setdefault(name[2], []).extend(chunk(v) for v in src)
            return raw

        GV, GG = [G, V], [G]
        wa, wb, wc = a["w_branch_a_2"], a["w_branch_b_2"], a["w_branch_c_2"]
        def t_(eng, *ns):
            return [("t", pair(w2, n), eng) for n in ns]

        def n_(eng, *ns):
            return [("n", pair(w2, n), eng) for n in ns]

        raw = wire(t_([V], 4) + t_(GG, 0, 1, 2, 3) + n_(GG, 5, 6) + t_(GG, 27) + t_(GV, 28)
                   + [("raw", [wa[n] for n in range(4)], "a")]
                   + t_(GV, 9, 10, 7, 8) + n_(GV, 11, 12) + n_(GG, 13, 14) + t_(GG, 29, 30)
                   + [("raw", [wb[n] for n in range(4)], "b")]
                   + t_(GV, 15, 16, 17, 18) + n_(GV, 19, 23, 20, 24, 21, 25, 22, 26) + t_(GV, 31, 32)
                   + [("w", pair(wc, n), GV) for n in range(4)]
                   + [("raw", halves(a["w_out_2"][n]), "o") for n in range(2)])

        def merge(cks, oT, first, toks, t_sg):
            for u, c in enumerate(cks):
                b, w = bank(), r3(c.ap, 8)
                for j in range(2):
                    for k in range(8):
                        f = mm(b.ap[:, j * 256:j * 256 + 256], w[:, k, j * 128:j * 128 + 128], oT[:, k, :], k == 0, k == 7)
                        if j == 1 and k == 7:
                            c.done = t = T.do(f)
                        else:
                            T.plain(f, c.tok, b.free, *toks)
                t = gated(b, t, 2 * u, sg[:, 2 * u:2 * u + 2, :], t_sg[u], first)
            return t

        inner()
        toks = [T.last(), A.last(), V.last(), G.last()]
        aq_f, ak_f = ar(2048), ar(2048)
        aq, ak = r3(aq_f, 8), r3(ak_f, 8)
        iq = r3(ar(1024), 4)
        ikE, ikO = ar(256), ar(256)
        iw = r3(ar(16), 2)
        bias = [r3(ar(8 * 128), 8), r3(ar(8 * 256), 8)]
        Ls = [ar(8 * 128), ar(8 * 256)]
        sc = [ar(128), ar(256)]
        sc2 = [ar(128), ar(256)]
        m8 = ar(8)
        mx = ar(48)
        inner()
        wsm = ar(8 * 136)
        wsh, wsl = ar(8 * 136, F32R), ar(8 * 136, F32R)
        flip = ar(128)
        g_a = group("att")
        A.dma(g_a, lambda e: e.dma_start(wsm, a["w_small"]), toks)
        t_ga = A.dma(g_a, lambda e: e.dma_start(flip, a["cst"][:, C_OH + 512:C_OH + 640]))
        ht = transposes_split(r3(hold, 2), hT[0], hT[1], 8, t_hold)
        z1 = G.do(lambda e: e.memset(ikE, 0.0))
        z2 = G.do(lambda e: e.memset(ikO, 0.0))
        g_rev = group("rev")
        t_aq, t_av, t_iq, t_oa = [], [], [], []
        go(run_t(iq, 0, t_iq))
        for tt in range(2):
            n = 128 * (tt + 1)
            for h in range(8):
                t_rev = A.dma(g_rev, lambda e, tt=tt, n=n, h=h: e.dma_start(
                    bias[tt][:, h, :], bass.AP(tensor=rr_d.tensor, offset=h * 512 + 128 - tt * 128,
                                               ap=[[1, 128], [1, n]])), t_rr)
        k = A.do(lambda e: e.activation(wsh, wsm, ACT.Copy), t_ga)
        t_ws = V.do(lambda e: e.tensor_tensor(wsl, wsm, wsh.bitcast(F32), ALU.subtract), k)
        go(run_t(aq, 0, t_aq))
        w3h, w3l = r3(wsh, 8), r3(wsl, 8)
        b = bank()
        for k in range(8):
            o = b.ap[:, 0:256]
            T.plain(mm(o, w3h[:, k, 0:128], hT[0][:, k, :], k == 0, False), t_ws, b.free)
            T.plain(mm(o, w3h[:, k, 0:128], hT[1][:, k, :], False, False))
            f = mm(o, w3l[:, k, 0:128], hT[0][:, k, :], False, k == 7)
            if k == 7:
                t = T.do(f)
            else:
                T.plain(f)
        A.do(lambda e, b=b: e.activation(ikE[0:64, :], b.ap[0:64, 0:256], ACT.Copy), t, z1)
        b.free = t_ik = A.do(lambda e, b=b: e.activation(ikO[64:128, :], b.ap[64:128, 0:256], ACT.Copy), t, z2)
        b = bank()
        iwT = sc2[1][0:8, :]
        for k in range(8):
            o = b.ap[0:8, 0:256]
            T.plain(mm(o, w3h[:, k, 128:136], hT[0][:, k, :], k == 0, False), b.free)
            T.plain(mm(o, w3h[:, k, 128:136], hT[1][:, k, :], False, False))
            f = mm(o, w3l[:, k, 128:136], hT[0][:, k, :], False, k == 7)
            if k == 7:
                t = T.do(f)
            else:
                T.plain(f)
        b.free = t = A.do(lambda e, b=b: e.activation(iwT, b.ap[0:8, 0:256], ACT.Copy, scale=IDX_SCALE), t)
        b = bank()
        T.plain(mm(b.ap[:, 0:8], iwT[:, 0:128], ident[0:8, 0:8], True, True), b.free, t)
        t = T.do(mm(b.ap[:, 8:16], iwT[:, 128:256], ident[0:8, 0:8], True, True))
        b.free = t_iw = V.do(lambda e, b=b: e.tensor_copy(iw, r3(b.ap[:, 0:16], 2)), t)

        for tt in range(2):
            n = 128 * (tt + 1)
            qs = slice(tt * 128, tt * 128 + 128)
            rl3 = r3(Ls[tt], 8)
            for hp in range(4):
                b = bank()
                for j in range(2):
                    f = mm(b.ap[:, j * 256:j * 256 + n], iq[:, hp, qs], (ikO if j else ikE)[:, 0:n], True, True)
                    if j:
                        t = T.do(f)
                    else:
                        T.plain(f, b.free, t_ik, t_iq)
                rl = rl3[:, 2 * hp:2 * hp + 2, :]
                b.free = k = A.do(lambda e, b=b, n=n, rl=rl: e.activation(rl, r3(b.ap[:, :], 2)[:, :, 0:n], ACT.Relu), t)
                for j in range(2):
                    h = 2 * hp + j
                    if h == 0:
                        V.do(lambda e, rl=rl, tt=tt, h=h: e.tensor_scalar(
                            sc[tt], rl[:, 0, :], iw[:, tt, h:h + 1], None, ALU.mult), k, t_iw)
                    else:
                        V.do(lambda e, rl=rl, tt=tt, h=h, j=j: e.scalar_tensor_tensor(
                            out=sc[tt], in0=rl[:, j, :], scalar=iw[:, tt, h:h + 1], in1=sc[tt],
                            op0=ALU.mult, op1=ALU.add), k)
            t_af = G.do(lambda e, tt=tt, n=n: e.affine_select(
                out=sc[tt], in_=sc[tt], pattern=[[-1, n]], compare_op=ALU.is_ge, fill=-BIG,
                base=tt * 128, channel_multiplier=1), V.last())
            V.do(lambda e, tt=tt: e.max(m8, sc[tt]), t_af)
            V.do(lambda e, tt=tt: e.match_replace(sc2[tt], m8, sc[tt], -BIG))
            for _ in range(7):
                V.do(lambda e, tt=tt: e.max(m8, sc2[tt]))
                V.do(lambda e, tt=tt: e.match_replace(sc2[tt], m8, sc2[tt], -BIG))
            V.do(lambda e, tt=tt: e.tensor_tensor(sc2[tt], sc2[tt], sc[tt], ALU.is_equal))
        t_gt1 = row_load(A, g_r[0], 0, mod_d[2, :], t_hold, t_md)
        k1 = row_load(A, g_r[1], 1, mod_d[4, :], t_hold, t_md)
        t_sh = row_load(A, g_r[2], 2, mod_d[3, :], t_hold, t_md)
        k3 = row_load(A, g_r[3], 3, a["norm2_g_2"][0, :], t_hold)
        go(run_t(aq, 1, t_aq))
        t_rows = scale_rows(1, 3, k1, k3)
        t_gf = row_load(A, g_r[3], 3, a["final_norm_g_2"], t_rows)
        t_bias = []
        for tt in range(2):
            hs = 4 >> tt
            for hq in range(8 // hs):
                b = bank()
                bs = bias[tt][:, hq * hs:hq * hs + hs, :]
                t = T.do(mm(b.ap[:, :], flip, bs, True, True), t_rev, t_ga, b.free)
                b.free = A.do(lambda e, b=b, bs=bs, hs=hs: e.activation(bs, r3(b.ap[:, :], hs), ACT.Copy), t)
        t_bias = b.free
        leave()
        av = r3(ar(2048), 2)
        for n in range(2):
            go(run_t(ak, n, t_aq))
        for tt in range(2):
            n = 128 * (tt + 1)
            qs = slice(tt * 128, tt * 128 + 128)
            L3 = r3(Ls[tt], 8)
            for hp in range(4):
                b = bank()
                for j in range(2):
                    h = 2 * hp + j
                    f = mm(b.ap[:, j * 256:j * 256 + n], aq[:, h, qs], ak[:, h, 0:n], True, True)
                    if j:
                        t = T.do(f)
                    else:
                        T.plain(f, b.free, t_aq)
                Lh = L3[:, 2 * hp:2 * hp + 2, :]
                b.free = V.do(lambda e, b=b, Lh=Lh, tt=tt, hp=hp, n=n: e.scalar_tensor_tensor(
                    out=Lh, in0=r3(b.ap[:, :], 2)[:, :, 0:n], scalar=ATT_SCALE,
                    in1=bias[tt][:, 2 * hp:2 * hp + 2, :], op0=ALU.mult, op1=ALU.add), t, t_bias)
            V.do(lambda e, L3=L3, n=n, tt=tt: e.scalar_tensor_tensor(
                out=L3, in0=free_dims(sc2[tt], [0, 8], [1, n]), scalar=-1e30, in1=L3, op0=ALU.mult, op1=ALU.add))
            V.do(lambda e, L3=L3, tt=tt: e.tensor_reduce(mx[:, 24 * tt:24 * tt + 8], L3, AX.X, ALU.max))
            t_L = V.do(lambda e, L3=L3, n=n, tt=tt: e.tensor_tensor(
                L3, L3, free_dims(mx[:, 24 * tt:24 * tt + 8], [1, 8], [0, n]), ALU.subtract))
        t_lg = T.last()
        t_sm = {}
        t_sg, make_a = gates(sp, sg, None, ht)
        for tt in range(2):
            go(run_n(av, tt, t_av))
            n = 128 * (tt + 1)
            L, L3, o = Ls[tt], r3(Ls[tt], 8), 24 * tt
            k = A.do(lambda e, L=L: e.activation(L, L, ACT.Exp), t_L)
            V.do(lambda e, L3=L3, o=o: e.tensor_reduce(mx[:, o + 8:o + 16], L3, AX.X, ALU.add), k)
            V.do(lambda e, o=o: e.reciprocal(mx[:, o + 16:o + 24], mx[:, o + 8:o + 16]))
            t_sm[tt] = V.do(lambda e, L3=L3, n=n, o=o: e.tensor_tensor(
                L3, L3, free_dims(mx[:, o + 16:o + 24], [1, 8], [0, n]), ALU.mult))
        go(make_a)
        PT = [[r3(aq_f[:, 0:1024], 8), None], [r3(aq_f[:, 1024:2048], 8), r3(Ls[0], 8)]]
        oaT = r3(ak_f, 8)
        for tt in range(2):
            L3 = r3(Ls[tt], 8)
            t_pt = []
            for s in range(tt + 1):
                for hq in range(2):
                    b = bank()
                    for j in range(4):
                        f = (lambda e, b=b, j=j, hq=hq, s=s, L3=L3: e.transpose(
                            b.ap[:, j * 128:j * 128 + 128], L3[:, 4 * hq + j, s * 128:s * 128 + 128], ident))
                        if j == 3:
                            t = T.do(f)
                        else:
                            T.plain(f, b.free, t_sm[tt])
                    b.free = copy_out(hq, PT[tt][s][:, 4 * hq:4 * hq + 4, :], r3(b.ap[:, :], 4), t, t_lg)
                    t_pt.append(b.free)
            for hq in range(2):
                b = bank()
                for j in range(4):
                    h = 4 * hq + j
                    for s in range(tt + 1):
                        f = mm(b.ap[:, j * 128:j * 128 + 128], av[:, s, h * 128:h * 128 + 128], PT[tt][s][:, h, :],
                               s == 0, s == tt)
                        if j == 3 and s == tt:
                            t = T.do(f)
                        else:
                            T.plain(f, b.free, t_pt, t_av)
                b.free = copy_out(hq, oaT[:, 4 * hq:4 * hq + 4, tt * 128:tt * 128 + 128], r3(b.ap[:, :], 4), t, t_lg)
                t_oa.append(b.free)
        t_m = merge(raw["a"], oaT, True, t_oa, t_sg)

        toks = barrier()
        leave()
        inner()
        bq, bk, bb, E, Gt = (ar(2048) for _ in range(5))
        bl = Gt
        bi, bg = r3(ar(2048), 2), r3(ar(2048), 2)
        acc = ar(2048)
        accx = E[:, 0:1024]
        masks = ar(8 * 128).bitcast(I32)
        lbt = ar(40)
        hg = ar(128)
        bls = ar(8)
        sst = ar(80)
        g_b = group("hgrn")
        A.dma(g_b, lambda e: e.dma_start(masks, a["masks"]), toks)
        A.dma(g_b, lambda e: e.dma_start(lbt[:, 0:8], a["hgrn_lb_raw_2"]))
        t_gb = A.dma(g_b, lambda e: e.dma_start(hg, a["hgrn_norm_g_2"][0, :].partition_broadcast(P)))
        t_bq, t_bf, t_bi, t_bg = [], [], [], []
        b3 = lambda ap: r3(ap, 8)
        go(run_t(b3(bk), 0, t_bf, ACT.Sigmoid))
        G.do(lambda e, E=E: e.memset(E, 1.0))
        t_rm = G.do(lambda e, E=E: e.memset(free_dims(E, [64, 32]), 0.0))
        t_az = G.do(lambda e, acc=acc: e.memset(acc, 0.0))
        V.do(lambda e: e.tensor_tensor(lbt[:, 8:16], lbt[:, 0:8], lbt[:, 0:8], ALU.subtract), t_gb)
        k = A.do(lambda e: e.activation(lbt[:, 16:24], lbt[:, 8:16], ACT.Exp), V.last())
        V.do(lambda e: e.reciprocal(lbt[:, 24:32], lbt[:, 16:24]), k)
        V.do(lambda e: e.tensor_tensor(lbt[:, 24:32], lbt[:, 24:32], lbt[:, 16:24], ALU.mult))
        V.do(lambda e: e.tensor_tensor(lbt[:, 24:32], lbt[:, 24:32], lbt[:, 24:32], ALU.subtract))
        V.do(lambda e: e.tensor_scalar(lbt[:, 32:40], lbt[:, 24:32], -1.0, 1.0, ALU.mult, ALU.add))
        go(run_t(b3(bk), 1, t_bf, ACT.Sigmoid))
        lb_b = free_dims(lbt[:, 24:32], [1, 8], [0, 256])
        om_b = free_dims(lbt[:, 32:40], [1, 8], [0, 256])
        V.do(lambda e, bk=bk: e.tensor_tensor(b3(bk), b3(bk), om_b, ALU.mult), t_bf)
        V.do(lambda e, bk=bk: e.tensor_tensor(b3(bk), b3(bk), lb_b, ALU.add))
        t_f = V.do(lambda e, bl=bl, bk=bk: e.tensor_scalar(bl, bk, 2.0 ** -63, None, ALU.max))
        V.do(lambda e, bk=bk: e.tensor_scalar(bk, bk, -1.0, 1.0, ALU.mult, ALU.add))
        go(run_t(b3(bq), 0, t_bq))
        k = A.do(lambda e, bl=bl: e.activation(bl, bl, ACT.Ln), t_f)
        t_ln = k
        t_b = V.do(lambda e, bb=bb, E=E, bl=bl: e.tensor_tensor_scan(bb, E, bl, 0.0, ALU.mult, ALU.add), k, t_rm)
        go(run_t(b3(bq), 1, t_bq))
        G3, acc3 = b3(Gt), r3(acc, 16)

        t_sg, make_b = gates(sp, sg, t_m, ht)

        def filling():
            for n in range(2):
                yield from run_n(bi, n, t_bi)
            for n in range(2):
                yield from run_n(bg, n, t_bg)
            yield from make_b
        filler = filling()

        def fill(n):
            for _ in range(n):
                next(filler, None)

        def pair_views(t, l, hf):
            even = free_dims(t[:, hf * 1024:hf * 1024 + 1], [2 * l, 512 // l], [1, l])
            odd = free_dims(t[:, hf * 1024 + l:hf * 1024 + l + 1], [2 * l, 512 // l], [1, l])
            return even, odd

        def products(hf, lhs, rhs, *toks):
            bs = []
            for q in range(2 * hf, 2 * hf + 2):
                b = bank()
                for j in range(4):
                    h, half = (4 * q + j) // 2, j % 2
                    sl = slice(half * 128, half * 128 + 128)
                    f = mm(b.ap[:, j * 128:j * 128 + 128], b3(lhs)[:, h, sl], b3(rhs)[:, h, sl], True, True)
                    if j == 3:
                        bs.append((q, b, T.do(f)))
                    else:
                        T.plain(f, b.free, *toks)
            return bs

        def kept(m, bs):
            for q, b, t in bs:
                b.free = V.do(lambda e, q=q, b=b, acc3=acc3, masks=masks: e.copy_predicated(
                    acc3[:, 4 * q:4 * q + 4, :], free_dims(masks[:, m * 128:m * 128 + 128], [0, 4], [1, 128]),
                    r3(b.ap, 4)), t, t_gb, t_az)
            return b.free

        def decays(lv, hf, E=E, bb=bb):
            l = 1 << lv
            (Ee, Eo), (be, bo) = pair_views(E, l, hf), pair_views(bb, l, hf)
            ref = free_dims(bb[:, hf * 1024 + l - 1:hf * 1024 + l], [2 * l, 512 // l], [0, l])
            V.do(lambda e: e.tensor_tensor(Ee, ref, be, ALU.subtract), t_ln)
            if l < 64:
                t = V.do(lambda e: e.tensor_tensor(Eo, bo, ref, ALU.subtract))
            else:
                t = V.do(lambda e: e.tensor_copy(Eo, bo))
            Eh = E[:, hf * 1024:hf * 1024 + 1024]
            return A.do(lambda e: e.activation(Eh, Eh, ACT.Exp), t)

        def scaled(lv, hf, k, t, E=E, Gt=Gt, bk=bk, bq=bq):
            l = 1 << lv
            (Ee, Eo), (Ge, Go) = pair_views(E, l, hf), pair_views(Gt, l, hf)
            ke, qo = pair_views(bk, l, hf)[0], pair_views(bq, l, hf)[1]
            V.do(lambda e: e.tensor_tensor(Ge, Ee, ke, ALU.mult), k, t)
            return V.do(lambda e: e.tensor_tensor(Go, Eo, qo, ALU.mult))

        t_ex = [decays(0, hf) for hf in range(2)]
        blocks = [products(hf, bk, bq, t_b, t_bq) for hf in range(2)]
        t_mm = [None, None]
        for lv in range(7):
            new = [None, None]
            for hf in range(2):
                k = scaled(lv, hf, t_ex[hf], t_mm[hf])
                if lv < 6:
                    t_ex[hf] = decays(lv + 1, hf)
                t_acc = kept(lv - 1 if lv else 7, blocks[hf])
                new[hf] = products(hf, Gt, Gt, k)
                t_mm[hf] = new[hf][-1][2]
                fill(1)
            blocks = new
        t_acc = [kept(6, blocks[hf]) for hf in range(2)]
        t_mm = T.last()
        B4 = bb.rearrange("p (h c t) -> p h c t", h=8, c=4)
        E4 = E.rearrange("p (h c t) -> p h c t", h=8, c=4)
        lastc = lambda c: bb[:, c * 64 + 63:c * 64 + 64]
        v8 = lambda ap: free_dims(ap, [256, 8], [0, 64])
        V.do(lambda e: e.tensor_tensor(bls[:, 0:8], free_dims(lastc(0), [256, 8]), free_dims(lastc(1), [256, 8]), ALU.add))
        V.do(lambda e: e.tensor_tensor(E4[:, :, 0, :], free_dims(bls[:, 0:8], [1, 8], [0, 64]), B4[:, :, 0, :], ALU.subtract), A.last())
        V.do(lambda e: e.tensor_tensor(E4[:, :, 1, :], v8(lastc(1)), B4[:, :, 1, :], ALU.subtract))
        V.do(lambda e: e.tensor_copy(E4[:, :, 2, :], B4[:, :, 2, :]))
        t_e = V.do(lambda e: e.tensor_tensor(E4[:, :, 3, :], v8(lastc(2)), B4[:, :, 3, :], ALU.add))
        fill(2)
        k = A.do(lambda e, E=E: e.activation(E, E, ACT.Exp), t_e)
        hv = lambda t, s: b3(t)[:, :, s * 128:s * 128 + 128]
        V.do(lambda e, E=E, Gt=Gt, bk=bk: e.tensor_tensor(hv(Gt, 0), hv(E, 0), hv(bk, 0), ALU.mult), k, t_mm)
        k = V.do(lambda e, E=E, Gt=Gt, bq=bq: e.tensor_tensor(hv(Gt, 1), hv(E, 1), hv(bq, 1), ALU.mult))
        accx3 = b3(accx)
        t_ax = []
        for q in range(2):
            b = bank()
            for j in range(4):
                h = 4 * q + j
                f = mm(b.ap[:, j * 128:j * 128 + 128], G3[:, h, 0:128], G3[:, h, 128:256], True, True)
                if j == 3:
                    t = T.do(f)
                else:
                    T.plain(f, b.free, k)
            b.free = copy_out(q, accx3[:, 4 * q:4 * q + 4, :], r3(b.ap[:, :], 4), t, k)
            t_ax.append(b.free)
        oN = r3(bq, 2)
        sqj = bk
        t_fin = [T.last(), V.last()]
        bg_f = bg.rearrange("p a b -> p (a b)")
        k = A.do(lambda e, Gt=Gt: e.activation(Gt, bg_f, ACT.Sigmoid), t_fin, t_bg)
        V.do(lambda e, Gt=Gt: e.tensor_tensor(bg_f, bg_f, Gt, ALU.mult), k)
        V.do(lambda e: e.tensor_tensor(r3(bg_f, 16), r3(bg_f, 16), free_dims(hg, [0, 16], [1, 128]), ALU.mult), t_gb)
        t_on = []
        for tt in range(2):
            for q in range(2):
                b = bank()
                for j in range(4):
                    h = 4 * q + j
                    o = b.ap[:, j * 128:j * 128 + 128]
                    v = slice(h * 128, h * 128 + 128)
                    if tt:
                        T.plain(mm(o, accx3[:, h, :], bi[:, 0, v], True, False), b.free, t_ax, t_bi)
                    f = mm(o, acc3[:, 2 * h + tt, :], bi[:, tt, v], tt == 0, True)
                    if j == 3:
                        t = T.do(f, t_acc)
                    else:
                        T.plain(f, b.free, t_acc, t_bi)
                b.free = copy_out(q, oN[:, tt, q * 512:q * 512 + 512], b.ap[:, :], t, t_fin)
                t_on.append(b.free)
        V.do(lambda e, sqj=sqj, bq=bq: e.tensor_tensor(sqj, bq, bq, ALU.mult), t_on)
        h_ss, h_ms, h_sq, h_r, h_t = (sst[:, 16 * i:16 * i + 16] for i in range(5))
        V.do(lambda e, sqj=sqj: e.tensor_reduce(h_ss, r3(sqj, 16), AX.X, ALU.add))
        t_e = V.do(lambda e: e.tensor_scalar(h_ms, h_ss, 1.0 / 128, 1e-6, ALU.mult, ALU.add))
        for _ in filler:
            pass
        k = A.do(lambda e: e.activation(h_sq, h_ms, ACT.Sqrt), t_e)
        inv_sqrt(h_r, h_sq, h_ms, h_t, k)
        V.do(lambda e, bq=bq: e.tensor_tensor(r3(bq, 16), r3(bq, 16), free_dims(h_r, [1, 16], [0, 128]), ALU.mult))
        k = V.do(lambda e, oN=oN, bg=bg: e.tensor_tensor(oN, oN, bg, ALU.mult), t_bg)
        obT = b3(bb)
        t_ob = transposes(oN, obT, 8, k)
        t_m = merge(raw["b"], obT, False, t_ob, t_sg)

        toks = barrier()
        leave()
        inner()
        cq, ck_ = ar(2048), ar(2048)
        ocT = r3(ar(16 * 256), 16)
        rt1, rt2 = ar(1024), ar(1024)
        at0, at1 = r3(ar(1024), 4), r3(ar(512), 4)
        cv = [r3(ar(1024), 2) for _ in range(2)]
        cg = [r3(ar(1024), 2) for _ in range(2)]
        oc = [r3(rt1, 2), r3(rt2, 2)]
        tab = ar(1536)
        cst_ = ar(40)
        sjunk = rel
        g_t = group("ret")
        t_gt = A.dma(g_t, lambda e: e.dma_start(tab, a["cst"][:, C_COS:C_COS + 1536]), toks)
        cosb = free_dims(tab[:, 0:256], [0, 4], [1, 256])
        sinb = free_dims(tab[:, 256:512], [0, 4], [1, 256])
        dec = tab[:, 512:1536]
        t_rot = []
        u0, u1 = r3(rt1, 4), r3(rt2, 4)
        for src in (cq, ck_):
            tk = []
            for n in range(2):
                go(run_t(b3(src), n, tk))
            ev = src.rearrange("p (h e t) -> p h e t", h=4, e=2)
            s0, s1 = ev[:, :, 0, :], ev[:, :, 1, :]
            V.do(lambda e, s0=s0: e.tensor_tensor(u0, s0, cosb, ALU.mult), tk, t_gt)
            V.do(lambda e, s0=s0: e.tensor_tensor(u1, s0, sinb, ALU.mult))
            V.do(lambda e, s0=s0, s1=s1: e.tensor_tensor(s0, s1, sinb, ALU.mult))
            V.do(lambda e, s0=s0: e.tensor_tensor(s0, u0, s0, ALU.subtract))
            V.do(lambda e, s1=s1: e.tensor_tensor(s1, s1, cosb, ALU.mult))
            t_rot.append(V.do(lambda e, s1=s1: e.tensor_tensor(s1, s1, u1, ALU.add)))
        rq3, rk3 = b3(cq), b3(ck_)
        t_at = []
        oc_free, cv_free, cg_free = [None, None], [None, None], [None, None]
        t_oc = {}
        turned = None
        t_cv, t_cg = {}, {}

        def values(h):
            i = h % 2
            t_cv[h], t_cg[h] = [], []

            def evac_v(tt, ps, t):
                k = A.do(lambda e, o=cv[i][:, tt, :]: e.activation(o, ps, ACT.Copy), t, cv_free[i])
                t_cv[h].append(k)
                return k
            go(proj_n(sp, hT, evac_v))
            go(run_silu([cg[i][:, tt, :] for tt in range(2)], t_cg[h], cg_free[i]))

        def turn_back(h):
            t_oc[h] = transposes(oc[h % 2], ocT[:, 4 * h:4 * h + 4, :], 4, cg_free[h % 2])
            oc_free[h % 2] = T.last()

        values(0)
        for h in range(4):
            b = bank()
            for e2 in range(2):
                T.plain(mm(b.ap[:, 0:256], rk3[:, 2 * h + e2, 0:128], rq3[:, 2 * h + e2, :], e2 == 0, e2 == 1),
                        b.free, t_rot)
            for e2 in range(2):
                f = mm(b.ap[:, 256:384], rk3[:, 2 * h + e2, 128:256], rq3[:, 2 * h + e2, 128:256], e2 == 0, e2 == 1)
                if e2:
                    t = T.do(f)
                else:
                    T.plain(f)
            V.do(lambda e, h=h, b=b: e.tensor_tensor(at0[:, h, :], b.ap[:, 0:256], dec[:, h * 256:h * 256 + 256], ALU.mult), t)
            b.free = V.do(lambda e, h=h, b=b: e.tensor_tensor(at1[:, h, :], b.ap[:, 256:384],
                                                              dec[:, h * 256:h * 256 + 128], ALU.mult))
            t_at.append(b.free)
        for h in range(4):
            i = h % 2
            if h < 3:
                values(h + 1)
            if h:
                turn_back(h - 1)
            bs = []
            for tt in range(2):
                b = bank()
                if tt == 0:
                    t = T.do(mm(b.ap[:, :], at0[:, h, 0:128], cv[i][:, 0, :], True, True), b.free, t_cv[h], t_at)
                else:
                    T.plain(mm(b.ap[:, :], at0[:, h, 128:256], cv[i][:, 0, :], True, False), b.free)
                    t = T.do(mm(b.ap[:, :], at1[:, h, :], cv[i][:, 1, :], False, True))
                k = A.do(lambda e, b=b, tt=tt: e.activation(sjunk, b.ap[:, :], ACT.Square,
                                                            accum_out=cst_[:, tt:tt + 1]), t, V.last())
                bs.append(b)
            cv_free[i] = t
            ms, sq, r_, t_ = (cst_[:, 8 * q:8 * q + 2] for q in range(1, 5))
            k = V.do(lambda e, ms=ms: e.tensor_scalar(ms, cst_[:, 0:2], 1.0 / 512, 1e-6, ALU.mult, ALU.add), k)
            k = A.do(lambda e, ms=ms, sq=sq: e.activation(sq, ms, ACT.Sqrt), k)
            inv_sqrt(r_, sq, ms, t_, k)
            for tt in range(2):
                bs[tt].free = k = V.do(lambda e, tt=tt, i=i, b=bs[tt], r_=r_: e.scalar_tensor_tensor(
                    out=oc[i][:, tt, :], in0=b.ap[:, :], scalar=r_[:, tt:tt + 1], in1=cg[i][:, tt, :],
                    op0=ALU.mult, op1=ALU.mult), oc_free[i], t_cg[h])
            cg_free[i] = k
        t_sg, make_c = gates(sp, sg, t_m, ht)
        go(make_c)
        t_hT = [T.last()] * 2
        turn_back(3)
        bs = [bank() for _ in range(8)]
        t_sp = {}

        def parted(kq):
            i, v = kq % 2, ocT[:, 4 * kq:4 * kq + 4, :]
            hi, lo = (t[:, 4 * i:4 * i + 4, :] for t in hT)
            k = A.do(lambda e: e.activation(hi, v, ACT.Copy), t_oc[kq], t_hT[i])
            t_sp[kq] = V.do(lambda e: e.tensor_tensor(lo, v, hi.bitcast(F32), ALU.subtract), k)
            return hi, lo

        xs = [parted(0), parted(1)]
        for kq in range(4):
            for q in range(4):
                p = sp.take()
                two = bs[2 * q:2 * q + 2]
                t = block_pair(p, [b.ap[:, 0:256] for b in two], xs[kq % 2], kq == 0, kq == 3, t_sp[kq],
                               [b.free for b in two] if kq == 0 else None)
                sp.give(p, t)
                for j, b in enumerate(two if kq == 3 else []):
                    m_, g_, t_ = mT[:, 2 * q + j, :], sg[:, 2 * q + j, :], tmp[:, j, :]
                    b.free = V.do(lambda e, b=b, g_=g_, t_=t_: e.tensor_tensor(t_, g_, b.ap[:, 0:256], ALU.mult),
                                  t, t_sg[q])
                    t_m = V.do(lambda e, m_=m_, t_=t_: e.tensor_tensor(m_, m_, t_, ALU.add))
            t_hT[kq % 2] = t
            if kq < 2:
                xs[kq] = parted(kq + 2)

        hN = r3(hold, 2)
        for tt in range(2):
            for n in range(2):
                b = bank()
                for k in range(8):
                    c = raw["o"][2 * n + k // 4]
                    f = mm(b.ap, mT[:, k, tt * 128:tt * 128 + 128], r3(c.ap, 4)[:, k % 4, :], k == 0, k == 7)
                    T.wait(c.tok, b.free, t_m)
                    if k % 4 == 3:
                        c.done = t = T.do(f)
                    else:
                        T.plain(f)
                xs = x[:, tt, n * 512:n * 512 + 512]
                b.free = V.do(lambda e, b=b, n=n: e.tensor_tensor(
                    rel, b.ap, grow[0][:, n * 512:n * 512 + 512], ALU.mult), t, t_gt1)
                V.do(lambda e, xs=xs: e.tensor_tensor(xs, xs, rel, ALU.add))
            rmsnorm(x, grow[1][:, :], hN, rt1, 1024, V.last(), tiles=(tt,))
            t_hn = V.do(lambda e, tt=tt: e.tensor_tensor(hN[:, tt, :], hN[:, tt, :], grow[2][:, :], ALU.add), t_sh)
        t_g2 = row_load(A, g_r[0], 0, mod_d[5, :], V.last())
        leave()

        toks = barrier()
        leave()
        inner()
        hT_f = ar(2048)
        hT, junk = r3(hT_f, 8), hT_f[:, 0:1024]
        hNh, hNl = (r3(ar(2048, F32R), 2) for _ in range(2))
        rw = ar(8 * 36)
        rbb = ar(36)
        lg = ar(72)
        sc4 = ar(96)
        s8 = ar(200)
        cm = ar(384)
        pos = ar(16)
        cnt = ar(16)
        many = ar(1).bitcast(I32)
        sel_r = ar(1024, F32R)
        sel = sel_r.bitcast(F32)
        selT = ar(1024)
        xg = (r3(ar(4096, F32R), 8), r3(ar(4096, F32R), 8))
        gsel = ar(32)
        sgb = [ar(512) for _ in range(2)]
        hge = [ar(512) for _ in range(2)]
        hgT = [(r3(ar(512, F32R), 4), r3(ar(512, F32R), 4)) for _ in range(2)]
        bufs = split_bufs()
        yg = [ar(1024) for _ in range(2)]
        ytmp = ar(512)
        ctx.callback(leave)
        ctx.callback(leave)
        g_o = group("moe")
        A.dma(g_o, lambda e: e.dma_start(rw, a["rw"]), toks)
        A.dma(g_o, lambda e: e.dma_start(cm, a["cst"][:, C_MOE:C_MOE + 384]))
        t_go = A.dma(g_o, lambda e: e.dma_start(rbb, a["rb"][0, :].partition_broadcast(P)))
        ht = transposes(hN, hT, 8, t_hn)
        k = A.do(lambda e, hN=hN: e.activation(hNh, hN, ACT.Copy), t_hn)
        t_hs = G.do(lambda e, hN=hN: e.tensor_tensor(hNl, hN, hNh.bitcast(F32), ALU.subtract), k)

        def weights(T, A, chunk, engines, at_first):
            sp = Splitter(T, A, chunk, bufs)
            for src, ex in ([("eg", 0), ("eu", 0)] + [(src, ex + (src != "ed")) for ex in range(32)
                                                      for src in ("eg", "eu", "ed") if ex + (src != "ed") < 32]):
                sp.expect(halves(a[src][ex]), engines if sp.parts else at_first, "rows")
            sp.ahead(PARTS)
            return sp

        sp = weights(T, A, chunk, [V], [G])
        b = bank()
        rw3 = r3(rw, 8)
        for tt in range(2):
            for k in range(8):
                f = mm(b.ap[:, tt * 36:tt * 36 + 36], hT[:, k, tt * 128:tt * 128 + 128], rw3[:, k, :], k == 0, k == 7)
                if tt and k == 7:
                    t = T.do(f)
                else:
                    T.plain(f, b.free, ht, t_go)
        lg3 = r3(lg, 2)
        b.free = V.do(lambda e, b=b: e.tensor_tensor(lg3, r3(b.ap[:, 0:72], 2), free_dims(rbb, [0, 2], [1, 36]), ALU.add), t, t_go)
        gl = lg3[:, :, 0:4]
        vv = lambda o, n: free_dims(sc4[:, o:o + 1], [n, 2], [1, n])
        vb = lambda o, n: free_dims(sc4[:, o:o + 1], [1, 2], [0, n])
        gsum, gp = sc4[:, 2:4], sc4[:, 4:6]
        eqg, ohg = vv(8, 4), vv(16, 4)

        def first_one(dst, src, mx_o, n, tmp_o):
            rank = free_dims(iota[:, 0:1], [0, 2], [1, n])
            return [lambda fn=fn: V.do(fn) for fn in (
                lambda e: e.tensor_reduce(sc4[:, mx_o:mx_o + 2], src, AX.X, ALU.max),
                lambda e: e.tensor_tensor(dst, src, vb(mx_o, n), ALU.is_equal),
                lambda e: e.scalar_tensor_tensor(out=dst, in0=rank, scalar=-16.0, in1=dst, op0=ALU.add, op1=ALU.mult),
                lambda e: e.tensor_reduce(sc4[:, tmp_o:tmp_o + 2], dst, AX.X, ALU.min),
                lambda e: e.tensor_tensor(dst, dst, vb(tmp_o, n), ALU.is_equal))]

        for step in first_one(ohg, gl, 0, 4, 24):
            t_oh = step()
        b = bank()
        tri, ones = cm[:, 128:256], cm[:, 256:384]
        T.plain(mm(b.ap[:, 0:4], tri, sc4[:, 16:20], True, True), b.free, t_oh, t_go)
        T.plain(mm(b.ap[:, 4:8], ones, sc4[:, 16:20], True, False))
        T.plain(mm(b.ap[:, 4:8], tri, sc4[:, 20:24], False, True))
        T.plain(mm(b.ap[:, 8:12], ones, sc4[:, 16:20], True, False))
        t = T.do(mm(b.ap[:, 8:12], ones, sc4[:, 20:24], False, True))
        V.do(lambda e, b=b: e.tensor_scalar(pos[:, 0:8], b.ap[:, 0:8], 1.0, None, ALU.add), t)
        V.do(lambda e: e.tensor_tensor(pos[:, 0:8], pos[:, 0:8], sc4[:, 16:24], ALU.mult))
        V.do(lambda e: e.tensor_scalar(pos[:, 0:8], pos[:, 0:8], -1.0, None, ALU.add))
        b.free = V.do(lambda e, b=b: e.tensor_reduce(cnt[:, 0:1], b.ap[:, 8:12], AX.X, ALU.max))
        t_many = V.do(lambda e: e.tensor_copy(many, cnt[:, 0:1]))
        def gating():
            steps = []

            def v(fn):
                steps.append(lambda: V.do(fn))

            def expo(d):
                def f():
                    k = A.do(lambda e: e.activation(d, d, ACT.Exp), V.last())
                    V.wait(k)
                steps.append(f)

            v(lambda e: e.tensor_tensor(eqg, gl, vb(0, 4), ALU.subtract))
            expo(sc4[:, 8:16])
            v(lambda e: e.tensor_reduce(gsum, eqg, AX.X, ALU.add))
            v(lambda e: e.reciprocal(gp, gsum))
            el = free_dims(lg[:, 4:5], [36, 2], [1, 8], [8, 4])
            prod = s8[:, 0:64]
            v(lambda e: e.tensor_tensor(free_dims(prod, [32, 2], [4, 8], [1, 4]), el,
                                           free_dims(sc4[:, 16:17], [4, 2], [0, 8], [1, 4]), ALU.mult))
            ing = r3(s8[:, 64:80], 2)
            v(lambda e: e.tensor_reduce(s8[:, 64:80], free_dims(prod, [4, 16], [1, 4]), AX.X, ALU.add))
            oh1, oh2, in2 = r3(s8[:, 80:96], 2), r3(s8[:, 96:112], 2), r3(s8[:, 112:128], 2)
            steps += first_one(oh1, ing, 26, 8, 28)
            v(lambda e: e.scalar_tensor_tensor(out=in2, in0=oh1, scalar=-BIG, in1=ing, op0=ALU.mult, op1=ALU.add))
            steps += first_one(oh2, in2, 30, 8, 32)
            gex, den, w1 = sc4[:, 34:36], sc4[:, 36:38], sc4[:, 38:40]
            v(lambda e: e.tensor_tensor(gex, sc4[:, 30:32], sc4[:, 26:28], ALU.subtract))
            expo(gex)
            v(lambda e: e.tensor_scalar(den, gex, 1.0, None, ALU.add))
            v(lambda e: e.reciprocal(w1, den))
            v(lambda e: e.tensor_tensor(w1, w1, gp, ALU.mult))
            v(lambda e: e.tensor_tensor(gex, gex, w1, ALU.mult))
            v(lambda e: e.tensor_tensor(oh1, oh1, vb(38, 8), ALU.mult))
            v(lambda e: e.tensor_tensor(oh2, oh2, vb(34, 8), ALU.mult))
            v(lambda e: e.tensor_tensor(oh1, oh1, oh2, ALU.add))
            return steps

        y = [[banks[4], banks[5]], [banks[6], banks[7]]]
        usable[:] = [0, 1, 2, 3]

        t_gate = []
        gate_steps = gating()

        def experts(T, V, A, sp, first):
            done = {}
            for g in range(4):
                for tt in range(2):
                    t_sel = V.do(lambda e, g=g, tt=tt: e.tensor_scalar(
                        sel_r[:, tt * 512 + g * 128:tt * 512 + g * 128 + 128], cm[:, 0:128], float(first),
                        pos[:, 4 * tt + g:4 * tt + g + 1], ALU.add, ALU.is_equal), t_go, T.last())
            if CAP < 128:
                over = sel_r.rearrange("p (a b) -> p a b", b=128)[:, :, CAP:128]
                t_sel = V.do(lambda e: e.tensor_scalar(over, over.bitcast(F32), 0.0, None, ALU.mult))
            t_xg = []
            for k in range(8):
                bs = [bank(), bank()]
                for b, src in zip(bs, (hNh, hNl)):
                    T.plain(mm(b.ap, src[:, 0, k * 128:k * 128 + 128], sel_r[:, 0:512], True, False), b.free, t_sel, t_hs)
                    t = T.do(mm(b.ap, src[:, 1, k * 128:k * 128 + 128], sel_r[:, 512:1024], False, True))
                bs[0].free = A.do(lambda e, k=k, b=bs[0]: e.activation(xg[0][:, k, :], b.ap, ACT.Copy), t)
                bs[1].free = V.do(lambda e, k=k, b=bs[1]: e.tensor_copy(xg[1][:, k, :], b.ap), t)
                t_xg += [b.free for b in bs]
                for step in gate_steps[:7]:
                    step()
                del gate_steps[:7]
            if not t_gate:
                for step in gate_steps:
                    step()
                t_gate.append(V.last())
            def places():
                b = bank()
                for g in range(4):
                    for tt in range(2):
                        f = mm(b.ap[:, g * 8:g * 8 + 8], sel[:, tt * 512 + g * 128:tt * 512 + g * 128 + 128],
                               s8[:, 80 + 8 * tt:88 + 8 * tt], tt == 0, tt == 1)
                        if g == 3 and tt:
                            t = T.do(f)
                        else:
                            T.plain(f, b.free, t_gate)
                b.free = done["gs"] = V.do(lambda e, b=b: e.tensor_copy(gsel, b.ap[:, 0:32]), t)
                for q in range(2):
                    b = bank()
                    for j in range(4):
                        g, tt = 2 * q + j // 2, j % 2
                        f = (lambda e, b=b, j=j, g=g, tt=tt: e.transpose(
                            b.ap[:, j * 128:j * 128 + 128], sel[:, tt * 512 + g * 128:tt * 512 + g * 128 + 128], ident))
                        if j == 3:
                            t = T.do(f)
                        else:
                            T.plain(f, b.free)
                    b.free = done["st"] = V.do(lambda e, q=q, b=b: e.tensor_copy(selT[:, q * 512:q * 512 + 512], b.ap[:, :]), t)

            def up(ex, between):
                g = ex // 8
                hb, sb_ = hge[ex % 2], sgb[ex % 2]
                got = []
                rows = slice(g * 128, g * 128 + 128)
                for part in range(2):
                    if part:
                        (bg_, tg), = got
                        bg_.free = k_s = A.do(lambda e: e.activation(sb_, bg_.ap, ACT.Silu), tg, done.get(("h", ex - 2)))
                        between()
                    b = bank()
                    for q in range(4):
                        p = sp.take()
                        for kk in range(2):
                            k, w = 2 * q + kk, slice(kk * 512, kk * 512 + 512)
                            T.plain(mm(b.ap, xg[0][:, k, rows], p.hi[:, w], k == 0, False), p.tok, b.free, t_xg)
                            T.plain(mm(b.ap, xg[1][:, k, rows], p.hi[:, w], False, False))
                            f = mm(b.ap, xg[0][:, k, rows], p.lo[:, w], False, k == 7)
                            if kk:
                                t = T.do(f)
                            else:
                                T.plain(f)
                        sp.give(p, t)
                    got.append((b, t))
                bu_, tu = got[1]
                bu_.free = done["h", ex] = V.do(lambda e: e.scalar_tensor_tensor(
                    out=hb, in0=sb_, scalar=gsel[:, ex:ex + 1], in1=bu_.ap[:, :], op0=ALU.mult, op1=ALU.mult),
                    k_s, tu, done["gs"], done.get(("t", ex - 2)))

            def turned(ex):
                b = bank()
                for j in range(4):
                    f = (lambda e, b=b, j=j: e.transpose(b.ap[:, j * 128:j * 128 + 128],
                                                         hge[ex % 2][:, j * 128:j * 128 + 128], ident))
                    if j == 3:
                        done["t", ex] = T.do(f)
                    else:
                        T.plain(f, b.free, done["h", ex])
                hh, hl = hgT[ex % 2]
                k = A.do(lambda e, b=b: e.activation(hh, r3(b.ap, 4), ACT.Copy), done["t", ex], done.get(("d", ex - 2)))
                b.free = done["hT", ex] = V.do(lambda e, b=b: e.tensor_tensor(
                    hl, r3(b.ap, 4), hh.bitcast(F32), ALU.subtract), k, done.get(("d", ex - 2)))

            def down(ex):
                g = ex // 8
                hh, hl = hgT[ex % 2]
                t_h = done["hT", ex]
                for k in range(4):
                    p = sp.take()
                    for n in range(2):
                        yb = y[g % 2][n]
                        w = slice(n * 512, n * 512 + 512)
                        T.plain(mm(yb.ap, hh[:, k, :], p.hi[:, w], ex % 8 == 0 and k == 0, False),
                                p.tok, t_h, yb.free if ex % 8 == 0 else None)
                        T.plain(mm(yb.ap, hl[:, k, :], p.hi[:, w], False, False))
                        f = mm(yb.ap, hh[:, k, :], p.lo[:, w], False, ex % 8 == 7 and k == 3)
                        if n:
                            t = T.do(f)
                        else:
                            T.plain(f)
                    sp.give(p, t)
                done["d", ex] = t
                if ex % 8 == 7:
                    for n in range(2):
                        y[g % 2][n].free = done["y", g] = A.do(lambda e, n=n: e.activation(
                            yg[g % 2][:, n * 512:n * 512 + 512], y[g % 2][n].ap[:, :], ACT.Copy),
                            done["d", ex], done.get(("s", g - 2)))

            def back(g):
                for tt in range(2):
                    for n in range(2):
                        b = bank()
                        done["s", g] = t = T.do(mm(
                            b.ap[:, :], selT[:, g * 256 + tt * 128:g * 256 + tt * 128 + 128],
                            yg[g % 2][:, n * 512:n * 512 + 512], True, True), b.free, done["y", g], done["st"])
                        xs = x[:, tt, n * 512:n * 512 + 512]
                        b.free = V.do(lambda e, b=b, n=n: e.tensor_tensor(
                            ytmp, b.ap[:, :], grow[0][:, n * 512:n * 512 + 512], ALU.mult), t, t_g2)
                        V.do(lambda e, xs=xs: e.tensor_tensor(xs, xs, ytmp, ALU.add))

            up(0, places)
            for ex in range(32):
                if ex < 31:
                    up(ex + 1, lambda: turned(ex))
                else:
                    turned(ex)
                down(ex)
                if ex % 8 == 1 and ex > 8:
                    back(ex // 8 - 1)
            back(3)

        experts(T, V, A, sp, 0)
        rest = []
        for p in range(1, 256 // CAP):
            marks = [q.last() for q in (T, V, A, G)]
            T2, V2, A2 = (Queue(sem(f"s_{n}{p}"), n != "pe") for n in ("pe", "dve", "act"))
            for q in (T2, V2, A2):
                q.wait(*marks)
            sems2 = [sem(f"s_ring{i}_{p}") for i in range(RING)]
            more = []

            def chunk2(src, more=more, sems2=sems2):
                c = Chunk(len(more), src, sems2)
                more.append(c)
                c.ap = ring[c.slot][:, :]
                return c

            frees = [(b, b.free) for b in banks]
            for b in banks:
                b.free = None
            experts(T2, V2, A2, weights(T2, A2, chunk2, [V2], [V2]), p * CAP)
            for b, f in frees:
                b.free = f
            for q in (T2, V2, A2):
                q.wait(T2.last(), V2.last(), A2.last())
            rest.append((p, T2, V2, A2, more, marks))
            for q, q2 in ((T, T2), (V, V2), (A, A2)):
                q.ops.append((p, q2.ops))
        t_x = V.last()
        g_out = group("out")
        for tt in range(2):
            t_f = rmsnorm(x, grow[3][:, :], hN, junk, 1024, t_x, t_gf, tiles=(tt,))
            t_out = A.dma(g_out, lambda e, tt=tt: e.dma_start(out[0, tt * 128:tt * 128 + 128, :], hN[:, tt, :]), t_f)
        A.wait(t_out)

        block = ctx.enter_context(nc.Block())

        def run(e, ops):
            for f in ops:
                if isinstance(f, tuple):
                    p, inner = f
                    e.wait_ge(*t_many)
                    with e.If(e.value_load(many[0:1, 0:1], min_val=0, max_val=256) > p * CAP):
                        run(e, inner)
                else:
                    f(e)

        def load(e, cs, before):
            for c in cs:
                if c.n >= RING:
                    done = cs[c.n - RING].done
                    for t in (done if isinstance(done, list) else [done]):
                        e.wait_ge(*t)
                elif before:
                    for t in before:
                        e.wait_ge(*t)
                e.dma_start(c.ap, c.src).then_inc(c.tok[0], 16)

        @block.sync
        def _(e):
            load(e, chunks, [t_x0])
            for p, _, _, _, more, marks in rest:
                e.wait_ge(*t_many)
                with e.If(e.value_load(many[0:1, 0:1], min_val=0, max_val=256) > p * CAP):
                    load(e, more, marks)

        @block.tensor
        def _(e):
            run(e, T.ops)

        @block.vector
        def _(e):
            run(e, V.ops)

        @block.scalar
        def _(e):
            run(e, A.ops)

        @block.gpsimd
        def _(e):
            run(e, G.ops)


def constants():
    c = np.zeros((P, C_END), np.float32)
    c[:, C_ID:C_ID + 128] = np.eye(128)
    c[:, C_IOTA:C_IOTA + 16] = np.arange(16)
    pos = np.arange(256, dtype=np.float32)
    theta = (np.float32(1.0) / np.power(np.float32(10000.0), np.linspace(0.0, 1.0, 128, dtype=np.float32))).astype(np.float32)
    ang = (theta[:, None] * pos[None, :]).astype(np.float32).astype(np.float64)
    c[:, C_COS:C_COS + 256] = np.cos(ang)
    c[:, C_SIN:C_SIN + 256] = np.sin(ang)
    s, t = np.arange(128)[:, None], np.arange(256)[None, :]
    for h in range(4):
        g = np.log(1.0 - 2.0 ** (-5.0 - h))
        d = np.where(t >= s, np.exp((t - s) * g), 0.0) * (256.0 ** -0.5)
        c[:, C_DEC + h * 256:C_DEC + h * 256 + 256] = d
    for g, w in enumerate((2, 4, 8, 16)):
        c[:, C_INV + g * 256:C_INV + g * 256 + 256] = 1.0 / np.minimum(np.arange(256) + 1, w)
    rel = np.maximum(255 - np.arange(512), 0)
    relf = np.maximum(rel, 1).astype(np.float32)
    large = 16 + (np.log(relf / np.float32(16)) / np.float32(np.log(8.0)) * np.float32(16)).astype(np.int32)
    bucket = np.where(rel < 16, rel, np.minimum(large, 31))
    c[bucket, C_OH + np.arange(512)] = 1.0
    c[:, C_OH + 512:C_OH + 640] = np.eye(128)[::-1]
    c[:, C_MOE:C_MOE + 128] = np.arange(128)
    c[:, C_MOE + 128:C_MOE + 256] = np.triu(np.ones((128, 128)), 1)
    c[:, C_MOE + 256:C_MOE + 384] = 1.0
    m = np.zeros((P, 8, 128), np.int32)
    s, t = np.arange(128)[:, None], np.arange(128)[None, :]
    for lv in range(7):
        l = 1 << lv
        m[:, lv, :] = (s // (2 * l) == t // (2 * l)) & ((s // l) % 2 == 0) & ((t // l) % 2 == 1)
    m[:, 7, :] = s == t
    return c, m.reshape(P, 1024)


def kernel(**inputs):
    import concourse.bacc as bacc
    from concourse.bass_utils import run_bass_kernel_spmd

    i = {k: np.asarray(v) for k, v in inputs.items()}

    def cols(w, cw=512):
        k, n = w.shape
        return w.reshape(k // 128, 128, n // cw, cw).transpose(2, 1, 0, 3).reshape(n // cw, 128, -1)

    def rows(w):
        k, n = w.shape
        return w.reshape(k // 128, 128, n).transpose(1, 0, 2).reshape(128, -1)

    w2 = i["w_in_2"][0]
    offs = np.cumsum([0, 1024, 1024, 1024, 512, 64, 8] + [1024] * 4 + [1024, 1024, 2048, 2048] + [1024] * 3)
    aq, ak, av, iq, ik, iw, bq, bf, bi, bg, cq, ck, cv, cg, ga, gb, gc = (
        w2[:, offs[n]:offs[n + 1]] for n in range(17))
    pairs = lambda w: w.reshape(1024, 4, 128, 2).transpose(0, 1, 3, 2).reshape(1024, 1024)
    big = np.concatenate([aq, ak, iq, av, bq, bf, bi, bg, pairs(cq), pairs(ck), cv, cg, ga, gb, gc], axis=1)
    big = np.concatenate([
        cols(big[:, n * 512:n * 512 + 512], 256) if n not in (5, 6, 11, 12, 13, 14, *range(19, 27))
        else rows(big[:, n * 512:n * 512 + 512]).reshape(128, 2, 2048).transpose(1, 0, 2) for n in range(33)])
    wc = i["w_branch_c_2"][0]
    cst, masks = constants()
    arrays = {
        "x": i["x"], "cst": cst, "masks": masks,
        "g_mix": i["g_mix"], "g_ffn": i["g_ffn"], "g_final": i["g_final"],
        "w_in": cols(i["w_in"][0], 256),
        "pgw": i["pool_group_w"][0].transpose(1, 0, 2).reshape(128, 512),
        "pcs": i["pool_scale"][0].reshape(4, 128).T,
        "cvw": i["conv_w"][0].reshape(3, 4, 128).transpose(2, 0, 1).reshape(128, 12),
        "wbp": cols(i["w_branch_pool"][0]), "wbc": cols(i["w_branch_conv"][0]),
        "w_out": cols(i["w_out"][0]), "w_q": cols(i["w_q"][0], 256),
        "skT": i["sub_keys"][0].transpose(3, 0, 1, 2).reshape(128, 2048),
        "expert_uv": np.concatenate([i["expert_u"][0], i["expert_v"][0]], axis=1),
        "c_2": i["c_2"].reshape(8, 128).T, "ada_w_2": cols(i["ada_w_2"][0]), "ada_b_2": i["ada_b_2"],
        "norm1_g_2": i["norm1_g_2"], "norm2_g_2": i["norm2_g_2"], "final_norm_g_2": i["final_norm_g_2"],
        "w_in_2": big, "w_small": rows(np.concatenate([ik, ik, iw], axis=1)),
        "rel_bias_2": i["rel_bias_2"],
        "hgrn_lb_raw_2": i["hgrn_lb_raw_2"].reshape(8, 128).T, "hgrn_norm_g_2": i["hgrn_norm_g_2"],
        "w_branch_a_2": cols(i["w_branch_a_2"][0], 256), "w_branch_b_2": cols(i["w_branch_b_2"][0], 256),
        "w_branch_c_2": np.concatenate([cols(wc[n * 512:n * 512 + 512]) for n in range(4)]),
        "w_out_2": cols(i["w_out_2"][0]),
        "rw": rows(np.concatenate([i["router_group_w_2"][0], i["router_expert_w_2"][0]], axis=1)),
        "rb": np.concatenate([i["router_group_b_2"], i["router_expert_b_2"]], axis=1),
        "eg": i["expert_w_gate_2"][0].reshape(32, 8, 128, 512).transpose(0, 2, 1, 3).reshape(32, 128, 4096),
        "eu": i["expert_w_up_2"][0].reshape(32, 8, 128, 512).transpose(0, 2, 1, 3).reshape(32, 128, 4096),
        "ed": i["expert_w_down_2"][0].reshape(32, 4, 128, 1024).transpose(0, 2, 1, 3).reshape(32, 128, 4096),
    }
    nc = bacc.Bacc("TRN2", target_bir_lowering=False, num_devices=1)
    feed, aps = {}, {}
    for name, v in arrays.items():
        feed["in_" + name] = np.ascontiguousarray(v)
        aps[name] = nc.dram_tensor("in_" + name, v.shape, mybir.dt.from_np(v.dtype), kind="ExternalInput").ap()
    out = nc.dram_tensor("out_0", (1, 256, 1024), F32, kind="ExternalOutput").ap()
    build(nc, aps, out)
    r = run_bass_kernel_spmd(nc, [feed], core_ids=[0])
    return r.results[0]["out_0"]
```
